# Optimizing a Trainium2 kernel written in Bass

```python
import math, functools
import jax, jax.numpy as jnp
from jax import lax
import numpy as np

D_MODEL = 2048
BATCH = 1
SEQ = 256
DEPTH = 1
DEC_BATCH = 8
DEC_SEQ = 1
PAST_LEN = 2048
PAGE_SIZE = 128

EPS = 1e-6
MIX_WIDTH = D_MODEL
GLA_WIDTH = MIX_WIDTH // 2
GDN_WIDTH = MIX_WIDTH - GLA_WIDTH
GLA_HEADS = 4
GLA_DV = GLA_WIDTH // GLA_HEADS
GLA_DK = GLA_DV // 2
GLA_KW = GLA_HEADS * GLA_DK
GLA_GATE_RANK = 16
GLA_GATE_TEMP = 16.0
GDN_HEADS = 8
GDN_DV = GDN_WIDTH // GDN_HEADS
GDN_DK = GDN_DV
GDN_KW = GDN_HEADS * GDN_DK
GDN_VW = GDN_HEADS * GDN_DV
GDN_CONV_DIM = 2 * GDN_KW + GDN_VW
CONV_W = 4
CHUNK = 64
N_MEM = 256
XA_HEADS = 4
XA_HD = D_MODEL // XA_HEADS
D_FF = ((8 * D_MODEL + 767) // 768) * 256
IN_SIZES = (GLA_KW, GLA_KW, GLA_WIDTH, GLA_WIDTH, GLA_GATE_RANK, GDN_CONV_DIM, GDN_VW, GDN_HEADS, GDN_HEADS)
IN_COLS = sum(IN_SIZES)

kernel_name = "hybrid_gla_gdn_memory_decoder"

def _split_points(sizes):
    return [int(s) for s in np.cumsum(sizes)[:-1]]

def rmsnorm(x, g):
    xf = x.astype(jnp.float32)
    y = xf * lax.rsqrt(jnp.mean(xf * xf, axis=-1, keepdims=True) + EPS)
    return (y * g.astype(jnp.float32)).astype(x.dtype)

def l2norm(x):
    return x * lax.rsqrt(jnp.sum(x * x, axis=-1, keepdims=True) + EPS)

def gla_chunked(q, k, v, log_a, s0):
    B, H, T, DK = q.shape
    DV = v.shape[-1]
    n = T // CHUNK
    to_c = lambda t: jnp.moveaxis(t.reshape(B, H, n, CHUNK, t.shape[-1]), 2, 0)
    idx = jnp.arange(CHUNK)
    incl = (idx[:, None] >= idx[None, :])[:, :, None]

    def step(s, inp):
        qi, ki, vi, ai = inp
        b = jnp.cumsum(ai, axis=2)
        decay = jnp.exp(jnp.where(incl, b[:, :, :, None, :] - b[:, :, None, :, :], -jnp.inf))
        scores = jnp.einsum('bhtd,bhsd,bhtsd->bhts', qi, ki, decay)
        o = jnp.einsum('bhtd,bhde->bhte', qi * jnp.exp(b), s) + jnp.einsum('bhts,bhse->bhte', scores, vi)
        b_last = b[:, :, -1:, :]
        s = jnp.exp(b_last[:, :, 0, :])[..., None] * s + jnp.einsum('bhsd,bhse->bhde', ki * jnp.exp(b_last - b), vi)
        return s, o

    s_fin, oc = lax.scan(step, s0, (to_c(q), to_c(k), to_c(v), to_c(log_a)))
    return jnp.moveaxis(oc, 0, 2).reshape(B, H, T, DV), s_fin

def gla_recurrent(q, k, v, log_a, s0):
    def step(s, inp):
        qt, kt, vt, at = inp
        s = jnp.exp(at)[..., None] * s + kt[..., None] * vt[..., None, :]
        return s, jnp.einsum('bhd,bhde->bhe', qt, s)
    xs = tuple(jnp.moveaxis(t, 2, 0) for t in (q, k, v, log_a))
    s_fin, o = lax.scan(step, s0, xs)
    return jnp.moveaxis(o, 0, 2), s_fin

def gdn_chunked(q, k, v, g, beta, s0):
    B, H, T, DK = q.shape
    DV = v.shape[-1]
    n = T // CHUNK
    qc = q.reshape(B, H, n, CHUNK, DK)
    kc = k.reshape(B, H, n, CHUNK, DK)
    vc = v.reshape(B, H, n, CHUNK, DV)
    gc = g.reshape(B, H, n, CHUNK)
    bc = beta.reshape(B, H, n, CHUNK)
    G = jnp.cumsum(gc, axis=-1)
    idx = jnp.arange(CHUNK)
    incl = idx[:, None] >= idx[None, :]
    strict = idx[:, None] > idx[None, :]
    decay = jnp.exp(jnp.where(incl, G[..., :, None] - G[..., None, :], -jnp.inf))
    kb = kc * bc[..., None]
    lower = jnp.where(strict, jnp.einsum('bhntd,bhnsd->bhnts', kb, kc) * decay, 0.0)
    a_mat = lower + jnp.eye(CHUNK, dtype=lower.dtype)
    rhs = jnp.concatenate([vc * bc[..., None], kb * jnp.exp(G)[..., None]], axis=-1)
    sol = lax.linalg.triangular_solve(a_mat, rhs, left_side=True, lower=True, unit_diagonal=True)
    u_base, w = sol[..., :DV], sol[..., DV:]
    qk = jnp.einsum('bhntd,bhnsd->bhnts', qc, kc) * decay
    q_dec = qc * jnp.exp(G)[..., None]
    k_dec = kc * jnp.exp(G[..., -1:] - G)[..., None]
    g_last = jnp.exp(G[..., -1])
    xs = tuple(jnp.moveaxis(t, 2, 0) for t in (u_base, w, qk, q_dec, k_dec, g_last))

    def step(s, inp):
        u_b, w_i, qk_i, qd_i, kd_i, gl_i = inp
        u = u_b - jnp.einsum('bhtd,bhde->bhte', w_i, s)
        o = jnp.einsum('bhtd,bhde->bhte', qd_i, s) + jnp.einsum('bhts,bhse->bhte', qk_i, u)
        s = gl_i[..., None, None] * s + jnp.einsum('bhsd,bhse->bhde', kd_i, u)
        return s, o

    s_fin, oc = lax.scan(step, s0, xs)
    return jnp.moveaxis(oc, 0, 2).reshape(B, H, T, DV), s_fin

def gdn_recurrent(q, k, v, g, beta, s0):
    def step(s, inp):
        qt, kt, vt, gt, bt = inp
        s = jnp.exp(gt)[..., None, None] * s
        u = bt[..., None] * (vt - jnp.einsum('bhd,bhde->bhe', kt, s))
        s = s + kt[..., None] * u[..., None, :]
        return s, jnp.einsum('bhd,bhde->bhe', qt, s)
    xs = tuple(jnp.moveaxis(t, 2, 0) for t in (q, k, v, g, beta))
    s_fin, o = lax.scan(step, s0, xs)
    return jnp.moveaxis(o, 0, 2), s_fin

def memory_kv(mem, g_mem, w_k, w_v):
    B = mem.shape[0]
    m = rmsnorm(mem, g_mem)
    k = jnp.einsum('bmd,de->bme', m, w_k).reshape(B, N_MEM, XA_HEADS, XA_HD)
    v = jnp.einsum('bmd,de->bme', m, w_v).reshape(B, N_MEM, XA_HEADS, XA_HD)
    return k, v

def cross_attention(h, mem_k, mem_v, w_q, w_o):
    B, T, _ = h.shape
    q = jnp.einsum('btd,de->bte', h, w_q).reshape(B, T, XA_HEADS, XA_HD)
    s = jnp.einsum('bthd,bmhd->bhtm', q, mem_k.astype(h.dtype)).astype(jnp.float32) * (XA_HD ** -0.5)
    p = jax.nn.softmax(s, axis=-1).astype(h.dtype)
    o = jnp.einsum('bhtm,bmhd->bthd', p, mem_v.astype(h.dtype)).reshape(B, T, D_MODEL)
    return jnp.einsum('btd,de->bte', o, w_o)

def block(x, mem_k, mem_v, conv_buf, s_gla, s_gdn, chunked,
          g_mix, w_in, gla_w_gate2, gla_b_gate, gla_g_out, gdn_conv_w, gdn_a_log,
          gdn_dt_bias, gdn_g_out, w_out, g_xattn, xa_w_q, xa_w_o,
          g_ffn, ffn_w_gate, ffn_w_up, ffn_w_down):
    B, T, _ = x.shape
    f32 = jnp.float32
    heads = lambda t, nh, d: t.reshape(B, T, nh, d).transpose(0, 2, 1, 3).astype(f32)

    h = rmsnorm(x, g_mix)
    proj = jnp.einsum('btd,de->bte', h, w_in)
    gq, gk, gv, gr, glr, cqkv, dz, da, db = jnp.split(proj, _split_points(IN_SIZES), axis=-1)

    q_a = heads(gq, GLA_HEADS, GLA_DK) * (GLA_DK ** -0.5)
    k_a = heads(gk, GLA_HEADS, GLA_DK)
    v_a = heads(gv, GLA_HEADS, GLA_DV)
    gate_pre = jnp.einsum('btr,rk->btk', glr, gla_w_gate2) + gla_b_gate
    la = heads(jax.nn.log_sigmoid(gate_pre.astype(f32)) / GLA_GATE_TEMP, GLA_HEADS, GLA_DK)

    xc = jnp.concatenate([conv_buf.astype(cqkv.dtype), cqkv], axis=1)
    conv = jax.nn.silu(sum(xc[:, j:j + T] * gdn_conv_w[j] for j in range(CONV_W)))
    new_buf = xc[:, T:]
    cq, ck, cv = jnp.split(conv, [GDN_KW, 2 * GDN_KW], axis=-1)
    q_b = l2norm(heads(cq, GDN_HEADS, GDN_DK)) * (GDN_DK ** -0.5)
    k_b = l2norm(heads(ck, GDN_HEADS, GDN_DK))
    v_b = heads(cv, GDN_HEADS, GDN_DV)
    beta = jax.nn.sigmoid(db.astype(f32)).transpose(0, 2, 1)
    g = (-jnp.exp(gdn_a_log.astype(f32)) * jax.nn.softplus(da.astype(f32) + gdn_dt_bias.astype(f32))).transpose(0, 2, 1)

    s_gla = s_gla.astype(f32)
    s_gdn = s_gdn.astype(f32)
    if chunked:
        o_a, s_gla = gla_chunked(q_a, k_a, v_a, la, s_gla)
        o_b, s_gdn = gdn_chunked(q_b, k_b, v_b, g, beta, s_gdn)
    else:
        o_a, s_gla = gla_recurrent(q_a, k_a, v_a, la, s_gla)
        o_b, s_gdn = gdn_recurrent(q_b, k_b, v_b, g, beta, s_gdn)

    o_a = rmsnorm(o_a.transpose(0, 2, 1, 3), gla_g_out) * jax.nn.silu(gr.astype(f32).reshape(B, T, GLA_HEADS, GLA_DV))
    o_b = rmsnorm(o_b.transpose(0, 2, 1, 3), gdn_g_out) * jax.nn.silu(dz.astype(f32).reshape(B, T, GDN_HEADS, GDN_DV))
    o = jnp.concatenate([o_a.reshape(B, T, GLA_WIDTH), o_b.reshape(B, T, GDN_WIDTH)], axis=-1).astype(x.dtype)
    x = x + jnp.einsum('bte,ed->btd', o, w_out)

    x = x + cross_attention(rmsnorm(x, g_xattn), mem_k, mem_v, xa_w_q, xa_w_o)

    h = rmsnorm(x, g_ffn)
    ff = jax.nn.silu(jnp.einsum('btd,df->btf', h, ffn_w_gate)) * jnp.einsum('btd,df->btf', h, ffn_w_up)
    x = x + jnp.einsum('btf,fd->btd', ff, ffn_w_down)
    return x, s_gla, s_gdn, new_buf

def setup_inputs(seed: int = 0) -> dict:
    key = jax.random.key(seed)
    ks = jax.random.split(key, 32)
    f32 = jnp.float32
    nrm = lambda k, shape, scale: jax.random.normal(k, shape, f32) * scale
    gain = lambda k, shape: 1.0 + 0.02 * jax.random.normal(k, shape, f32)
    return {
        "x_prompt": nrm(ks[0], (BATCH, SEQ, D_MODEL), 1.0),
        "x_sample": nrm(ks[1], (DEC_BATCH, DEC_SEQ, D_MODEL), 1.0),
        "mem_prompt": nrm(ks[2], (BATCH, N_MEM, D_MODEL), 1.0),
        "cache_mem_k": nrm(ks[3], (DEPTH, DEC_BATCH, N_MEM, XA_HEADS, XA_HD), 1.0),
        "cache_mem_v": nrm(ks[4], (DEPTH, DEC_BATCH, N_MEM, XA_HEADS, XA_HD), 1.0),
        "state_gla": nrm(ks[5], (DEPTH, DEC_BATCH, GLA_HEADS, GLA_DK, GLA_DV), 0.1),
        "state_gdn": nrm(ks[6], (DEPTH, DEC_BATCH, GDN_HEADS, GDN_DK, GDN_DV), 0.1),
        "state_conv": nrm(ks[7], (DEPTH, DEC_BATCH, CONV_W - 1, GDN_CONV_DIM), 1.0),
        "g_mix": gain(ks[8], (DEPTH, D_MODEL)),
        "w_in": nrm(ks[9], (DEPTH, D_MODEL, IN_COLS), D_MODEL ** -0.5),
        "gla_w_gate2": nrm(ks[10], (DEPTH, GLA_GATE_RANK, GLA_KW), GLA_GATE_RANK ** -0.5),
        "gla_b_gate": nrm(ks[11], (DEPTH, GLA_KW), 0.01),
        "gla_g_out": gain(ks[12], (DEPTH, GLA_DV)),
        "gdn_conv_w": nrm(ks[13], (DEPTH, CONV_W, GDN_CONV_DIM), CONV_W ** -0.5),
        "gdn_a_log": jnp.log(jax.random.uniform(ks[14], (DEPTH, GDN_HEADS), f32, 1.0, 16.0)),
        "gdn_dt_bias": 1.0 + nrm(ks[15], (DEPTH, GDN_HEADS), 0.01),
        "gdn_g_out": gain(ks[16], (DEPTH, GDN_DV)),
        "w_out": nrm(ks[17], (DEPTH, MIX_WIDTH, D_MODEL), MIX_WIDTH ** -0.5),
        "g_xattn": gain(ks[18], (DEPTH, D_MODEL)),
        "g_mem": gain(ks[19], (DEPTH, D_MODEL)),
        "xa_w_q": nrm(ks[20], (DEPTH, D_MODEL, D_MODEL), D_MODEL ** -0.5),
        "xa_w_k": nrm(ks[21], (DEPTH, D_MODEL, D_MODEL), D_MODEL ** -0.5),
        "xa_w_v": nrm(ks[22], (DEPTH, D_MODEL, D_MODEL), D_MODEL ** -0.5),
        "xa_w_o": nrm(ks[23], (DEPTH, D_MODEL, D_MODEL), D_MODEL ** -0.5),
        "g_ffn": gain(ks[24], (DEPTH, D_MODEL)),
        "ffn_w_gate": nrm(ks[25], (DEPTH, D_MODEL, D_FF), D_MODEL ** -0.5),
        "ffn_w_up": nrm(ks[26], (DEPTH, D_MODEL, D_FF), D_MODEL ** -0.5),
        "ffn_w_down": nrm(ks[27], (DEPTH, D_FF, D_MODEL), D_FF ** -0.5),
        "g_final": gain(ks[28], (D_MODEL,)),
    }

def reference(x_prompt, x_sample, mem_prompt, cache_mem_k, cache_mem_v, state_gla, state_gdn, state_conv,
              g_mix, w_in, gla_w_gate2, gla_b_gate, gla_g_out, gdn_conv_w, gdn_a_log, gdn_dt_bias, gdn_g_out,
              w_out, g_xattn, g_mem, xa_w_q, xa_w_k, xa_w_v, xa_w_o, g_ffn, ffn_w_gate, ffn_w_up, ffn_w_down,
              g_final):
    bp = x_prompt.shape[0]
    zero_conv = jnp.zeros((bp, CONV_W - 1, GDN_CONV_DIM), x_prompt.dtype)
    zero_gla = jnp.zeros((bp, GLA_HEADS, GLA_DK, GLA_DV), jnp.float32)
    zero_gdn = jnp.zeros((bp, GDN_HEADS, GDN_DK, GDN_DV), jnp.float32)
    xp, xs = x_prompt, x_sample
    p_gla, p_gdn, p_conv, p_mk, p_mv = [], [], [], [], []
    s_gla_l, s_gdn_l, s_conv_l = [], [], []
    for l in range(DEPTH):
        lp = (g_mix[l], w_in[l], gla_w_gate2[l], gla_b_gate[l], gla_g_out[l], gdn_conv_w[l], gdn_a_log[l],
              gdn_dt_bias[l], gdn_g_out[l], w_out[l], g_xattn[l], xa_w_q[l], xa_w_o[l],
              g_ffn[l], ffn_w_gate[l], ffn_w_up[l], ffn_w_down[l])
        mk, mv = memory_kv(mem_prompt, g_mem[l], xa_w_k[l], xa_w_v[l])
        xp, sa, sb, cb = block(xp, mk, mv, zero_conv, zero_gla, zero_gdn, True, *lp)
        p_gla.append(sa); p_gdn.append(sb); p_conv.append(cb); p_mk.append(mk); p_mv.append(mv)
        xs, sa, sb, cb = block(xs, cache_mem_k[l], cache_mem_v[l], state_conv[l], state_gla[l], state_gdn[l], False, *lp)
        s_gla_l.append(sa); s_gdn_l.append(sb); s_conv_l.append(cb)
    y_prompt = rmsnorm(xp, g_final)
    y_sample = rmsnorm(xs, g_final)
    new_gla_prompt = jnp.stack(p_gla).astype(state_gla.dtype)
    new_gdn_prompt = jnp.stack(p_gdn).astype(state_gdn.dtype)
    new_conv_prompt = jnp.stack(p_conv).astype(state_conv.dtype)
    new_mem_k_prompt = jnp.stack(p_mk).astype(cache_mem_k.dtype)
    new_mem_v_prompt = jnp.stack(p_mv).astype(cache_mem_v.dtype)
    new_gla_sample = jnp.stack(s_gla_l).astype(state_gla.dtype)
    new_gdn_sample = jnp.stack(s_gdn_l).astype(state_gdn.dtype)
    new_conv_sample = jnp.stack(s_conv_l).astype(state_conv.dtype)
    return (y_prompt, y_sample, new_gla_prompt, new_gdn_prompt, new_conv_prompt, new_mem_k_prompt, new_mem_v_prompt, new_gla_sample, new_gdn_sample, new_conv_sample)


_drawn_inputs = setup_inputs


def setup_inputs(seed=0):
    import zlib

    import numpy as np

    out = dict(_drawn_inputs(seed))
    spreads = {}
    factors = {'gla_b_gate': 8.0,
     'gla_g_out': 7.251,
     'gdn_dt_bias': 64.0,
     'gdn_g_out': 7.066,
     'g_xattn': 8.0,
     'g_mem': 2.908,
     'g_ffn': 4.237,
     'g_final': 7.396,
     'state_gdn': 8.0,
     'gdn_a_log': 8.0}
    for name, (base, spread) in spreads.items():
        noise = np.random.default_rng([zlib.crc32(name.encode()), seed]).standard_normal(out[name].shape)
        drawn = base * np.exp(spread * noise) if base else spread * noise
        out[name] = __import__('jax').numpy.asarray(drawn.astype(out[name].dtype))
    for name, factor in factors.items():
        out[name] = (out[name] * factor).astype(out[name].dtype)
    return out
```

```python
from contextlib import ExitStack

import concourse.bass as bass
from concourse import mybir

F32 = mybir.dt.float32
R32 = mybir.dt.float32r
U32 = mybir.dt.uint32
ACT = mybir.ActivationFunctionType
ALU = mybir.AluOpType
AX_X = mybir.AxisListType.X
ds = bass.ds

P = 128
D = 2048
KT = D // P
T = 256
NB = 8
TT = T + NB
NC = T // P
EPS = 1e-6
GH, GDK, GDV = 4, 128, 256
HB = 8
RANK = 16
CT = 3 * HB
CW = 4
COL_GLA = 0
COL_CODE = 3072
COL_GDN = COL_CODE + RANK
COL_Z = COL_GDN + CT * P
COL_AB = COL_Z + HB * P
IN_COLS = COL_AB + 2 * HB
XH, XD = 4, 512
NM = 256
DFF = 5632
HALF_K = DFF // 2 // P
DK_ = HALF_K // 2
GAIN_MIX, GAIN_X, GAIN_MEM, GAIN_FFN, GAIN_FINAL, GAIN_GATE_B, GAIN_GLA, GAIN_GDN = 0, 16, 32, 48, 64, 80, 84, 86
LEVELS = 8
UNIT_CREDIT = 2
LO_CREDIT = 4
ACC_CREDIT = 4


class Phase:

    def __init__(self, name, slots, k, s0, u0, t0):
        self.name, self.slots, self.k, self.s0, self.u0, self.t0 = name, slots, k, s0, u0, t0
        self.down = k == DK_
        self.loops = slots // 2
        self.narrow = self.down or name == "gu1"
        self.per = 2 if self.down else 4
        self.cols = NM if name in ("mem_k", "mem_v") else TT


def plan():
    runs = [("strip", 1, KT), ("gdn", 12, KT), ("gla", 12, KT), ("z", 4, KT), ("w_out", 8, KT), ("x_q", 8, KT),
            ("mem_k", 8, KT), ("mem_v", 8, KT), ("x_o", 8, KT), ("gu0", HALF_K, KT), ("dn0", 16, DK_),
            ("gu1", HALF_K, KT), ("dn1", 16, DK_)]
    s = u = t = 0
    out = {}
    for name, slots, k in runs:
        out[name] = Phase(name, slots, k, s, u, t)
        s += slots
        u += 1 if name == "strip" else 2 * slots
        t += 1 if name == "strip" else slots if k == DK_ else 2 * slots
    return out


def build(nc, a, o):
    PH = plan()
    LAST = PH["dn1"]
    with ExitStack() as ctx:
        def sem(name):
            return ctx.enter_context(nc.semaphore(name))

        base = (nc.sbuf_base + 31) // 32 * 32

        class Here:
            at = base

        def place(name, shape, dt, at=None):
            n = 4
            for d in shape[1:]:
                n *= d
            if at is None:
                at = Here.at
                Here.at += (n + 31) // 32 * 32
            return nc.alloc_sbuf_tensor_at(name, shape, dt, offset=at)

        cols = place("cols", [P, 87], F32)
        convw = place("convw", [P, CW * CT], F32)
        ident = place("ident", [P, P], F32)
        ones = place("ones", [P, P], F32)
        tri = place("tri", [P, P], F32)
        levels = place("levels", [P, LEVELS, P], F32)
        consts = place("consts", [P, 2], F32)
        dtb = place("dtb", [P, HB], F32)
        alog = place("alog", [P, HB], F32)
        rstd = place("rstd", [P, TT], F32)
        sq = place("sq", [P, 2, TT], F32)
        ssq = place("ssq", [P, TT], F32)
        small = place("small", [P, 16, 24], F32)
        x = place("x", [P, KT, TT], F32)
        raw = place("raw", [P, 2, KT, 256], F32)
        C0 = Here.at
        w_hi = [place(f"w_hi{b}", [P, KT, P], R32) for b in range(2)]
        w_lo = [place(f"w_lo{b}", [P, KT, P], R32) for b in range(2)]
        A0 = Here.at
        act_hi = place("act_hi", [P, KT, TT], R32)
        act_lo = place("act_lo", [P, KT, TT], R32)
        M0 = Here.at
        cv = place("cv", [P, CT, TT], F32)
        gla = place("gla", [P, 32, TT], F32)
        S0 = Here.at
        strip = place("strip", [P, TT], F32)
        tail = place("tail", [P, 11, CT], F32)
        pre = place("pre", [P, 2, CW - 1 + TT], F32)
        G0 = Here.at
        cst = place("cst", [P, CT, 3 * NB], F32)
        cacc = place("cacc", [P, 2, TT], F32)
        B0 = Here.at

        xrows = place("xrows", [P, NC, D], F32, M0)
        xsrow = place("xsrow", [NB, D], F32, M0 + 16384)
        grows = place("grows", [87, P], F32, C0)
        cwrows = place("cwrows", [CW * CT, P], F32, C0 + 512)
        crows = place("crows", [3 * NB, CT * P], F32, C0 + 1024)

        UNIT = 16 * P * 4
        gE = [place(f"gE{b}", [P, GH, T], F32, C0 + 4096 * b) for b in range(2)]
        gst = place("gst", [P, NB, GH, GDV], F32, C0 + UNIT)
        A1 = C0 + UNIT + 32768
        gq = [place(f"gq{b}", [P, GH, T], F32, A1 + 8192 * b) for b in range(2)]
        gk = [place(f"gk{b}", [P, GH, T], F32, A1 + 8192 * b + 4096) for b in range(2)]
        gb = place("gb", [P, GH, T], F32, A1 + 16384)
        gsc = place("gsc", [P, GH * NC, P], F32, A1 + 20480)
        gkd = place("gkd", [P, GH, T], F32, A1)
        gkdt = place("gkdt", [P, GH * NC, P], F32, A1 + 4096)
        gqd = place("gqd", [P, GH, P], F32, A1 + 8192)
        gs1 = place("gs1", [P, GH, GDV], F32, B0 + 8192)
        gsf = place("gsf", [P, GH, GDV], F32, B0 + 12288)
        gz = place("gz", [P, GH, TT], F32, B0)
        gaz = place("gaz", [P, GH, TT], F32, B0 + 4224)
        w2 = place("w2", [RANK, GH * GDK], F32, B0 + 8448)
        tails = place("tails", [4 * CT, 3, P], F32, B0 + 10496)
        gvt = place("gvt", [P, NC, GH * GDV], F32, B0)
        gvrow = place("gvrow", [NB, GH * GDV], F32, A1 + 12288)
        ges = place("ges", [P, GH, NB], F32, G0)
        gqe = place("gqe", [P, GH, NB], F32, G0 + 128)
        gkq = place("gkq", [P, GH, NB], F32, G0 + 256)
        gks = place("gks", [P, GH, NB], F32, G0 + 384)
        gel = place("gel", [P, GH, 1], F32, G0 + 512)
        got = place("got", [P, 8, NB], F32, G0 + 544)

        U = place("U", [P, 16, P], F32, C0)
        Tm = place("Tm", [P, 16, P], F32, C0 + UNIT)
        Y = place("Y", [P, 16, P], F32, C0 + 2 * UNIT)
        Bt = place("Bt", [P, 16, P], F32, C0 + 3 * UNIT)
        Lt = place("Lt", [P, 16, P], F32, C0 + 4 * UNIT)
        QK = place("QK", [P, 16, P], F32, C0 + 5 * UNIT)
        ktok = place("ktok", [P, 16, P], F32, C0 + 6 * UNIT)
        vb = place("vb", [P, 16, P], F32, C0 + 7 * UNIT)
        sqb = place("sqb", [P, 16, TT], F32, A1)
        bst = place("bst", [P, NB, HB, P], F32, C0 + UNIT)
        EG = place("EG", [P, HB, P], F32, B0)
        kbg = place("kbg", [P, HB, P], F32, B0 + 4096)
        nw = place("nw", [P, HB, P], F32, B0 + 8192)
        bs1 = place("bs1", [P, HB, P], F32, B0 + 12288)
        uu = place("uu", [P, 16, P], F32, S0)
        bsf = place("bsf", [P, HB, P], F32, B0)
        urow = place("urow", [HB * NB, P], F32, B0 + 4096)
        sbc = place("sbc", [P, 2, NB * HB], F32, B0 + 4608)
        sdiag = place("sdiag", [NB, 2, NB, HB], F32, B0 + 5120)
        skq = place("skq", [P, NB, HB], F32, B0 + 5632)
        su = place("su", [P, NB, HB], F32, B0 + 5888)
        so = place("so", [P, NB, HB], F32, B0 + 6144)
        skq2 = place("skq2", [P, NB, HB], F32, B0 + 6400)
        nsq = place("nsq", [P, 16, TT], F32, A1)

        ow_hi = place("ow_hi", [P, KT, TT], R32, M0)
        ow_lo = place("ow_lo", [P, KT, TT], R32, M0 + 4 * KT * TT)
        Q0 = M0 + 8 * KT * TT
        q = place("q", [P, KT, TT], F32, Q0)
        kT = place("kT", [P, KT, NM], F32, Q0 + 4 * KT * TT)
        vm = place("vm", [P, 2, D], F32, Q0 + 4 * KT * (TT + NM))
        mrows = place("mrows", [P, 2, D], F32, Q0 + 4 * KT * (TT + NM))
        vT = place("vT", [P, KT, NM], F32, A0)
        km = place("km", [P, 2, D], F32, A0 + 16384)
        cache = [place(f"cache{b}", [P, 2, D], F32, C0 + 16384 * b) for b in range(2)]
        pr = place("pr", [P, XH * NC, NM], F32, A0)
        prT = place("prT", [P, XH, 2, T], F32, A0 + 8192)
        qrow = place("qrow", [NB, D], F32, A0 + 16384)
        sc_s = place("sc_s", [P, 2, NB * XH], F32, A0 + 24576)
        p_s = place("p_s", [NB * XH, NM], F32, A0 + 25088)
        pT_s = place("pT_s", [P, 2, NB * XH], F32, A0 + 26112)
        osm = place("osm", [P, KT, NB], F32, A0 + 26880)

        ff_hi = place("ff_hi", [P, HALF_K, TT], R32, M0)
        ff_lo = place("ff_lo", [P, HALF_K, TT], R32, M0 + 4 * HALF_K * TT)
        F0 = M0 + 8 * HALF_K * TT
        g_s = place("g_s", [P, 2, TT], F32, F0)
        u_s = place("u_s", [P, 2, TT], F32, F0 + 8 * TT)
        f_s = place("f_s", [P, 2, TT], F32, F0 + 16 * TT)
        yT = place("yT", [P, KT, TT], F32, A0)
        yrows = place("yrows", [P, NC, D], F32, F0 + 24 * TT)
        ysrow = place("ysrow", [NB, D], F32, C0)

        ps = ctx.enter_context(nc.psum_tensor("ps", [P, 8, 512], F32))
        W4 = 4

        raw_landed = [sem(f"raw_landed{b}") for b in range(2)]
        hi_split = sem("hi_split")
        lo_split = sem("lo_split")
        units_done = sem("units_done")
        acc_free = sem("acc_free")
        rows_landed = sem("rows_landed")
        crows_landed = sem("crows_landed")
        xrows_landed = sem("xrows_landed")
        mrows_landed = sem("mrows_landed")
        consts_ready = sem("consts_ready")
        cols_turned = sem("cols_turned")
        cols_ready = sem("cols_ready")
        x_turned = sem("x_turned")
        x_ready = sem("x_ready")
        x_split = sem("x_split")
        pool_order = sem("pool_order")
        sq_ready = sem("sq_ready")
        ssq_zero = sem("ssq_zero")
        m_taken = sem("m_taken")
        x_taken = sem("x_taken")
        kv_out = sem("kv_out")
        scalars_landed = sem("scalars_landed")
        tails_out = sem("tails_out")
        ff_split = sem("ff_split")
        dve_credit = sem("dve_credit")
        cache_landed1 = sem("cache_landed1")
        ssq_ready = sem("ssq_ready")
        sum_ready = sem("sum_ready")
        rstd_ready = sem("rstd_ready")
        dve_order = sem("dve_order")
        act_order = sem("act_order")
        conv_ready = sem("conv_ready")
        conv_done = sem("conv_done")
        gate_act = sem("gate_act")
        gate_in = sem("gate_in")
        outs = sem("outs")

        class Count:
            dve = act = pool = out = 0

        def dve_link(dve, ins):
            Count.dve += 1
            ins.then_inc(dve_order, 1)
            dve.wait_ge(dve_order, Count.dve)

        def act_link(act, ins):
            Count.act += 1
            ins.then_inc(act_order, 1)
            act.wait_ge(act_order, Count.act)

        def pool_link(pool, ins):
            Count.pool += 1
            ins.then_inc(pool_order, 1)
            pool.wait_ge(pool_order, Count.pool)

        def kview(w, k0, k, c0, n):
            return w.rearrange("(k p) n -> p k n", p=P)[:, k0:k0 + k, ds(c0, n)]

        wi, wo, xq, xk, xv, xo = (a[n][0] for n in ("w_in", "w_out", "xa_w_q", "xa_w_k", "xa_w_v", "xa_w_o"))
        wg, wu, wd = (a[n][0] for n in ("ffn_w_gate", "ffn_w_up", "ffn_w_down"))

        def load(sp, ph, i, j):
            s = ph.s0 + 2 * i + j
            r = (ph.s0 + j) % 2
            sp.wait_ge(lo_split, 2 * s + 1)
            if ph.name == "strip":
                parts = [(raw[:, r, :, 0:32], kview(wi, 0, KT, COL_CODE, 32)),
                         (raw[:, r, :, 32:P], kview(wi, 0, KT, IN_COLS - 96, 96))]
            elif ph.name in ("gu0", "gu1"):
                c0 = (i * 2 + j) * P + (HALF_K * P if ph.name == "gu1" else 0)
                parts = [(raw[:, r, :, 0:P], kview(wg, 0, KT, c0, P)), (raw[:, r, :, P:2 * P], kview(wu, 0, KT, c0, P))]
            elif ph.down:
                k0 = (HALF_K if ph.name == "dn1" else 0) + j * DK_
                c0 = i * 256
                parts = [(raw[:, r, 0:6, :], kview(wd, k0, 6, c0, 256)),
                         (raw[:, r, 6:DK_, :], kview(wd, k0 + 6, DK_ - 6, c0, 256))]
            else:
                w = {"gdn": wi, "gla": wi, "z": wi, "w_out": wo, "x_q": xq, "mem_k": xk, "mem_v": xv, "x_o": xo}[ph.name]
                c0 = i * 512 + j * 256 + {"gdn": COL_GDN, "z": COL_Z}.get(ph.name, 0)
                parts = [(raw[:, r, 8 * m:8 * m + 8, :], kview(w, 8 * m, 8, c0, 256)) for m in range(2)]
            for dst, src in parts:
                sp.dma_start(dst, src).then_inc(raw_landed[r], 16)

        def unit_of(ph, i, u):
            s = ph.s0 + u // 2
            return s % 2, 32 * (s // 2 + i + 1), u % 2, (ph.u0 + u) % 2, ph.u0 + 4 * i + u

        def split_hi(act, ph, i, u):
            r, landed, half, b, n = unit_of(ph, i, u)
            act.wait_ge(raw_landed[r], landed)
            act.wait_ge(units_done, n + 1)
            act.activation(w_hi[b][:, 0:ph.k, :], raw[:, r, 0:ph.k, half * P:half * P + P], ACT.Copy)\
               .then_inc(hi_split, 1)

        def split_lo(dve, ph, i, u):
            r, landed, half, b, n = unit_of(ph, i, u)
            dve.wait_ge(hi_split, n + 1)
            dve.tensor_tensor(w_lo[b][:, 0:ph.k, :], raw[:, r, 0:ph.k, half * P:half * P + P],
                              w_hi[b][:, 0:ph.k, :], ALU.subtract).then_inc(lo_split, 1)

        def products(pe, ph, i, u, hi, lo, k0=0):
            b, n = (ph.u0 + u) % 2, ph.u0 + 4 * i + u
            t = ph.t0 + ph.per * i + (u % 2 if ph.down else u)
            first = not ph.down or u < 2
            last = not ph.down or u >= 2
            if first:
                pe.wait_ge(acc_free, t + (3 if ph.narrow else 1))
            pe.wait_ge(lo_split, n + 1 + LO_CREDIT)
            kk = k0 + (DK_ * (u // 2) if ph.down else 0)
            for k in range(ph.k):
                for m, (w, v) in enumerate(((w_lo, hi), (w_hi, lo), (w_hi, hi))):
                    mm = pe.matmul(ps[:, acc(ph, u), 0:ph.cols], w[b][:, k, :], v[:, kk + k, 0:ph.cols],
                                   start=first and k == 0 and m == 0,
                                   stop=last and k == ph.k - 1 and m == 2)
            mm.then_inc(units_done, 1)

        def acc(ph, u):
            return (ph.t0 + (u % 2 if ph.down else u)) % 4

        def phase_pe(pe, ph, hi, lo):
            with pe.Fori(0, ph.loops) as i:
                for u in range(4):
                    products(pe, ph, i, u, hi, lo)

        def phase_split(eng, split, ph, take, nxt):
            with eng.Fori(0, ph.loops - 1) as i:
                for u in range(4):
                    take(ph, i, u)
                    split(eng, ph, i, u + 2) if u < 2 else split(eng, ph, i + 1, u - 2)
            for u in range(4):
                take(ph, ph.loops - 1, u)
                if u < 2:
                    split(eng, ph, ph.loops - 1, u + 2)
                elif nxt is not None:
                    split(eng, nxt, 0, u - 2)

        X_INIT, X_OUT, X_ATT, X_FFN = KT, 2 * KT, 3 * KT, 4 * KT

        N = {}
        for name in ("strip_done turned scalars prep gla_pre gla_exp gla_lvl gla_scored gla_picked gla_turned "
                     "gla_tok gla_mm gla_out gla_s gla_smm gla_sst gla_norm sstate_landed state_out gla_dec gla_qe gla_row "
                     "gla_bc gla_sc gla_srow gdn_sq gdn_sum gdn_ln gdn_normed gdn_turned gdn_ktok gdn_vb gdn_g gdn_gcol gdn_scal "
                     "gdn_pair gdn_dmin gdn_dexp gdn_lt gdn_qkm gdn_bt gdn_t0 y_done y_copied tyuy_done inv_ready "
                     "gdn_kbg gdn_f1 gdn_e1 gdn_f2 gdn_e2 gdn_f3 gdn_e3 gdn_f4 gdn_e4 bst_landed gdn_sx gdn_sbc gdn_sval "
                     "gdn_scaled gdn_ub gdn_ubt gdn_surow gdn_u norm_sq norm_sum norm_rb norm_g silu_g o_ready tails_turned tails_copied "
                     "m_turned m_ready mrstd kv_turned kv_copied att_qk att_max att_exp att_norm att_pturned att_pT att_o att_oe "
                     "gdn_uspread s_smq s_qrow s_qb s_dot cache_landed s_st s_sm s_exp s_pn s_ptt s_pT s_o s_oe o_ready0 y_norm y_turned y_copied_act y_copied_dve "
                     "gla_eexp gla_qk mem_sq qe_exp gla_la gla_bgate").split():
            N[name] = sem(name)

        def W(eng, name, n):
            eng.wait_ge(N[name], n)

        def tile_wait(eng, ph, i, u):
            eng.wait_ge(units_done, ph.u0 + 4 * i + u + 1 + UNIT_CREDIT)

        def out_of(ph, u):
            return ps[:, acc(ph, u), 0:ph.cols]

        def dve_take(dve):
            R = rstd[:, :]

            def residual(ph, i, u, base, gain):
                n = i * 2 + (u - 2) if ph.down else i * 4 + u
                tile_wait(dve, ph, i, u)
                dve.tensor_tensor(x[:, ds(n, 1), :], x[:, ds(n, 1), :], out_of(ph, u), ALU.add).then_inc(x_ready, 1)
                dve.wait_ge(x_ready, n + base + KT + 1)
                if gain is not None:
                    g = cols[:, ds(n + gain, 1)]
                    dve.tensor_scalar(act_hi[:, ds(n, 1), :], x[:, ds(n, 1), :], g, None, ALU.mult).then_inc(x_split, 1)
                    dve.wait_ge(x_split, n + base + 1)
                    dve.scalar_tensor_tensor(out=act_lo[:, ds(n, 1), :], in0=x[:, ds(n, 1), :], scalar=g,
                                             in1=act_hi[:, ds(n, 1), :], op0=ALU.mult, op1=ALU.subtract)\
                       .then_inc(acc_free, 1)

            def scaled(dst, r):
                def f(ph, i, u):
                    tile_wait(dve, ph, i, u)
                    dve.tensor_tensor(dst[:, ds(i * 4 + u, 1), 0:ph.cols], out_of(ph, u), r, ALU.mult)\
                       .then_inc(acc_free, 1)
                return f

            def gdn(ph, i, u):
                n = i * 4 + u
                b = u % 2
                tile_wait(dve, ph, i, u)
                dve.wait_ge(conv_done, i * 4 + u + 1)
                dve.tensor_tensor(pre[:, b, 3:3 + TT], out_of(ph, u), R, ALU.mult).then_inc(acc_free, 1)
                dve.wait_ge(acc_free, ph.t0 + n + 1 + ACC_CREDIT)
                for j in range(CW):
                    w = convw[:, ds(n + j * CT, 1)]
                    for dst, src in ((cacc[:, b, 0:T], pre[:, b, j:j + T]),
                                     (cacc[:, b, T:TT], cst[:, ds(n, 1), j * NB:(j + 1) * NB] if j < CW - 1
                                      else pre[:, b, 3 + T:3 + TT])):
                        if j == 0:
                            ins = dve.tensor_scalar(dst, src, w, None, ALU.mult)
                        else:
                            ins = dve.scalar_tensor_tensor(out=dst, in0=src, scalar=w, in1=dst, op0=ALU.mult,
                                                           op1=ALU.add)
                    ins.then_inc(conv_ready, 1)
                    dve.wait_ge(conv_ready, n * 4 + j + 1)

            def gate_up(half):
                def f(ph, i, u):
                    n = 2 * i + u // 2
                    c = HALF_K * half + n
                    b = u // 2
                    tile_wait(dve, ph, i, u)
                    if u % 2 == 0:
                        dve.tensor_tensor(g_s[:, b, :], out_of(ph, u), R, ALU.mult).then_inc(acc_free, 1)
                        return
                    dve.tensor_tensor(u_s[:, b, :], out_of(ph, u), R, ALU.mult).then_inc(acc_free, 1)
                    dve.wait_ge(gate_act, c + 1)
                    dve.wait_ge(acc_free, ph.t0 + 4 * i + u + 1 + ACC_CREDIT)
                    dve.tensor_tensor(f_s[:, b, :], g_s[:, b, :], u_s[:, b, :], ALU.mult).then_inc(gate_in, 1)
                    dve.wait_ge(gate_in, 2 * c + 1)
                    dve.tensor_copy(ff_hi[:, ds(n, 1), :], f_s[:, b, :]).then_inc(gate_in, 1)
                    dve.wait_ge(gate_in, 2 * c + 2)
                    dve.tensor_tensor(ff_lo[:, ds(n, 1), :], f_s[:, b, :], ff_hi[:, ds(n, 1), :], ALU.subtract)\
                       .then_inc(ff_split, 1)
                return f

            def down(last):
                def f(ph, i, u):
                    if u < 2:
                        return
                    n = i * 2 + (u - 2)
                    tile_wait(dve, ph, i, u)
                    ins = dve.tensor_tensor(x[:, ds(n, 1), :], x[:, ds(n, 1), :], out_of(ph, u), ALU.add)
                    ins.then_inc(acc_free, 1)
                return f

            return scaled, gdn, residual, gate_up, down

        scaled_by = None
        G2 = [a["gla_w_gate2"][0], a["gla_b_gate"][0]]
        DA, DB, TMP, SP_, EB, EAL, G_, BETA, GC, GL, GD, EG1, KD, EGL, BG = range(15)

        def sm(k):
            return small[:, k, :].rearrange("p (h c) -> p h c", c=3)

        def unit_ps(b0, n):
            return ps[:, b0 + n // 4, (n % 4) * P:(n % 4) * P + P]

        def heads_of(bank):
            return ps[:, bank, :].rearrange("p (u t) -> p u t", u=4)

        def halves(v, m):
            return v.rearrange("p h (n s m) -> p h n s m", s=2, m=m)

        block = ctx.enter_context(nc.Block())

        @block.sync
        def _(sp):
            for name, r0, n in (("g_mix", GAIN_MIX, 16), ("g_xattn", GAIN_X, 16), ("g_mem", GAIN_MEM, 16),
                                ("g_ffn", GAIN_FFN, 16), ("g_final", GAIN_FINAL, 16),
                                ("gla_b_gate", GAIN_GATE_B, 4), ("gla_g_out", GAIN_GLA, 2), ("gdn_g_out", GAIN_GDN, 1)):
                src = a[name] if name == "g_final" else a[name][0]
                sp.dma_start(grows[r0:r0 + n, :], src.rearrange("(r p) -> r p", p=P)).then_inc(rows_landed, 16)
            sp.dma_start(cwrows[:, :], a["gdn_conv_w"][0].rearrange("j (t p) -> (j t) p", p=P)).then_inc(rows_landed, 16)
            sp.dma_start(crows[:, :], a["state_conv"][0].rearrange("b j c -> (b j) c")).then_inc(crows_landed, 16)
            sp.dma_start(xrows[:, :, :], a["x_prompt"][0].rearrange("(c p) d -> p c d", p=P)).then_inc(xrows_landed, 16)
            sp.dma_start(xsrow[:, :], a["x_sample"].rearrange("b s d -> (b s) d")).then_inc(xrows_landed, 16)
            load(sp, PH["strip"], 0, 0)
            sp.dma_start(w2[:, :], G2[0]).then_inc(scalars_landed, 16)
            sp.dma_start(dtb[:, :], a["gdn_dt_bias"][0].partition_broadcast(P)).then_inc(scalars_landed, 16)
            sp.dma_start(alog[:, :], a["gdn_a_log"][0].partition_broadcast(P)).then_inc(scalars_landed, 16)
            sp.dma_start(o["conv_s"][0][:, 0:CW - 2, :], a["state_conv"][0][:, 1:CW - 1, :]).then_inc(outs, 16)

            def stream(name):
                ph = PH[name]
                with sp.Fori(0, ph.loops) as i:
                    for j in range(2):
                        load(sp, ph, i, j)

            stream("gdn")
            stream("gla")
            stream("z")
            for j in range(2):
                load(sp, PH["w_out"], 0, j)
            sp.wait_ge(units_done, PH["w_out"].u0 + UNIT_CREDIT)
            sp.dma_start(gst[:, :, :, :], a["state_gla"][0].rearrange("b h k v -> k b h v")).then_inc(N["sstate_landed"], 16)
            W(sp, "tails_copied", 3)
            sp.dma_start(o["conv_p"][0, 0].rearrange("j (t p) -> (j t) p", p=P), tails[0:3 * CT, 0, :]).then_inc(tails_out, 16)
            for b in range(NB):
                sp.dma_start(o["conv_s"][0][b, CW - 2].rearrange("(t p) -> t p", p=P),
                             tails[(b % 4) * CT:(b % 4 + 1) * CT, 1 + b // 4, :]).then_inc(tails_out, 16)
            W(sp, "gla_out", 3)
            sp.dma_start(o["gla_p"][0, 0].rearrange("h k v -> k h v"), gsf[:, :, :]).then_inc(N["state_out"], 16)
            W(sp, "gla_srow", NB)
            sp.dma_start(o["gla_s"][0].rearrange("b h k v -> k b h v"), gst[:, :, :, :]).then_inc(N["state_out"], 16)
            W(sp, "inv_ready", 4 * (LEVELS - 2))
            W(sp, "tyuy_done", 4 * (LEVELS - 2))
            sp.dma_start(bst[:, :, :, :], a["state_gdn"][0].rearrange("b h k v -> k b h v")).then_inc(N["bst_landed"], 16)
            W(sp, "gdn_e4", 4)
            sp.dma_start(o["gdn_p"][0, 0].rearrange("h k v -> k h v"), bsf[:, :, :]).then_inc(N["state_out"], 16)
            W(sp, "gdn_surow", 16)
            sp.dma_start(o["gdn_s"][0].rearrange("b h k v -> k b h v"), bst[:, :, :, :]).then_inc(N["state_out"], 16)

            def rest(name, first):
                ph = PH[name]
                if first:
                    with sp.Fori(1, ph.loops) as i:
                        for j in range(2):
                            load(sp, ph, i, j)
                else:
                    stream(name)

            rest("w_out", True)
            W(sp, "o_ready", 16)
            W(sp, "state_out", 16 * 4)
            sp.dma_start(mrows[:, :, :], a["mem_prompt"][0].rearrange("(c p) d -> p c d", p=P)).then_inc(mrows_landed, 16)
            rest("x_q", False)
            rest("mem_k", False)
            rest("mem_v", False)
            for j in range(2):
                load(sp, PH["x_o"], 0, j)
            sp.wait_ge(units_done, PH["x_o"].u0 + UNIT_CREDIT)
            for n in range(2 * NB):
                if n >= 2:
                    if n - 2 < NB:
                        W(sp, "s_dot", n - 1)
                    else:
                        W(sp, "s_o", n - 1 - NB)
                src = a["cache_mem_k" if n < NB else "cache_mem_v"][0][n % NB].rearrange("(m p) h d -> p m (h d)", p=P)
                for m in range(2):
                    sp.dma_start(cache[n % 2][:, m, :], src[:, m, :]).then_inc(N[f"cache_landed"] if n % 2 == 0 else cache_landed1, 16)
                if n == 0:
                    W(sp, "kv_copied", 16)
                    for m, dst in ((0, "mem_k"), (1, "mem_v")):
                        sp.dma_start(o[dst][0, 0].rearrange("(c p) h d -> p c (h d)", p=P), (km, vm)[m][:, :, :])\
                          .then_inc(kv_out, 16)
            rest("x_o", True)
            for name in ("gu0", "dn0", "gu1", "dn1"):
                stream(name)
            W(sp, "y_copied_act", 4)
            W(sp, "y_copied_dve", 4)
            sp.dma_start(o["y_p"][0].rearrange("(c p) d -> p c d", p=P), yrows[:, :, :]).then_inc(outs, 16)
            sp.dma_start(o["y_s"].rearrange("b s d -> (b s) d"), ysrow[:, :]).then_inc(outs, 16)
            sp.wait_ge(outs, 16 * 3)
            sp.wait_ge(tails_out, 16 * (1 + NB))
            sp.wait_ge(kv_out, 16 * 2)

        @block.gpsimd
        def _(pool):
            pool_link(pool, pool.memset(levels[:, :, :], 0.0))
            pool_link(pool, pool.memset(consts[:, 0:1], EPS))
            pool_link(pool, pool.memset(consts[:, 1:2], 1.0))
            pool_link(pool, pool.memset(ones[:, :], 1.0))
            pool_link(pool, pool.affine_select(out=levels[:, 0, :], in_=levels[:, 0, :], compare_op=ALU.not_equal,
                                               fill=1.0, base=0, pattern=[[-1, P]], channel_multiplier=1))
            pool_link(pool, pool.tensor_copy(ident[:, :], levels[:, 0, :]))
            pool_link(pool, pool.affine_select(out=tri[:, :], in_=ones[:, :], compare_op=ALU.is_ge, fill=0.0, base=0,
                                               pattern=[[1, P]], channel_multiplier=-1))
            for l in range(1, LEVELS):
                m = 1 << (l - 1)
                v = levels[:, l, :].rearrange("p (n s m) -> p n s m", s=2, m=m)[:, :, 1, :]
                nb = P // (2 * m)
                pool_link(pool, pool.memset(v, 1.0))
                pool_link(pool, pool.affine_select(out=v, in_=v, compare_op=ALU.is_ge, fill=0.0, base=0,
                                                   pattern=[[-2 * m, nb], [0, m]], channel_multiplier=1))
                pool_link(pool, pool.affine_select(out=v, in_=v, compare_op=ALU.is_ge, fill=0.0, base=m - 1,
                                                   pattern=[[2 * m, nb], [0, m]], channel_multiplier=-1))
            pool.memset(pre[:, :, 0:CW - 1], 0.0).then_inc(consts_ready, 1)

            def squares(k, waits, src, width):
                base = KT * (k - 1)
                waits(0)
                pool.memset(ssq[:, 0:width], 0.0).then_inc(ssq_zero, 1)
                pool.wait_ge(ssq_zero, k)
                with pool.Fori(0, KT // 2) as i:
                    for b in range(2):
                        n = i * 2 + b
                        waits(n)
                        pool.tensor_tensor(sq[:, b, 0:width], src[:, ds(n, 1), 0:width], src[:, ds(n, 1), 0:width],
                                           ALU.mult).then_inc(sq_ready, 1)
                        pool.wait_ge(sq_ready, n + base + 1)
                        pool.tensor_tensor(ssq[:, 0:width], ssq[:, 0:width], sq[:, b, 0:width], ALU.add)\
                            .then_inc(ssq_ready, 1)

            def taken(ph):
                return lambda n: pool.wait_ge(acc_free, n + ph.t0 + 1 + ACC_CREDIT)

            squares(1, lambda n: pool.wait_ge(x_ready, n + 1), x, TT)
            pool.wait_ge(acc_free, PH["w_out"].t0 + ACC_CREDIT)
            for b in range(2):
                pool.memset(gq[b][:, :, :], 0.0)
                last = pool.memset(gk[b][:, :, :], 0.0)
            last.then_inc(N["prep"], 1)
            for g in range(4):
                W(pool, "gdn_lt", g + 1)
                v = QK[:, 4 * g:4 * g + 4, :]
                pool.tensor_tensor(v, v, tri[:, :].unsqueeze(1).broadcast_to([P, 4, P]), ALU.mult)\
                    .then_inc(N["gdn_qkm"], 1)
                pool.tensor_tensor(Bt[:, 4 * g:4 * g + 4, :], Lt[:, 4 * g:4 * g + 4, :],
                                   levels[:, 1, :].unsqueeze(1).broadcast_to([P, 4, P]), ALU.mult)\
                    .then_inc(N["gdn_bt"], 1)
            for l in range(2, LEVELS):
                for g in range(4):
                    if l == 2:
                        W(pool, "gdn_t0", g + 1)
                        W(pool, "inv_ready", g + 1)
                    else:
                        W(pool, "y_done", 4 * (l - 3) + g + 1)
                    pool.tensor_tensor(Bt[:, 4 * g:4 * g + 4, :], Lt[:, 4 * g:4 * g + 4, :],
                                       levels[:, l, :].unsqueeze(1).broadcast_to([P, 4, P]), ALU.mult)\
                        .then_inc(N["gdn_bt"], 1)
            W(pool, "gdn_sval", 1)
            for b in range(NB):
                pool.tensor_tensor(bst[:, b, :, :], bst[:, b, :, :],
                                   sbc[:, 0, b * HB:(b + 1) * HB].unsqueeze(2).broadcast_to([P, HB, P]), ALU.mult)\
                    .then_inc(N["gdn_ubt"], 1)
            squares(2, taken(PH["w_out"]), x, TT)
            squares(3, lambda n: pool.wait_ge(m_taken, n + 1), kT, NM)
            squares(4, taken(PH["x_o"]), x, TT)
            squares(5, taken(PH["dn1"]), x, TT)

        @block.tensor
        def _(pe):
            def turn(dst, src):
                return pe.transpose(dst, src, ident[0:src.shape[0], 0:src.shape[0]])

            def sum_squares(k, width):
                pe.wait_ge(ssq_ready, KT * k)
                pe.matmul(ps[:, 7, 0:width], ones[:, :], ssq[:, 0:width], start=True, stop=True).then_inc(sum_ready, 1)

            pe.wait_ge(consts_ready, 1)
            pe.wait_ge(rows_landed, 16 * 9)
            turn(ps[:, 4, 0:87], grows[:, :])
            turn(ps[:, 4, P:P + CW * CT], cwrows[:, :])
            pe.wait_ge(crows_landed, 16)
            for t in range(CT):
                mm = turn(ps[:, 5 + t // 12, (t % 12) * 24:(t % 12) * 24 + 24], crows[:, t * P:(t + 1) * P])
            mm.then_inc(cols_turned, 1)
            pe.wait_ge(xrows_landed, 32)
            pe.wait_ge(cols_ready, 3)
            for k in range(KT):
                if k >= 4:
                    pe.wait_ge(x_taken, k - 3)
                for c in range(NC):
                    turn(ps[:, W4 + k % 4, c * P:(c + 1) * P], xrows[:, c, k * P:(k + 1) * P])
                turn(ps[:, W4 + k % 4, T:TT], xsrow[:, k * P:(k + 1) * P]).then_inc(x_turned, 1)
            pe.wait_ge(x_taken, KT)
            sum_squares(1, TT)
            products(pe, PH["strip"], 0, 0, act_hi, act_lo)
            phase_pe(pe, PH["gdn"], act_hi, act_lo)
            phase_pe(pe, PH["gla"], act_hi, act_lo)
            phase_pe(pe, PH["z"], act_hi, act_lo)

            pe.wait_ge(acc_free, PH["w_out"].t0 + ACC_CREDIT)
            for c in range(NC):
                turn(ps[:, 0, c * P:(c + 1) * P], strip[:, c * P:(c + 1) * P])
            turn(ps[0:NB, 0, 2 * P:3 * P], strip[:, T:TT])
            pe.wait_ge(conv_done, CT + 2)
            for g, (j0, nj) in enumerate(((0, 3), (3, 4), (7, 4))):
                mm = turn(ps[0:nj * CT, 1, g * P:(g + 1) * P], tail[:, j0:j0 + nj, :].rearrange("p j t -> p (j t)"))
            mm.then_inc(N["turned"], 1)
            pe.wait_ge(scalars_landed, 16 * 3)
            for h in range(GH):
                mm = pe.matmul(ps[:, 4 + h, 0:TT], w2[:, h * P:(h + 1) * P], strip[0:RANK, :], start=True, stop=True)
            mm.then_inc(N["gla_pre"], 1)
            W(pe, "gdn_g", 1)
            for c in range(NC):
                pe.matmul(ps[:, 2, c * HB:(c + 1) * HB], tri[:, :], sm(G_)[:, :, c], start=True, stop=True)
                mm = pe.matmul(ps[:, 2, (2 + c) * HB:(3 + c) * HB], ones[:, :], sm(G_)[:, :, c], start=True, stop=True)
            mm.then_inc(N["gdn_gcol"], 1)
            W(pe, "gla_la", 1)
            W(pe, "gdn_scal", 1)
            for n in range(NC * 8):
                c, t = n // 8, n % 8
                mm = turn(unit_ps(4, n), gla[:, 8 + t, c * P:(c + 1) * P])
            mm.then_inc(N["gla_turned"], 1)
            for l in range(LEVELS):
                qs, ks = (gla[:, 0:GH, :], gla[:, GH:2 * GH, :]) if l == 0 else (gq[l % 2], gk[l % 2])
                if l:
                    W(pe, "gla_lvl", l)
                if l >= 2:
                    W(pe, "gla_picked", l - 1)
                for n in range(GH * NC):
                    h, c = n // NC, n % NC
                    mm = pe.matmul(unit_ps(2 * (l % 2), n), ks[:, h, c * P:(c + 1) * P], qs[:, h, c * P:(c + 1) * P],
                                   start=True, stop=True)
                mm.then_inc(N["gla_scored"], 1)
            W(pe, "gla_picked", LEVELS)
            W(pe, "gla_dec", LEVELS + 1)
            for n in range(GH * NC):
                mm = turn(unit_ps(0, n), gkd[:, n // NC, (n % NC) * P:(n % NC + 1) * P])
            for t in range(8):
                mm = turn(ps[0:NB, 2 + t // 4, (t % 4) * P:(t % 4 + 1) * P], gla[:, 8 + t, T:TT])
            mm.then_inc(N["gla_turned"], 1)
            W(pe, "gla_tok", 8)
            for h in range(GH):
                pe.matmul(ps[:, h // 2, (h % 2) * GDV:(h % 2 + 1) * GDV], gkdt[:, 2 * h, :],
                          gvt[:, 0, h * GDV:(h + 1) * GDV], start=True, stop=True)
            for j in range(8):
                mm = pe.matmul(unit_ps(4, j), gvt[:, 0, j * P:(j + 1) * P], gsc[:, 2 * (j // 2), :], start=True, stop=True)
            mm.then_inc(N["gla_mm"], 1)
            W(pe, "gla_out", 1)
            W(pe, "gla_s", 1)
            for j in range(8):
                h, e = j // 2, j % 2
                pe.matmul(unit_ps(6, j), gs1[:, h, e * P:(e + 1) * P], gqd[:, h, :], start=True, stop=False)
                mm = pe.matmul(unit_ps(6, j), gvt[:, 1, j * P:(j + 1) * P], gsc[:, 2 * h + 1, :], start=False, stop=True)
            for h in range(GH):
                mm = pe.matmul(ps[:, h // 2, (h % 2) * GDV:(h % 2 + 1) * GDV], gkdt[:, 2 * h + 1, :],
                               gvt[:, 1, h * GDV:(h + 1) * GDV], start=True, stop=True)
            mm.then_inc(N["gla_mm"], 1)
            W(pe, "gla_qe", 1)
            W(pe, "gla_out", 3)
            pe.wait_ge(N["sstate_landed"], 16)
            pe.matmul(ps[:, 4, 0:GH * NB], ones[:, :], gkq[:, :, :].rearrange("p h b -> p (h b)"), start=True, stop=True)
            for b in range(NB):
                for j in range(8):
                    h, e = j // 2, j % 2
                    mm = pe.matmul(ps[:, 5, j * NB + b:j * NB + b + 1], gst[:, b, h, e * P:(e + 1) * P],
                                   gqe[:, h, b:b + 1], start=True, stop=True)
            mm.then_inc(N["gla_smm"], 1)
            for b in range(NB):
                if b >= 3:
                    W(pe, "gla_srow", b - 2)
                bank = (0, 2, 6)[b % 3]
                for m in range(2):
                    mm = pe.matmul(ps[:, bank + m, :], ident[0:NB, b:b + 1].broadcast_to([NB, P]),
                                   gvrow[:, m * 512:(m + 1) * 512], start=True, stop=True)
                mm.then_inc(N["gla_bc"], 1)

            W(pe, "gla_srow", NB)
            for t in range(16):
                W(pe, "gdn_sq", t // 4 + 1)
                if t >= 4:
                    W(pe, "gdn_ln", t - 3)
                pe.matmul(ps[:, t % 4, 0:TT], ones[:, :], sqb[:, t, :], start=True, stop=True).then_inc(N["gdn_sum"], 1)
            W(pe, "gdn_normed", 4)
            for g in range(4):
                if g >= 2:
                    W(pe, "gdn_ktok", g - 1)
                    W(pe, "gdn_vb", g - 1)
                for t in range(2):
                    for n in range(4):
                        h, c = 2 * g + n // 2, n % 2
                        mm = turn(ps[:, 4 * (g % 2) + t, n * P:(n + 1) * P], cv[:, 8 + 8 * t + h, c * P:(c + 1) * P])
                mm.then_inc(N["gdn_turned"], 1)
            for g in range(4):
                if g >= 2:
                    W(pe, "gdn_lt", g - 1)
                else:
                    W(pe, "gdn_ktok", g + 3)
                    W(pe, "gdn_vb", g + 3)
                b0 = 4 * (g % 2)
                for n in range(4):
                    h, c = 2 * g + n // 2, n % 2
                    tok = slice(c * P, (c + 1) * P)
                    at_n = slice(n * P, (n + 1) * P)
                    pe.matmul(ps[:, b0, at_n], sm(G_)[:, h, c:c + 1].broadcast_to([P, P]), tri[:, :], start=True, stop=True)
                    pe.matmul(ps[:, b0 + 1, at_n], sm(BETA)[:, h, c:c + 1].broadcast_to([P, P]), ident[:, :],
                              start=True, stop=True)
                    pe.matmul(ps[:, b0 + 2, at_n], cv[:, 8 + h, tok], cv[:, 8 + h, tok], start=True, stop=True)
                    mm = pe.matmul(ps[:, b0 + 3, at_n], cv[:, 8 + h, tok], cv[:, h, tok], start=True, stop=True)
                mm.then_inc(N["gdn_pair"], 1)
            for g in range(4):
                W(pe, "gdn_bt", g + 1)
                if g == 0:
                    W(pe, "gdn_lt", 4)
                for n in range(4):
                    mm = turn(ps[:, g, n * P:(n + 1) * P], Bt[:, 4 * g + n, :])
                mm.then_inc(N["gdn_t0"], 1)
            for l in range(2, LEVELS):
                for g in range(4):
                    W(pe, "inv_ready", 4 * (l - 2) + g + 1)
                    W(pe, "gdn_bt", 4 * (l - 1) + g + 1)
                    for n in range(4):
                        mm = pe.matmul(ps[:, g, n * P:(n + 1) * P], Bt[:, 4 * g + n, :], Tm[:, 4 * g + n, :],
                                       start=True, stop=True)
                    mm.then_inc(N["y_done"], 1)
                for g in range(4):
                    W(pe, "y_copied", 4 * (l - 2) + g + 1)
                    if g >= 2:
                        W(pe, "inv_ready", 4 * (l - 1) + g - 1)
                    b0 = 4 + 2 * (g % 2)
                    for n in range(4):
                        v = 4 * g + n
                        if l < LEVELS - 1:
                            pe.matmul(ps[:, b0, n * P:(n + 1) * P], U[:, v, :], Y[:, v, :], start=True, stop=True)
                        mm = pe.matmul(ps[:, b0 + 1, n * P:(n + 1) * P], Y[:, v, :], U[:, v, :], start=True, stop=True)
                    mm.then_inc(N["tyuy_done"], 1)
            W(pe, "inv_ready", 4 * (LEVELS - 1))
            W(pe, "gdn_kbg", 1)
            W(pe, "gdn_qkm", 4)
            for g in range(2):
                for n in range(4):
                    h = 4 * g + n
                    pe.matmul(unit_ps(g, n), kbg[:, h, :], U[:, 2 * h + 1, :], start=True, stop=True)
                    mm = pe.matmul(unit_ps(2 + g, n), U[:, 2 * h, :], vb[:, 2 * h, :], start=True, stop=True)
                mm.then_inc(N["gdn_f1"], 1)
            for g in range(2):
                W(pe, "gdn_e1", g + 1)
                for n in range(4):
                    h = 4 * g + n
                    pe.matmul(unit_ps(4 + g, n), ktok[:, 2 * h, :], uu[:, 2 * h, :], start=True, stop=True)
                    mm = pe.matmul(unit_ps(6 + g, n), uu[:, 2 * h, :], QK[:, 2 * h, :], start=True, stop=True)
                mm.then_inc(N["gdn_f2"], 1)
            for g in range(2):
                W(pe, "gdn_e2", g + 1)
                for n in range(4):
                    h = 4 * g + n
                    pe.matmul(unit_ps(g, n), U[:, 2 * h + 1, :], vb[:, 2 * h + 1, :], start=True, stop=False)
                    mm = pe.matmul(unit_ps(g, n), nw[:, h, :], bs1[:, h, :], start=False, stop=True)
                mm.then_inc(N["gdn_f3"], 1)
            for g in range(2):
                W(pe, "gdn_e3", g + 1)
                for n in range(4):
                    h = 4 * g + n
                    pe.matmul(unit_ps(4 + g, n), bs1[:, h, :], cv[:, h, P:T], start=True, stop=False)
                    pe.matmul(unit_ps(4 + g, n), uu[:, 2 * h + 1, :], QK[:, 2 * h + 1, :], start=False, stop=True)
                    mm = pe.matmul(unit_ps(6 + g, n), ktok[:, 2 * h + 1, :], uu[:, 2 * h + 1, :], start=True, stop=True)
                mm.then_inc(N["gdn_f4"], 1)
            W(pe, "gdn_sx", 1)
            W(pe, "gdn_e4", 4)
            for m in range(2):
                pe.matmul(ps[:, 0, m * 64:(m + 1) * 64], ones[0:NB, :],
                          sdiag[:, m, :, :].rearrange("p b h -> p (b h)"), start=True, stop=True)
            pe.matmul(ps[:, 0, 2 * 64:3 * 64], ones[:, :], skq[:, :, :].rearrange("p b h -> p (b h)"), start=True, stop=True)
            pe.wait_ge(N["bst_landed"], 16)
            for n in range(NB * HB):
                b, h = n // HB, n % HB
                mm = pe.matmul(ps[:, 1, 2 * n:2 * n + 2], bst[:, b, h, :], cv[:, h:h + 9:8, T + b],
                               start=True, stop=True)
            mm.then_inc(N["gdn_sbc"], 1)
            W(pe, "gdn_sval", 1)
            turn(ps[0:NB * HB, 2, 0:P], su[:, :, :].rearrange("p b h -> p (b h)")).then_inc(N["gdn_u"], 1)
            W(pe, "gdn_ub", 1)
            for g in range(16):
                if g >= 4:
                    W(pe, "gdn_surow", g - 3)
                for n in range(4):
                    mm = pe.matmul(ps[:, 3 + g % 4, n * P:(n + 1) * P],
                                   ident[0:64, 4 * g + n:4 * g + n + 1].broadcast_to([64, P]), urow[:, :],
                                   start=True, stop=True)
                mm.then_inc(N["gdn_uspread"], 1)
            for t in range(12):
                W(pe, "norm_sq", 1 if t < 4 else 2)
                if t >= 4:
                    W(pe, "norm_rb", t - 3)
                if t == 0:
                    W(pe, "gdn_surow", 16)
                if t < 4:
                    pe.matmul(ps[:, t % 4, 0:TT], ones[:, :], nsq[:, 2 * t, :], start=True, stop=False)
                    mm = pe.matmul(ps[:, t % 4, 0:TT], ones[:, :], nsq[:, 2 * t + 1, :], start=False, stop=True)
                else:
                    mm = pe.matmul(ps[:, t % 4, 0:TT], ones[:, :], nsq[:, t - 4 + 8, :], start=True, stop=True)
                mm.then_inc(N["norm_sum"], 1)

            W(pe, "o_ready", 16)
            phase_pe(pe, PH["w_out"], ow_hi, ow_lo)
            sum_squares(2, TT)
            pe.wait_ge(acc_free, PH["x_q"].t0 + ACC_CREDIT)
            phase_pe(pe, PH["x_q"], act_hi, act_lo)

            pe.wait_ge(mrows_landed, 16)
            for k in range(KT):
                if k >= 4:
                    pe.wait_ge(m_taken, k - 3)
                for c in range(2):
                    mm = turn(ps[:, W4 + k % 4, c * P:(c + 1) * P], mrows[:, c, k * P:(k + 1) * P])
                mm.then_inc(N["m_turned"], 1)
            pe.wait_ge(m_taken, KT)
            sum_squares(3, NM)
            phase_pe(pe, PH["mem_k"], ow_hi, ow_lo)
            phase_pe(pe, PH["mem_v"], ow_hi, ow_lo)
            pe.wait_ge(acc_free, PH["x_o"].t0 + ACC_CREDIT)

            for h in range(XH):
                for c in range(NC):
                    for d in range(4):
                        mm = pe.matmul(ps[:, h, c * NM:(c + 1) * NM], q[:, 4 * h + d, c * P:(c + 1) * P],
                                       kT[:, 4 * h + d, :], start=d == 0, stop=d == 3)
                mm.then_inc(N["att_qk"], 1)
            for w in range(2):
                for c in range(2):
                    for g in range(4):
                        n = (w * 2 + c) * 4 + g
                        if n >= 4:
                            W(pe, "kv_copied", n - 3)
                        for t in range(4):
                            mm = turn(ps[:, 4 + n % 4, t * P:(t + 1) * P],
                                      (kT, vT)[w][:, 4 * g + t, c * P:(c + 1) * P])
                        mm.then_inc(N["kv_turned"], 1)
            for h in range(XH):
                W(pe, "att_norm", h + 1)
                for m in range(2):
                    for c in range(NC):
                        mm = turn(ps[:, h, m * T + c * P:m * T + (c + 1) * P], pr[:, 2 * h + c, m * P:(m + 1) * P])
                mm.then_inc(N["att_pturned"], 1)
            W(pe, "kv_copied", 16)
            for j in range(KT):
                W(pe, "att_pT", j // 4 + 1)
                if j >= 4:
                    W(pe, "att_oe", j - 3)
                for m in range(2):
                    mm = pe.matmul(ps[:, 4 + j % 4, 0:T], vm[:, m, j * P:(j + 1) * P], prT[:, j // 4, m, :],
                                   start=m == 0, stop=m == 1)
                mm.then_inc(N["att_o"], 1)
            W(pe, "att_pT", XH)
            for t in range(KT):
                mm = turn(ps[0:NB, t // 4, (t % 4) * P:(t % 4 + 1) * P], q[:, t, T:TT])
            mm.then_inc(N["s_smq"], 1)
            W(pe, "s_qrow", 1)
            W(pe, "att_oe", KT)
            for b in range(NB):
                if b >= 2:
                    W(pe, "s_dot", b - 1)
                for h in range(XH):
                    mm = pe.matmul(ps[:, 4 * (b % 2) + h, :], ident[0:NB, b:b + 1].broadcast_to([NB, P]),
                                   qrow[:, h * 512:(h + 1) * 512], start=True, stop=True)
                mm.then_inc(N["s_qb"], 1)
            W(pe, "s_dot", NB)
            for m in range(2):
                mm = turn(ps[0:32, 0, m * P:(m + 1) * P], sc_s[:, m, :])
            mm.then_inc(N["s_st"], 1)
            W(pe, "s_pn", 1)
            for m in range(2):
                mm = turn(ps[:, 1, m * 32:(m + 1) * 32], p_s[:, m * P:(m + 1) * P])
            mm.then_inc(N["s_ptt"], 1)
            W(pe, "s_pT", 1)
            for b in range(NB):
                pe.wait_ge(N["cache_landed"] if b % 2 == 0 else cache_landed1, 32 * (NB // 2 + b // 2 + 1))
                for j in range(KT):
                    for m in range(2):
                        mm = pe.matmul(ps[:, 2, j * NB + b:j * NB + b + 1], cache[b % 2][:, m, j * P:(j + 1) * P],
                                       pT_s[:, m, b * XH + j // 4:b * XH + j // 4 + 1], start=m == 0, stop=m == 1)
                mm.then_inc(N["s_o"], 1)

            W(pe, "s_oe", 1)
            phase_pe(pe, PH["x_o"], ow_hi, ow_lo)
            sum_squares(4, TT)
            for half in range(2):
                pe.wait_ge(acc_free, PH[f"gu{half}"].t0 + ACC_CREDIT)
                phase_pe(pe, PH[f"gu{half}"], act_hi, act_lo)
                pe.wait_ge(ff_split, HALF_K * (half + 1))
                phase_pe(pe, PH[f"dn{half}"], ff_hi, ff_lo)
            sum_squares(5, TT)
            for g in range(4):
                W(pe, "y_norm", g + 1)
                if g >= 2:
                    W(pe, "y_copied_act", g - 1)
                    W(pe, "y_copied_dve", g - 1)
                for c in range(NC):
                    for t in range(4):
                        turn(ps[:, 3 * (g % 2) + c, t * P:(t + 1) * P], yT[:, 4 * g + t, c * P:(c + 1) * P])
                for t in range(4):
                    mm = turn(ps[0:NB, 3 * (g % 2) + 2, t * P:(t + 1) * P], yT[:, 4 * g + t, T:TT])
                mm.then_inc(N["y_turned"], 1)

        MX, SUM, REC = 0, 1, 2
        SCALE = XD ** -0.5

        @block.scalar
        def _(act):
            def split(ph, i, u):
                split_hi(act, ph, i, u)

            def rms(k, width, n):
                act.wait_ge(sum_ready, k)
                act_link(act, act.activation(rstd[:, 0:width], ps[:, 7, 0:width], ACT.Ln, scale=1.0 / n,
                                             bias=consts[:, 0:1]))
                act.activation(rstd[:, 0:width], rstd[:, 0:width], ACT.Exp, scale=-0.5).then_inc(rstd_ready, 1)

            def none(ph, i, u):
                pass

            def gdn_take(ph, i, u):
                n = i * 4 + u
                act.wait_ge(conv_ready, 4 * n + 4)
                act.activation(tail[:, :, ds(n, 1)], pre[:, u % 2, T:T + 11].unsqueeze(2), ACT.Copy)
                act.activation(cv[:, ds(n, 1), :], cacc[:, u % 2, :], ACT.Silu).then_inc(conv_done, 1)

            def gate_take(ph, i, u):
                if u % 2 == 0:
                    act.wait_ge(acc_free, ph.t0 + 4 * i + u + 1 + ACC_CREDIT)
                    act.activation(g_s[:, u // 2, :], g_s[:, u // 2, :], ACT.Silu).then_inc(gate_act, 1)

            def run(name, take, nxt):
                ph = PH[name]
                with act.Fori(0, ph.loops - 1) as i:
                    for u in range(4):
                        split(ph, i, u + 2) if u < 2 else split(ph, i + 1, u - 2)
                        take(ph, i, u)
                i = ph.loops - 1
                for u in range(4):
                    if u < 2:
                        split(ph, i, u + 2)
                    elif nxt is not None:
                        split(PH[nxt], 0, u - 2)
                    take(ph, i, u)

            act.wait_ge(dve_credit, 1)
            act.wait_ge(cols_turned, 1)
            split(PH["strip"], 0, 0)
            split(PH["gdn"], 0, 0)
            act.wait_ge(consts_ready, 1)
            rms(1, TT, D)
            split(PH["gdn"], 0, 1)
            run("gdn", gdn_take, "gla")
            run("gla", none, "z")
            run("z", none, None)

            c1 = consts[:, 1:2]
            act.wait_ge(scalars_landed, 16 * 3)
            W(act, "scalars", 1)
            act_link(act, act.activation(sm(SP_), sm(TMP), ACT.Exp, scale=-1.0))
            act_link(act, act.activation(sm(SP_), sm(SP_), ACT.Ln, bias=c1))
            act.activation(sm(EB), sm(DB), ACT.Exp, scale=-1.0)
            act.activation(sm(EAL)[:, :, 0], alog[:, :], ACT.Exp).then_inc(N["scalars"], 1)
            act.wait_ge(N["turned"], 1)
            for g, rows in enumerate((3 * CT, 4 * CT, 4 * CT)):
                act.activation(tails[0:rows, g, :], ps[0:rows, 1, g * P:(g + 1) * P], ACT.Copy).then_inc(N["tails_copied"], 1)
            W(act, "gla_dec", 1)
            act_link(act, act.activation(gaz[:, :, :], gaz[:, :, :], ACT.Exp, scale=-1.0))
            act.activation(gaz[:, :, :], gaz[:, :, :], ACT.Ln, bias=c1).then_inc(N["gla_exp"], 1)
            W(act, "gdn_scal", 1)
            act.activation(sm(EG1), sm(GC), ACT.Exp)
            act.activation(sm(KD), sm(GD), ACT.Exp)
            act.activation(sm(EGL), sm(GL), ACT.Exp).then_inc(N["gdn_scal"], 1)
            W(act, "gla_la", 1)
            act.activation(ges[:, :, :], gz[:, :, T:TT], ACT.Exp).then_inc(N["gla_bgate"], 1)
            for l in range(1, LEVELS):
                W(act, "gla_dec", l + 1)
                act.activation(gE[l % 2][:, :, :], gE[l % 2][:, :, :], ACT.Exp).then_inc(N["gla_exp"], 1)
                if l == 2:
                    W(act, "gla_turned", 1)
                    W(act, "gla_bgate", 1)
                    for c in range(NC):
                        for m in range(2):
                            act.activation(gvt[:, c, m * 512:(m + 1) * 512], ps[:, 4 + 2 * c + m, :], ACT.Copy)\
                               .then_inc(N["gla_tok"], 1)
            W(act, "gla_eexp", 1)
            act.activation(gE[0][:, :, :], gE[0][:, :, :], ACT.Exp)
            act.activation(gE[1][:, :, 0:P], gb[:, :, P:T], ACT.Exp)
            act.activation(gel[:, :, :], gb[:, :, T - 1:T], ACT.Exp).then_inc(N["gla_exp"], 1)
            W(act, "gla_turned", 2)
            for m in range(2):
                act.activation(gkdt[:, 4 * m:4 * m + 4, :], heads_of(m), ACT.Copy).then_inc(N["gla_tok"], 1)
            for m in range(2):
                act.activation(gvrow[:, m * 512:(m + 1) * 512], ps[0:NB, 2 + m, :], ACT.Copy).then_inc(N["gla_tok"], 1)
            W(act, "gla_mm", 1)
            act.wait_ge(tails_out, 16 * (1 + NB))
            for m in range(2):
                ins = act.activation(gs1[:, 2 * m:2 * m + 2, :], ps[:, m, :].rearrange("p (h v) -> p h v", h=2), ACT.Copy)
            ins.then_inc(N["gla_s"], 1)
            W(act, "gla_smm", 1)
            for b in range(NB):
                for h in range(GH):
                    ins = act.activation(gst[:, b, h, :], gst[:, b, h, :], ACT.Copy, scale=ges[:, h, b:b + 1])
                ins.then_inc(N["gla_sc"], 1)
            W(act, "gla_bc", NB)
            for t in range(4):
                act.activation(sqb[:, 4 * t:4 * t + 4, :], cv[:, 4 * t:4 * t + 4, :], ACT.Square).then_inc(N["gdn_sq"], 1)
            for t in range(16):
                W(act, "gdn_sum", t + 1)
                act.activation(sqb[:, t, :], ps[:, t % 4, 0:TT], ACT.Ln, bias=consts[:, 0:1]).then_inc(N["gdn_ln"], 1)
            for t in range(4):
                W(act, "gdn_ln", 4 * t + 4)
                act.activation(sqb[:, 4 * t:4 * t + 4, :], sqb[:, 4 * t:4 * t + 4, :], ACT.Exp, scale=-0.5)\
                   .then_inc(N["gdn_ln"], 1)
            W(act, "gdn_normed", 4)
            for g in range(4):
                W(act, "gdn_turned", g + 1)
                act.activation(ktok[:, 4 * g:4 * g + 4, :], heads_of(4 * (g % 2)), ACT.Copy).then_inc(N["gdn_ktok"], 1)
            for g in range(4):
                W(act, "gdn_dmin", g + 1)
                W(act, "gdn_pair", g + 1)
                act.activation(EG[:, 2 * g:2 * g + 2, :],
                               ps[:, 4 * (g % 2), :].rearrange("p (h c t) -> p h c t", h=2, c=2)[:, :, 1, :], ACT.Exp)
                act.activation(QK[:, 4 * g:4 * g + 4, :], QK[:, 4 * g:4 * g + 4, :], ACT.Exp).then_inc(N["gdn_dexp"], 1)
            for l in range(2, LEVELS):
                for g in range(4):
                    W(act, "y_done", 4 * (l - 2) + g + 1)
                    if l == 2:
                        act.wait_ge(N["state_out"], 32)
                    act.activation(Y[:, 4 * g:4 * g + 4, :], heads_of(g), ACT.Copy).then_inc(N["y_copied"], 1)
            act.wait_ge(N["state_out"], 32)
            for g in range(2):
                W(act, "gdn_f1", g + 1)
                act.activation(nw[:, 4 * g:4 * g + 4, :], heads_of(g), ACT.Copy, scale=-1.0)
                act.activation(uu[:, 8 * g:8 * g + 8:2, :], heads_of(2 + g), ACT.Copy).then_inc(N["gdn_e1"], 1)
            for g in range(2):
                W(act, "gdn_f2", g + 1)
                act.activation(bs1[:, 4 * g:4 * g + 4, :], heads_of(4 + g), ACT.Copy)
                act.activation(cv[:, 4 * g:4 * g + 4, 0:P], heads_of(6 + g), ACT.Copy).then_inc(N["gdn_e2"], 1)
            for g in range(2):
                W(act, "gdn_f3", g + 1)
                act.activation(uu[:, 8 * g + 1:8 * g + 8:2, :], heads_of(g), ACT.Copy).then_inc(N["gdn_e3"], 1)
            W(act, "gdn_u", 1)
            act.activation(urow[:, :], ps[0:NB * HB, 2, 0:P], ACT.Copy).then_inc(N["gdn_ub"], 1)
            W(act, "gdn_f4", 2)
            act.activation(nsq[:, 0:8, :], gla[:, 0:8, :], ACT.Square).then_inc(N["norm_sq"], 1)
            W(act, "gdn_sval", 1)
            act.activation(nsq[:, 8:16, :], cv[:, 0:8, :], ACT.Square).then_inc(N["norm_sq"], 1)
            for t in range(12):
                W(act, "norm_sum", t + 1)
                act.activation(nsq[:, t, :], ps[:, t % 4, 0:TT], ACT.Ln, bias=consts[:, 0:1],
                               scale=1.0 / (GDV if t < 4 else P)).then_inc(N["norm_rb"], 1)
            W(act, "norm_rb", 12)
            act.activation(nsq[:, 0:12, :], nsq[:, 0:12, :], ACT.Exp, scale=-0.5).then_inc(N["norm_rb"], 1)
            act.activation(gla[:, 16:32, :], gla[:, 16:32, :], ACT.Silu).then_inc(N["silu_g"], 1)

            W(act, "o_ready", 16)
            act.wait_ge(N["state_out"], 64)
            split(PH["w_out"], 0, 0)
            split(PH["w_out"], 0, 1)
            run("w_out", none, "x_q")
            rms(2, TT, D)
            run("x_q", none, "mem_k")
            rms(3, NM, D)
            run("mem_k", none, "mem_v")
            run("mem_v", none, None)

            for n in range(16):
                W(act, "kv_turned", n + 1)
                w, c, g = n // 8, (n // 4) % 2, n % 4
                act.activation((km, vm)[w][:, c, g * 512:(g + 1) * 512], ps[:, 4 + n % 4, :], ACT.Copy)\
                   .then_inc(N["kv_copied"], 1)
            for h in range(XH):
                W(act, "att_max", h + 1)
                for c in range(NC):
                    ins = act.activation(pr[:, 2 * h + c, :], ps[:, h, c * NM:(c + 1) * NM], ACT.Exp, scale=SCALE,
                                         bias=small[:, MX, 2 * h + c:2 * h + c + 1],
                                         accum_out=small[:, SUM, 2 * h + c:2 * h + c + 1])
                ins.then_inc(N["att_exp"], 1)
            for h in range(XH):
                W(act, "att_pturned", h + 1)
                act.activation(prT[:, h, :, :], ps[:, h, :].rearrange("p (m t) -> p m t", m=2), ACT.Copy)\
                   .then_inc(N["att_pT"], 1)
            W(act, "s_smq", 1)
            act.wait_ge(kv_out, 32)
            act.activation(qrow[:, :], ps[0:NB, 0:4, :].rearrange("p b n -> p (b n)"), ACT.Copy).then_inc(N["s_qrow"], 1)
            W(act, "s_sm", 1)
            act.activation(p_s[:, :], ps[0:32, 0, 0:NM], ACT.Exp, scale=SCALE, bias=small[0:32, MX, 0:1],
                           accum_out=small[0:32, SUM, 0:1]).then_inc(N["s_exp"], 1)

            W(act, "s_o", NB)
            split(PH["x_o"], 0, 0)
            split(PH["x_o"], 0, 1)
            run("x_o", none, "gu0")
            rms(4, TT, D)
            run("gu0", gate_take, "dn0")
            run("dn0", none, "gu1")
            run("gu1", gate_take, "dn1")
            run("dn1", none, None)
            rms(5, TT, D)
            for g in range(4):
                W(act, "y_turned", g + 1)
                act.activation(ysrow[:, g * 512:(g + 1) * 512], ps[0:NB, 3 * (g % 2) + 2, :], ACT.Copy)
                act.activation(yrows[:, 1, g * 512:(g + 1) * 512], ps[:, 3 * (g % 2) + 1, :], ACT.Copy)\
                   .then_inc(N["y_copied_act"], 1)

        @block.vector
        def _(dve):
            scaled, gdn, residual, gate_up, down = dve_take(dve)

            def link(ins):
                dve_link(dve, ins)

            def split(ph, i, u):
                split_lo(dve, ph, i, u)

            def run(name, take, nxt):
                ph = PH[name]
                with dve.Fori(0, ph.loops - 1) as i:
                    for u in range(4):
                        take(ph, i, u)
                        split(ph, i, u + 2) if u < 2 else split(ph, i + 1, u - 2)
                i = ph.loops - 1
                for u in range(4):
                    take(ph, i, u)
                    if u < 2:
                        split(ph, i, u + 2)
                    elif nxt is not None:
                        split(PH[nxt], 0, u - 2)

            def halves_of(k, src, gain, hi, lo, done):
                w = src.shape[-1]
                g = cols[:, gain + k:gain + k + 1]
                link(dve.tensor_scalar(hi[:, k, 0:w], src, g, None, ALU.mult))
                dve.scalar_tensor_tensor(out=lo[:, k, 0:w], in0=src, scalar=g, in1=hi[:, k, 0:w], op0=ALU.mult,
                                         op1=ALU.subtract).then_inc(done, 1)

            dve.memset(strip[:, 0:1], 0.0).then_inc(units_done, UNIT_CREDIT)
            dve.memset(strip[:, 1:2], 0.0).then_inc(lo_split, LO_CREDIT)
            dve.memset(strip[:, 2:3], 0.0).then_inc(acc_free, ACC_CREDIT)
            dve.memset(strip[:, 3:4], 0.0).then_inc(conv_done, 2)
            dve.memset(small[:, :, :], 0.0).then_inc(dve_credit, 1)
            dve.wait_ge(cols_turned, 1)
            dve.tensor_copy(cols[:, :], ps[:, 4, 0:87]).then_inc(cols_ready, 1)
            dve.tensor_copy(convw[:, :], ps[:, 4, P:P + CW * CT]).then_inc(cols_ready, 1)
            for m in range(2):
                ins = dve.tensor_copy(cst[:, 12 * m:12 * m + 12, :].rearrange("p t (j b) -> p t b j", j=3),
                                      ps[:, 5 + m, 0:288].rearrange("p (t b j) -> p t b j", t=12, j=3))
            ins.then_inc(cols_ready, 1)
            dve.wait_ge(cols_ready, 3)
            for k in range(KT):
                dve.wait_ge(x_turned, k + 1)
                src = ps[:, W4 + k % 4, 0:TT]
                dve.tensor_copy(x[:, k, :], src).then_inc(x_ready, 1)
                halves_of(k, src, GAIN_MIX, act_hi, act_lo, x_taken)
            split(PH["strip"], 0, 0)
            split(PH["gdn"], 0, 0)
            dve.wait_ge(rstd_ready, 1)
            dve.wait_ge(consts_ready, 1)
            tile_wait(dve, PH["strip"], 0, 0)
            dve.tensor_tensor(strip[:, :], ps[:, 0, 0:TT], rstd[:, :], ALU.mult).then_inc(acc_free, 1)
            split(PH["gdn"], 0, 1)
            run("gdn", gdn, "gla")
            run("gla", scaled(gla, rstd[:, :]), "z")
            run("z", scaled(gla[:, 24:32, :], rstd[:, :]), None)

            def b3(v, n):
                return v.unsqueeze(1).broadcast_to([P, n, P])

            W(dve, "turned", 1)
            for dst, c0 in ((DA, 112), (DB, 120)):
                dve.tensor_copy(sm(dst)[:, :, 0:2], ps[:, 0, 0:256].rearrange("p (c h) -> p h c", h=P)[:, c0:c0 + HB, :])
                ins = dve.tensor_copy(sm(dst)[0:NB, :, 2], ps[0:NB, 0, 2 * P + c0:2 * P + c0 + HB])
            link(ins)
            dve.wait_ge(scalars_landed, 16 * 3)
            link(dve.tensor_tensor(sm(DA), sm(DA), dtb[:, :].unsqueeze(2).broadcast_to([P, HB, 3]), ALU.add))
            dve.scalar_tensor_tensor(out=sm(TMP), in0=sm(DA), scalar=-1.0, in1=sm(DA), op0=ALU.mult, op1=ALU.max)\
               .then_inc(N["scalars"], 1)
            W(dve, "gla_pre", 1)
            for h in range(GH):
                ins = dve.tensor_scalar(gz[:, h, :], ps[:, 4 + h, 0:TT], cols[:, GAIN_GATE_B + h:GAIN_GATE_B + h + 1], None,
                                        ALU.add)
            link(ins)
            dve.scalar_tensor_tensor(out=gaz[:, :, :], in0=gz[:, :, :], scalar=-1.0, in1=gz[:, :, :], op0=ALU.mult,
                                     op1=ALU.max).then_inc(N["gla_dec"], 1)
            W(dve, "scalars", 2)
            link(dve.scalar_tensor_tensor(out=sm(TMP), in0=sm(DA), scalar=0.0, in1=sm(SP_), op0=ALU.max, op1=ALU.add))
            link(dve.scalar_tensor_tensor(out=sm(G_), in0=sm(TMP), scalar=-1.0,
                                          in1=sm(EAL)[:, :, 0:1].broadcast_to([P, HB, 3]), op0=ALU.mult, op1=ALU.mult))
            link(dve.tensor_scalar(sm(EB), sm(EB), 1.0, None, ALU.add))
            dve.reciprocal(sm(BETA), sm(EB)).then_inc(N["gdn_g"], 1)
            W(dve, "gdn_gcol", 1)
            dve.tensor_copy(sm(GC)[:, :, 2], sm(G_)[:, :, 2])
            dve.tensor_copy(sm(GL)[:, :, 2], sm(G_)[:, :, 2])
            dve.tensor_copy(sm(GC)[:, :, 0:2], ps[:, 2, 0:16].rearrange("p (c h) -> p h c", c=2))
            link(dve.tensor_copy(sm(GL)[:, :, 0:2], ps[:, 2, 16:32].rearrange("p (c h) -> p h c", c=2)))
            dve.tensor_tensor(sm(GD), sm(GL), sm(GC), ALU.subtract).then_inc(N["gdn_scal"], 1)
            W(dve, "gla_exp", 1)
            link(dve.scalar_tensor_tensor(out=gz[:, :, :], in0=gz[:, :, :], scalar=0.0, in1=gaz[:, :, :], op0=ALU.min,
                                          op1=ALU.subtract))
            link(dve.tensor_scalar(gz[:, :, :], gz[:, :, :], 1.0 / 16.0, None, ALU.mult))
            link(dve.tensor_scalar(gla[:, 0:GH, :], gla[:, 0:GH, :], GDK ** -0.5, None, ALU.mult))
            for h in range(GH):
                for c in range(NC):
                    tok = slice(c * P, (c + 1) * P)
                    ins = dve.tensor_tensor_scan(gb[:, h, tok], ones[:, :], gz[:, h, tok], 0.0, ALU.mult, ALU.add)
            ins.then_inc(N["gla_la"], 1)
            W(dve, "gla_la", 1)
            W(dve, "prep", 1)
            W(dve, "gdn_scal", 2)
            dve.tensor_tensor(sm(BG), sm(EG1), sm(BETA), ALU.mult)

            def differences(l):
                m = 1 << (l - 1)
                nb = T // (2 * m)
                v = gb[:, :, :].rearrange("p h (n s m) -> p (h n) s m", s=2, m=m)
                e = gE[l % 2][:, :, :].rearrange("p h (n s m) -> p (h n) s m", s=2, m=m)
                if l >= 3:
                    W(dve, "gla_lvl", l - 2)
                mid = v[:, :, 0, m - 1:m].broadcast_to([P, GH * nb, m])
                dve.tensor_tensor(e[:, :, 1, :], v[:, :, 1, :], mid, ALU.subtract)
                dve.tensor_tensor(e[:, :, 0, :], mid, v[:, :, 0, :], ALU.subtract).then_inc(N["gla_dec"], 1)

            def pick(l):
                W(dve, "gla_scored", l + 1)
                if l:
                    W(dve, "gla_picked", l)
                for m in range(2):
                    v = gsc[:, 4 * m:4 * m + 4, :]
                    mask = b3(levels[:, l, :], 4)
                    if l == 0:
                        ins = dve.tensor_tensor(v, heads_of(m), mask, ALU.mult)
                    else:
                        ins = dve.copy_predicated(v, mask.bitcast(U32), heads_of(2 * (l % 2) + m))
                ins.then_inc(N["gla_picked"], 1)

            differences(1)
            for l in range(1, LEVELS):
                if l + 1 < LEVELS:
                    differences(l + 1)
                m = 1 << (l - 1)
                W(dve, "gla_exp", l + 1)
                if l >= 3:
                    W(dve, "gla_scored", l - 1)
                e = halves(gE[l % 2][:, :, :], m)
                dve.tensor_tensor(halves(gq[l % 2][:, :, :], m)[:, :, :, 1, :], halves(gla[:, 0:GH, 0:T], m)[:, :, :, 1, :],
                                  e[:, :, :, 1, :], ALU.mult)
                dve.tensor_tensor(halves(gk[l % 2][:, :, :], m)[:, :, :, 0, :],
                                  halves(gla[:, GH:2 * GH, 0:T], m)[:, :, :, 0, :],
                                  e[:, :, :, 0, :], ALU.mult).then_inc(N["gla_lvl"], 1)
                pick(l - 1)
            W(dve, "gla_lvl", LEVELS - 2)
            gv = gb[:, :, :].rearrange("p h (c s) -> p (h c) s", s=P)
            dve.tensor_tensor(gE[0][:, :, :].rearrange("p h (c s) -> p (h c) s", s=P),
                              gv[:, :, P - 1:P].broadcast_to([P, GH * NC, P]), gv, ALU.subtract).then_inc(N["gla_eexp"], 1)
            pick(LEVELS - 1)
            W(dve, "gla_exp", LEVELS + 1)
            dve.tensor_tensor(gkd[:, :, :], gla[:, GH:2 * GH, 0:T], gE[0][:, :, :], ALU.mult)
            dve.tensor_tensor(gqd[:, :, :], gla[:, 0:GH, P:T], gE[1][:, :, 0:P], ALU.mult).then_inc(N["gla_dec"], 1)
            W(dve, "gla_bgate", 1)
            dve.tensor_tensor(gqe[:, :, :], gla[:, 0:GH, T:TT], ges[:, :, :], ALU.mult)
            dve.tensor_tensor(gkq[:, :, :], gla[:, 0:GH, T:TT], gla[:, GH:2 * GH, T:TT], ALU.mult)
            dve.tensor_copy(gks[:, :, :], gla[:, GH:2 * GH, T:TT]).then_inc(N["gla_qe"], 1)
            W(dve, "gla_mm", 1)
            for m in range(2):
                ins = dve.tensor_copy(gla[:, 4 * m:4 * m + 4, 0:P], heads_of(4 + m))
            ins.then_inc(N["gla_out"], 1)
            W(dve, "gla_mm", 2)
            for m in range(2):
                ins = dve.tensor_copy(gla[:, 4 * m:4 * m + 4, P:T], heads_of(6 + m))
            ins.then_inc(N["gla_out"], 1)
            W(dve, "gla_s", 1)
            for h in range(GH):
                ins = dve.scalar_tensor_tensor(out=gsf[:, h, :], in0=gs1[:, h, :], scalar=gel[:, h, :],
                                               in1=ps[:, h // 2, (h % 2) * GDV:(h % 2 + 1) * GDV], op0=ALU.mult, op1=ALU.add)
            ins.then_inc(N["gla_out"], 1)
            W(dve, "gla_smm", 1)
            W(dve, "gla_qe", 1)
            link(dve.tensor_tensor(got[:, :, :].rearrange("p (h e) b -> p h e b", e=2),
                                   gla[:, 8:16, T:TT].rearrange("p (h e) b -> p h e b", e=2),
                                   ps[:, 4, 0:32].rearrange("p (h b) -> p h b", h=GH).unsqueeze(2).broadcast_to([P, GH, 2, NB]),
                                   ALU.mult))
            dve.tensor_tensor(gla[:, 0:8, T:TT], got[:, :, :], ps[:, 5, 0:64].rearrange("p (j b) -> p j b", b=NB), ALU.add)
            for b in range(NB):
                W(dve, "gla_bc", b + 1)
                W(dve, "gla_sc", b + 1)
                bank = (0, 2, 6)[b % 3]
                for h in range(GH):
                    ins = dve.scalar_tensor_tensor(out=gst[:, b, h, :],
                                                   in0=ps[:, bank + h // 2, (h % 2) * GDV:(h % 2 + 1) * GDV],
                                                   scalar=gks[:, h, b:b + 1], in1=gst[:, b, h, :], op0=ALU.mult, op1=ALU.add)
                ins.then_inc(N["gla_srow"], 1)

            for t in range(4):
                W(dve, "gdn_ln", 16 + t + 1)
                v = cv[:, 4 * t:4 * t + 4, :]
                dve.scalar_tensor_tensor(out=v, in0=v, scalar=P ** -0.5 if t < 2 else 1.0, in1=sqb[:, 4 * t:4 * t + 4, :],
                                         op0=ALU.mult, op1=ALU.mult).then_inc(N["gdn_normed"], 1)
            def of_units(k, g):
                return sm(k)[:, 2 * g:2 * g + 2, 0:2].unsqueeze(3).broadcast_to([P, 2, 2, P])

            def four(v):
                return v.rearrange("p (h c) d -> p h c d", c=2)

            for g in range(4):
                W(dve, "gdn_turned", g + 1)
                dve.tensor_tensor(four(vb[:, 4 * g:4 * g + 4, :]), four(heads_of(4 * (g % 2) + 1)), of_units(BETA, g), ALU.mult)\
                   .then_inc(N["gdn_vb"], 1)

            def decays(g):
                W(dve, "gdn_pair", g + 1)
                for n in range(4):
                    ins = dve.tensor_scalar(QK[:, 4 * g + n, :], ps[:, 4 * (g % 2), n * P:(n + 1) * P],
                                            sm(GC)[:, 2 * g + n // 2, n % 2:n % 2 + 1], 0.0, ALU.subtract, ALU.min)
                ins.then_inc(N["gdn_dmin"], 1)

            for g in range(4):
                decays(g)
                W(dve, "gdn_dexp", g + 1)
                b0 = 4 * (g % 2)
                lt, qk = Lt[:, 4 * g:4 * g + 4, :], QK[:, 4 * g:4 * g + 4, :]
                if g == 0:
                    dve.wait_ge(N["state_out"], 32)
                link(dve.tensor_tensor(lt, qk, heads_of(b0 + 1), ALU.mult))
                dve.tensor_tensor(lt, lt, heads_of(b0 + 2), ALU.mult)
                dve.tensor_tensor(qk, qk, heads_of(b0 + 3), ALU.mult).then_inc(N["gdn_lt"], 1)
            dve.tensor_tensor(cv[:, 0:HB, P:T], cv[:, 0:HB, P:T], EG[:, :, :], ALU.mult)
            W(dve, "gdn_ktok", 4)
            kt4 = four(ktok[:, :, :])
            link(dve.tensor_tensor(kbg[:, :, :], kt4[:, :, 1, :], sm(BG)[:, :, 1:2].broadcast_to([P, HB, P]), ALU.mult))
            dve.tensor_tensor(kt4, kt4, sm(KD)[:, :, 0:2].unsqueeze(3).broadcast_to([P, HB, 2, P]), ALU.mult)\
               .then_inc(N["gdn_kbg"], 1)
            for g in range(4):
                W(dve, "gdn_bt", g + 1)
                W(dve, "gdn_t0", g + 1)
                dve.tensor_tensor(U[:, 4 * g:4 * g + 4, :], b3(ident[:, :], 4), Bt[:, 4 * g:4 * g + 4, :], ALU.subtract)
                dve.tensor_tensor(Tm[:, 4 * g:4 * g + 4, :], b3(ident[:, :], 4), heads_of(g), ALU.subtract)\
                   .then_inc(N["inv_ready"], 1)
            for l in range(2, LEVELS):
                for g in range(4):
                    W(dve, "tyuy_done", 4 * (l - 2) + g + 1)
                    W(dve, "inv_ready", 4 * (l - 2) + g + 1)
                    b0 = 4 + 2 * (g % 2)
                    if l < LEVELS - 1:
                        tm = Tm[:, 4 * g:4 * g + 4, :]
                        dve.tensor_tensor(tm, tm, heads_of(b0), ALU.subtract)
                    um = U[:, 4 * g:4 * g + 4, :]
                    dve.tensor_tensor(um, um, heads_of(b0 + 1), ALU.subtract).then_inc(N["inv_ready"], 1)
            for g in range(2):
                W(dve, "gdn_f4", g + 1)
                dve.tensor_copy(cv[:, 4 * g:4 * g + 4, P:T], heads_of(4 + g)).then_inc(N["gdn_e4"], 1)
                link(dve.tensor_tensor(bsf[:, 4 * g:4 * g + 4, :], bs1[:, 4 * g:4 * g + 4, :],
                                       sm(EGL)[:, 4 * g:4 * g + 4, 1:2].broadcast_to([P, 4, P]), ALU.mult))
                dve.tensor_tensor(bsf[:, 4 * g:4 * g + 4, :], bsf[:, 4 * g:4 * g + 4, :], heads_of(6 + g), ALU.add)\
                   .then_inc(N["gdn_e4"], 1)

            i8 = ident[0:NB, 0:NB].unsqueeze(2).broadcast_to([NB, NB, HB])

            def on_samples(v):
                return v.rearrange("p h b -> p b h")

            for m, k in ((0, EG1), (1, BETA)):
                dve.tensor_tensor(sdiag[:, m, :, :], i8, sm(k)[0:NB, :, 2].unsqueeze(1).broadcast_to([NB, NB, HB]), ALU.mult)
            dve.tensor_tensor(skq[:, :, :], on_samples(cv[:, 0:8, T:TT]), on_samples(cv[:, 8:16, T:TT]), ALU.mult)\
               .then_inc(N["gdn_sx"], 1)
            W(dve, "gdn_sbc", 1)
            link(dve.tensor_copy(sbc[:, :, :], ps[:, 0, 0:128].rearrange("p (m n) -> p m n", m=2)))
            prod = ps[:, 1, 0:128].rearrange("p (n s) -> p s n", s=2)
            flat = [v[:, :, :].rearrange("p b h -> p (b h)") for v in (su, so, skq2)]
            link(dve.tensor_tensor(flat[0], prod[:, 1, :], sbc[:, 0, :], ALU.mult))
            link(dve.tensor_tensor(su[:, :, :], on_samples(cv[:, 16:24, T:TT]), su[:, :, :], ALU.subtract))
            link(dve.tensor_tensor(flat[0], flat[0], sbc[:, 1, :], ALU.mult))
            link(dve.tensor_tensor(flat[1], prod[:, 0, :], sbc[:, 0, :], ALU.mult))
            link(dve.tensor_tensor(flat[2], flat[0], ps[:, 0, 128:192], ALU.mult))
            dve.tensor_tensor(on_samples(cv[:, 0:8, T:TT]), so[:, :, :], skq2[:, :, :], ALU.add).then_inc(N["gdn_sval"], 1)
            for g in range(16):
                W(dve, "gdn_uspread", g + 1)
                W(dve, "gdn_ubt", g // 2 + 1)
                for n in range(4):
                    b, h = (4 * g + n) // HB, (4 * g + n) % HB
                    ins = dve.scalar_tensor_tensor(out=bst[:, b, h, :], in0=ps[:, 3 + g % 4, n * P:(n + 1) * P],
                                                   scalar=cv[:, 8 + h, T + b:T + b + 1], in1=bst[:, b, h, :],
                                                   op0=ALU.mult, op1=ALU.add)
                ins.then_inc(N["gdn_surow"], 1)
            W(dve, "norm_rb", 13)
            for j in range(KT):
                src, r, g = (gla[:, j, :], j // 2, GAIN_GLA + j % 2) if j < 8 else (cv[:, j - 8, :], j - 4, GAIN_GDN)
                ins = dve.scalar_tensor_tensor(out=src, in0=src, scalar=cols[:, g:g + 1], in1=nsq[:, r, :], op0=ALU.mult,
                                               op1=ALU.mult)
            link(ins)
            W(dve, "silu_g", 1)
            link(dve.tensor_tensor(gla[:, 16:24, :], gla[:, 16:24, :], gla[:, 0:8, :], ALU.mult))
            link(dve.tensor_tensor(gla[:, 24:32, :], gla[:, 24:32, :], cv[:, 0:8, :], ALU.mult))
            for j in range(KT):
                link(dve.tensor_copy(ow_hi[:, j, :], gla[:, 16 + j, :]))
                dve.tensor_tensor(ow_lo[:, j, :], gla[:, 16 + j, :], ow_hi[:, j, :], ALU.subtract).then_inc(N["o_ready"], 1)

            split(PH["w_out"], 0, 0)
            split(PH["w_out"], 0, 1)
            dve.wait_ge(x_ready, KT)
            run("w_out", lambda ph, i, u: residual(ph, i, u, 0, GAIN_X), "x_q")
            dve.wait_ge(rstd_ready, 2)
            run("x_q", scaled(q, rstd[:, :]), "mem_k")
            for k in range(KT):
                W(dve, "m_turned", k + 1)
                src = ps[:, W4 + k % 4, 0:NM]
                dve.tensor_copy(kT[:, k, :], src)
                halves_of(k, src, GAIN_MEM, ow_hi, ow_lo, m_taken)
            dve.wait_ge(rstd_ready, 3)
            run("mem_k", scaled(kT, rstd[:, 0:NM]), "mem_v")
            run("mem_v", scaled(vT, rstd[:, 0:NM]), None)

            for h in range(XH):
                W(dve, "att_qk", h + 1)
                link(dve.tensor_reduce(small[:, MX, 2 * h:2 * h + 2], ps[:, h, :].rearrange("p (c m) -> p c m", c=2), AX_X,
                                       ALU.max))
                dve.tensor_scalar(small[:, MX, 2 * h:2 * h + 2], small[:, MX, 2 * h:2 * h + 2], -SCALE, None, ALU.mult)\
                   .then_inc(N["att_max"], 1)
            for h in range(XH):
                W(dve, "att_exp", h + 1)
                link(dve.reciprocal(small[:, REC, 2 * h:2 * h + 2], small[:, SUM, 2 * h:2 * h + 2]))
                for c in range(NC):
                    v = pr[:, 2 * h + c, :]
                    ins = dve.tensor_scalar(v, v, small[:, REC, 2 * h + c:2 * h + c + 1], None, ALU.mult)
                ins.then_inc(N["att_norm"], 1)
            for j in range(KT):
                W(dve, "att_o", j + 1)
                src = ps[:, 4 + j % 4, 0:T]
                link(dve.tensor_copy(ow_hi[:, j, 0:T], src))
                dve.tensor_tensor(ow_lo[:, j, 0:T], src, ow_hi[:, j, 0:T], ALU.subtract).then_inc(N["att_oe"], 1)
            dve.wait_ge(kv_out, 32)
            for b in range(NB):
                W(dve, "s_qb", b + 1)
                dve.wait_ge(N["cache_landed"] if b % 2 == 0 else cache_landed1, 32 * (b // 2 + 1))
                for m in range(2):
                    for h in range(XH):
                        kk = cache[b % 2][:, m, h * XD:(h + 1) * XD]
                        ins = dve.tensor_tensor_reduce(kk, kk, ps[:, 4 * (b % 2) + h, :], 1.0, 0.0, ALU.mult, ALU.add,
                                                       sc_s[:, m, b * XH + h:b * XH + h + 1])
                ins.then_inc(N["s_dot"], 1)
            W(dve, "s_st", 1)
            link(dve.tensor_reduce(small[0:32, MX, 0:1], ps[0:32, 0, 0:NM], AX_X, ALU.max))
            dve.tensor_scalar(small[0:32, MX, 0:1], small[0:32, MX, 0:1], -SCALE, None, ALU.mult).then_inc(N["s_sm"], 1)
            W(dve, "s_exp", 1)
            link(dve.reciprocal(small[0:32, REC, 0:1], small[0:32, SUM, 0:1]))
            dve.tensor_scalar(p_s[:, :], p_s[:, :], small[0:32, REC, 0:1], None, ALU.mult).then_inc(N["s_pn"], 1)
            W(dve, "s_ptt", 1)
            dve.tensor_copy(pT_s[:, :, :], ps[:, 1, 0:64].rearrange("p (m n) -> p m n", m=2)).then_inc(N["s_pT"], 1)
            W(dve, "s_o", NB)
            src = ps[:, 2, 0:KT * NB].rearrange("p (j b) -> p j b", b=NB)
            link(dve.tensor_copy(ow_hi[:, :, T:TT], src))
            dve.tensor_tensor(ow_lo[:, :, T:TT], src, ow_hi[:, :, T:TT], ALU.subtract).then_inc(N["s_oe"], 1)

            split(PH["x_o"], 0, 0)
            split(PH["x_o"], 0, 1)
            run("x_o", lambda ph, i, u: residual(ph, i, u, KT, GAIN_FFN), "gu0")
            dve.wait_ge(rstd_ready, 4)
            for half in range(2):
                run(f"gu{half}", gate_up(half), f"dn{half}")
                run(f"dn{half}", down(half), "gu1" if half == 0 else None)
            dve.wait_ge(rstd_ready, 5)
            for g in range(4):
                for t in range(4):
                    k = 4 * g + t
                    ins = dve.scalar_tensor_tensor(out=yT[:, k, :], in0=x[:, k, :],
                                                   scalar=cols[:, GAIN_FINAL + k:GAIN_FINAL + k + 1], in1=rstd[:, :],
                                                   op0=ALU.mult, op1=ALU.mult)
                ins.then_inc(N["y_norm"], 1)
            for g in range(4):
                W(dve, "y_turned", g + 1)
                dve.tensor_copy(yrows[:, 0, g * 512:(g + 1) * 512], ps[:, 3 * (g % 2), :]).then_inc(N["y_copied_dve"], 1)


_INS = ["x_prompt", "x_sample", "mem_prompt", "cache_mem_k", "cache_mem_v", "state_gla", "state_gdn", "state_conv",
        "g_mix", "w_in", "gla_w_gate2", "gla_b_gate", "gla_g_out", "gdn_conv_w", "gdn_a_log", "gdn_dt_bias", "gdn_g_out",
        "w_out", "g_xattn", "g_mem", "xa_w_q", "xa_w_k", "xa_w_v", "xa_w_o", "g_ffn", "ffn_w_gate", "ffn_w_up",
        "ffn_w_down", "g_final"]
_OUTS = [("y_p", (1, T, D)), ("y_s", (NB, 1, D)), ("gla_p", (1, 1, GH, GDK, GDV)), ("gdn_p", (1, 1, HB, P, P)),
         ("conv_p", (1, 1, CW - 1, CT * P)), ("mem_k", (1, 1, NM, XH, XD)), ("mem_v", (1, 1, NM, XH, XD)),
         ("gla_s", (1, NB, GH, GDK, GDV)), ("gdn_s", (1, NB, HB, P, P)), ("conv_s", (1, NB, CW - 1, CT * P))]


def kernel(**inputs):
    import numpy as _np
    import concourse.bacc as _bacc
    from concourse import mybir as _mybir
    from concourse.bass_utils import run_bass_kernel_spmd as _run

    nc = _bacc.Bacc("TRN2", target_bir_lowering=False, num_devices=1)
    arrays, ins, outs = {}, {}, {}
    for name in _INS:
        v = _np.ascontiguousarray(inputs[name])
        arrays[f"in_{name}_dram"] = v
        ins[name] = nc.dram_tensor(f"in_{name}_dram", v.shape, _mybir.dt.from_np(v.dtype), kind="ExternalInput").ap()
    for name, shape in _OUTS:
        outs[name] = nc.dram_tensor(f"out_{name}_dram", shape, _mybir.dt.float32, kind="ExternalOutput").ap()
    build(nc, ins, outs)
    r = _run(nc, [arrays], core_ids=[0])
    return tuple(r.results[0][f"out_{name}_dram"] for name, _ in _OUTS)
```

```python
from contextlib import ExitStack

import concourse.bass as bass
from concourse import mybir

F32 = mybir.dt.float32
R32 = mybir.dt.float32r
U32 = mybir.dt.uint32
ACT = mybir.ActivationFunctionType
ALU = mybir.AluOpType
AX_X = mybir.AxisListType.X
ds = bass.ds

P = 128
D = 2048
KT = D // P
T = 256
NB = 8
TT = T + NB
NC = T // P
EPS = 1e-6
GH, GDK, GDV = 4, 128, 256
HB = 8
RANK = 16
CT = 3 * HB
CW = 4
COL_GLA = 0
COL_R = 2048
COL_CODE = 3072
COL_GDN = COL_CODE + RANK
COL_Z = COL_GDN + CT * P
COL_AB = COL_Z + HB * P
IN_COLS = COL_AB + 2 * HB
XH, XD = 4, 512
NM = 256
DFF = 5632
HALF_K = DFF // 2 // P
DK_ = HALF_K // 2
GAIN_MIX, GAIN_X, GAIN_MEM, GAIN_FFN, GAIN_FINAL, GAIN_GATE_B, GAIN_GLA, GAIN_GDN = 0, 16, 32, 48, 64, 80, 84, 86
LEVELS = 8
UNIT_CREDIT = 2
LO_CREDIT = 4
ACC_CREDIT = 4


class Phase:

    def __init__(self, name, slots, k, s0, u0, t0):
        self.name, self.slots, self.k, self.s0, self.u0, self.t0 = name, slots, k, s0, u0, t0
        self.down = k == DK_
        self.loops = slots // 2
        self.narrow = self.down or name == "gu1"
        self.per = 2 if self.down else 4
        self.cols = NM if name in ("mem_k", "mem_v") else TT


def plan():
    runs = [("strip", 1, KT), ("gdn", 12, KT), ("gla", 8, KT), ("r", 4, KT), ("z", 4, KT), ("w_out", 8, KT), ("x_q", 8, KT),
            ("mem_k", 8, KT), ("mem_v", 8, KT), ("x_o", 8, KT), ("gu0", HALF_K, KT), ("dn0", 16, DK_),
            ("gu1", HALF_K, KT), ("dn1", 16, DK_)]
    s = u = t = 0
    out = {}
    for name, slots, k in runs:
        out[name] = Phase(name, slots, k, s, u, t)
        s += slots
        u += 1 if name == "strip" else 2 * slots
        t += 1 if name == "strip" else slots if k == DK_ else 2 * slots
    return out


def build(nc, a, o):
    PH = plan()
    LAST = PH["dn1"]
    with ExitStack() as ctx:
        def sem(name):
            return ctx.enter_context(nc.semaphore(name))

        base = (nc.sbuf_base + 31) // 32 * 32

        class Here:
            at = base

        def place(name, shape, dt, at=None):
            n = 4
            for d in shape[1:]:
                n *= d
            if at is None:
                at = Here.at
                Here.at += (n + 31) // 32 * 32
            return nc.alloc_sbuf_tensor_at(name, shape, dt, offset=at)

        cols = place("cols", [P, 87], F32)
        convw = place("convw", [P, CW * CT], F32)
        ident = place("ident", [P, P], F32)
        ones = place("ones", [P, P], F32)
        tri = place("tri", [P, P], F32)
        levels = place("levels", [P, LEVELS, P], F32)
        consts = place("consts", [P, 2], F32)
        dtb = place("dtb", [P, HB], F32)
        alog = place("alog", [P, HB], F32)
        rstd = place("rstd", [P, TT], F32)
        sq = place("sq", [P, 2, TT], F32)
        ssq = place("ssq", [P, TT], F32)
        small = place("small", [P, 16, 24], F32)
        x = place("x", [P, KT, TT], F32)
        raw = place("raw", [P, 2, KT, 256], F32)
        C0 = Here.at
        w_hi = [place(f"w_hi{b}", [P, KT, P], R32) for b in range(2)]
        w_lo = [place(f"w_lo{b}", [P, KT, P], R32) for b in range(2)]
        A0 = Here.at
        act_hi = place("act_hi", [P, KT, TT], R32)
        act_lo = place("act_lo", [P, KT, TT], R32)
        M0 = Here.at
        cv = place("cv", [P, CT, TT], F32)
        gla = place("gla", [P, 32, TT], F32)
        S0 = Here.at
        strip = place("strip", [P, TT], F32)
        tail = place("tail", [P, 11, CT], F32)
        pre = place("pre", [P, 2, CW - 1 + TT], F32)
        G0 = Here.at
        cst = place("cst", [P, CT, 3 * NB], F32)
        cacc = place("cacc", [P, 2, TT], F32)
        B0 = Here.at

        xrows = place("xrows", [P, NC, D], F32, M0)
        xsrow = place("xsrow", [NB, D], F32, M0 + 16384)
        grows = place("grows", [87, P], F32, C0)
        cwrows = place("cwrows", [CW * CT, P], F32, C0 + 512)
        crows = place("crows", [3 * NB, CT * P], F32, C0 + 1024)

        UNIT = 16 * P * 4
        gE = [place(f"gE{b}", [P, GH, T], F32, C0 + 4096 * b) for b in range(2)]
        gst = place("gst", [P, NB, GH, GDV], F32, C0 + UNIT)
        A1 = C0 + UNIT + 32768
        gq = [place(f"gq{b}", [P, GH, T], F32, A1 + 8192 * b) for b in range(2)]
        gk = [place(f"gk{b}", [P, GH, T], F32, A1 + 8192 * b + 4096) for b in range(2)]
        gb = place("gb", [P, GH, T], F32, A1 + 16384)
        gsc = place("gsc", [P, GH * NC, P], F32, A1 + 20480)
        gkd = place("gkd", [P, GH, T], F32, A1)
        gkdt = place("gkdt", [P, GH * NC, P], F32, A1 + 4096)
        gqd = place("gqd", [P, GH, P], F32, A1 + 8192)
        gs1 = place("gs1", [P, GH, GDV], F32, B0 + 8192)
        gsf = place("gsf", [P, GH, GDV], F32, B0 + 12288)
        gz = place("gz", [P, GH, TT], F32, B0)
        gaz = place("gaz", [P, GH, TT], F32, B0 + 4224)
        w2 = place("w2", [RANK, GH * GDK], F32, G0)
        tails = place("tails", [4 * CT, 3, P], F32, B0 + 10496)
        gvt = place("gvt", [P, NC, GH * GDV], F32, B0)
        gvrow = place("gvrow", [NB, GH * GDV], F32, A1 + 12288)
        ges = place("ges", [P, GH, NB], F32, G0)
        gqe = place("gqe", [P, GH * NB, GH * NB], F32, C0)
        grow = place("grow", [GH * NB, GDV], F32, C0 + 4096)
        gkq = place("gkq", [P, GH, NB], F32, G0 + 256)
        gks = place("gks", [P, GH, NB], F32, G0 + 384)
        gel = place("gel", [P, GH, 1], F32, G0 + 512)
        got = place("got", [P, 8, NB], F32, G0 + 544)

        U = place("U", [P, 16, P], F32, C0)
        Tm = place("Tm", [P, 16, P], F32, C0 + UNIT)
        Y = place("Y", [P, 16, P], F32, C0 + 2 * UNIT)
        Bt = place("Bt", [P, 16, P], F32, C0 + 3 * UNIT)
        Lt = place("Lt", [P, 16, P], F32, C0 + 4 * UNIT)
        QK = place("QK", [P, 16, P], F32, C0 + 5 * UNIT)
        ktok = place("ktok", [P, 16, P], F32, C0 + 6 * UNIT)
        vb = place("vb", [P, 16, P], F32, C0 + 7 * UNIT)
        rlen = place("rlen", [P, 16, TT], F32, B0 - 8 * TT)
        bst = place("bst", [P, NB, HB, P], F32, C0 + UNIT)
        EG = place("EG", [P, HB, P], F32, B0)
        kbg = place("kbg", [P, HB, P], F32, B0 + 4096)
        nw = place("nw", [P, HB, P], F32, B0 + 8192)
        bs1 = place("bs1", [P, HB, P], F32, B0 + 12288)
        uu = place("uu", [P, 16, P], F32, S0)
        bsf = place("bsf", [P, HB, P], F32, B0)
        urow = place("urow", [HB * NB, P], F32, B0 + 4096)
        sbc = place("sbc", [P, 2, NB * HB], F32, B0 + 4608)
        sdiag = place("sdiag", [NB, 2, NB, HB], F32, C0 + 8 * UNIT)
        skq = place("skq", [P, NB, HB], F32, C0 + 8 * UNIT + 512)
        su = place("su", [P, NB, HB], F32, B0 + 5120)
        so = place("so", [P, NB, HB], F32, B0 + 5376)
        skq2 = place("skq2", [P, NB, HB], F32, B0 + 5632)
        srow = place("srow", [32, 4 * P], F32, B0 + 5888)
        sqk = cv[:, 16:24, 0:T]
        nsq = gla[:, 8:16, :]

        ow_hi = place("ow_hi", [P, KT, TT], R32, M0)
        ow_lo = place("ow_lo", [P, KT, TT], R32, M0 + 4 * KT * TT)
        Q0 = M0 + 8 * KT * TT
        q = place("q", [P, KT, TT], F32, Q0)
        kT = place("kT", [P, KT, NM], F32, Q0 + 4 * KT * TT)
        vm = place("vm", [P, 2, D], F32, Q0 + 4 * KT * (TT + NM))
        mrows = place("mrows", [P, 2, D], F32, Q0 + 4 * KT * (TT + NM))
        R1 = Q0 + 4 * KT * (TT + NM) + 8 * D
        ident_r = place("ident_r", [P, P], R32, R1)
        qc_hi = place("qc_hi", [P, KT], R32, R1 + 4 * P)
        qc_lo = place("qc_lo", [P, KT], R32, R1 + 4 * P + 4 * KT)
        mt = [kT[:, 8 + b, :].rearrange("p (c d) -> p c d", c=2) for b in range(2)]
        vt = [ssq[:, 0:NM], place("vt1", [P, NM], F32, A0 + 2 * 16384)[:, :]]
        kc = [place(f"kc{h}", [P, 2, XD], F32, A0 + 4096 * h) for h in range(XH)]
        vc = [place(f"vc{b}", [P, 2, D], F32, A0 + 16384 * (1 - b)) for b in range(2)]
        pr = place("pr", [P, XH, KT // XH * TT], F32, Q0)
        prT = place("prT", [P, XH, KT // XH * NM], F32, Q0 + 4 * KT * TT)
        sc_s = sq[:, 0, 0:2 * NB * XH].rearrange("p (m n) -> p m n", m=2)
        pT_s = sq[:, 0, 2 * NB * XH:4 * NB * XH].rearrange("p (m n) -> p m n", m=2)
        sc_b = sq[:, 0, 4 * NB * XH:4 * NB * XH + 2 * XH].rearrange("p (m h) -> p m h", m=2)
        p_s = sq[0:NB * XH, 1, 0:NM]
        window = sq[:, 0, 5 * NB * XH:7 * NB * XH - 1]
        orow = place("orow", [NB * XH, XD], F32, Q0 + 4 * KT * TT + 4 * (KT // XH * NM - XD))

        ff_hi = place("ff_hi", [P, HALF_K, TT], R32, M0)
        ff_lo = place("ff_lo", [P, HALF_K, TT], R32, M0 + 4 * HALF_K * TT)
        F0 = M0 + 8 * HALF_K * TT
        g_s = place("g_s", [P, 2, TT], F32, F0)
        u_s = place("u_s", [P, 2, TT], F32, F0 + 8 * TT)
        f_s = place("f_s", [P, 2, TT], F32, F0 + 16 * TT)
        yT = place("yT", [P, KT, TT], F32, A0)
        yrows = place("yrows", [P, NC, D], F32, F0 + 24 * TT)
        ysrow = place("ysrow", [NB, D], F32, C0)

        ps = ctx.enter_context(nc.psum_tensor("ps", [P, 8, 512], F32))
        W4 = 4

        raw_landed = [sem(f"raw_landed{b}") for b in range(2)]
        hi_split = sem("hi_split")
        lo_split = sem("lo_split")
        units_done = sem("units_done")
        acc_free = sem("acc_free")
        rows_landed = sem("rows_landed")
        crows_landed = sem("crows_landed")
        xrows_landed = sem("xrows_landed")
        mrows_landed = sem("mrows_landed")
        consts_ready = sem("consts_ready")
        cols_turned = sem("cols_turned")
        cols_ready = sem("cols_ready")
        x_turned = sem("x_turned")
        x_ready = sem("x_ready")
        x_split = sem("x_split")
        pool_order = sem("pool_order")
        sq_ready = sem("sq_ready")
        ssq_zero = sem("ssq_zero")
        m_taken = sem("m_taken")
        x_taken = sem("x_taken")
        kv_out = sem("kv_out")
        scalars_landed = sem("scalars_landed")
        tails_out = sem("tails_out")
        ff_split = sem("ff_split")
        dve_credit = sem("dve_credit")
        kc_landed = [sem(f"kc_landed{h}") for h in range(XH)]
        vc_landed = [sem(f"vc_landed{b}") for b in range(2)]
        qc_ready = sem("qc_ready")
        mt_ready = sem("mt_ready")
        m_squared = sem("m_squared")
        columns_ready = sem("columns_ready")
        v_first = sem("v_first")
        gla_done = sem("gla_done")
        srow_done = sem("srow_done")
        gla_gated = sem("gla_gated")
        o_gated = sem("o_gated")
        o_hi = sem("o_hi")
        bst_landed1 = sem("bst_landed1")
        v_mixed = sem("v_mixed")
        rows_copied = sem("rows_copied")
        rows_turned = sem("rows_turned")
        s_kept = sem("s_kept")
        k_kept = sem("k_kept")
        ssq_ready = sem("ssq_ready")
        sum_ready = sem("sum_ready")
        rstd_ready = sem("rstd_ready")
        dve_order = sem("dve_order")
        act_order = sem("act_order")
        conv_ready = sem("conv_ready")
        conv_done = sem("conv_done")
        gate_act = sem("gate_act")
        gate_in = sem("gate_in")
        outs = sem("outs")

        class Count:
            dve = act = pool = out = 0

        def dve_link(dve, ins):
            Count.dve += 1
            ins.then_inc(dve_order, 1)
            dve.wait_ge(dve_order, Count.dve)

        def act_link(act, ins):
            Count.act += 1
            ins.then_inc(act_order, 1)
            act.wait_ge(act_order, Count.act)

        def pool_link(pool, ins):
            Count.pool += 1
            ins.then_inc(pool_order, 1)
            pool.wait_ge(pool_order, Count.pool)

        def kview(w, k0, k, c0, n):
            return w.rearrange("(k p) n -> p k n", p=P)[:, k0:k0 + k, ds(c0, n)]

        wi, wo, xq, xk, xv, xo = (a[n][0] for n in ("w_in", "w_out", "xa_w_q", "xa_w_k", "xa_w_v", "xa_w_o"))
        wg, wu, wd = (a[n][0] for n in ("ffn_w_gate", "ffn_w_up", "ffn_w_down"))

        def load(sp, ph, i, j):
            s = ph.s0 + 2 * i + j
            r = (ph.s0 + j) % 2
            sp.wait_ge(lo_split, 2 * s + 1)
            if ph.name == "strip":
                parts = [(raw[:, r, :, 0:32], kview(wi, 0, KT, COL_CODE, 32)),
                         (raw[:, r, :, 32:P], kview(wi, 0, KT, IN_COLS - 96, 96))]
            elif ph.name in ("gu0", "gu1"):
                c0 = (i * 2 + j) * P + (HALF_K * P if ph.name == "gu1" else 0)
                parts = [(raw[:, r, :, 0:P], kview(wg, 0, KT, c0, P)), (raw[:, r, :, P:2 * P], kview(wu, 0, KT, c0, P))]
            elif ph.down:
                k0 = (HALF_K if ph.name == "dn1" else 0) + j * DK_
                c0 = i * 256
                parts = [(raw[:, r, 0:6, :], kview(wd, k0, 6, c0, 256)),
                         (raw[:, r, 6:DK_, :], kview(wd, k0 + 6, DK_ - 6, c0, 256))]
            else:
                w = {"gdn": wi, "gla": wi, "r": wi, "z": wi, "w_out": wo, "x_q": xq, "mem_k": xk, "mem_v": xv, "x_o": xo}[ph.name]
                c0 = i * 512 + j * 256 + {"gdn": COL_GDN, "r": COL_R, "z": COL_Z}.get(ph.name, 0)
                parts = [(raw[:, r, 8 * m:8 * m + 8, :], kview(w, 8 * m, 8, c0, 256)) for m in range(2)]
            for dst, src in parts:
                sp.dma_start(dst, src).then_inc(raw_landed[r], 16)

        def unit_of(ph, i, u):
            s = ph.s0 + u // 2
            return s % 2, 32 * (s // 2 + i + 1), u % 2, (ph.u0 + u) % 2, ph.u0 + 4 * i + u

        def split_hi(act, ph, i, u):
            r, landed, half, b, n = unit_of(ph, i, u)
            act.wait_ge(raw_landed[r], landed)
            act.wait_ge(units_done, n + 1)
            act.activation(w_hi[b][:, 0:ph.k, :], raw[:, r, 0:ph.k, half * P:half * P + P], ACT.Copy)\
               .then_inc(hi_split, 1)

        def split_lo(dve, ph, i, u):
            r, landed, half, b, n = unit_of(ph, i, u)
            dve.wait_ge(hi_split, n + 1)
            dve.tensor_tensor(w_lo[b][:, 0:ph.k, :], raw[:, r, 0:ph.k, half * P:half * P + P],
                              w_hi[b][:, 0:ph.k, :], ALU.subtract).then_inc(lo_split, 1)

        def products(pe, ph, i, u, hi, lo, k0=0):
            b, n = (ph.u0 + u) % 2, ph.u0 + 4 * i + u
            t = ph.t0 + ph.per * i + (u % 2 if ph.down else u)
            first = not ph.down or u < 2
            last = not ph.down or u >= 2
            if first:
                pe.wait_ge(acc_free, t + (3 if ph.narrow else 1))
            pe.wait_ge(lo_split, n + 1 + LO_CREDIT)
            kk = k0 + (DK_ * (u // 2) if ph.down else 0)
            for k in range(ph.k):
                for m, (w, v) in enumerate(((w_lo, hi), (w_hi, lo), (w_hi, hi))):
                    mm = pe.matmul(ps[:, acc(ph, u), 0:ph.cols], w[b][:, k, :], v[:, kk + k, 0:ph.cols],
                                   start=first and k == 0 and m == 0,
                                   stop=last and k == ph.k - 1 and m == 2)
            mm.then_inc(units_done, 1)

        def acc(ph, u):
            return (ph.t0 + (u % 2 if ph.down else u)) % 4

        def phase_pe(pe, ph, hi, lo):
            with pe.Fori(0, ph.loops) as i:
                for u in range(4):
                    products(pe, ph, i, u, hi, lo)


        N = {}
        for name in ("turned scalars prep gla_pre gla_exp gla_lvl gla_scored gla_picked gla_turned "
                     "gla_tok gla_mm gla_out gla_s gla_smm sstate_landed state_out gla_dec gla_qe "
                     "gla_bc gla_sc gla_srow gdn_sq gdn_sum gdn_ln gdn_normed gdn_turned gdn_ktok gdn_vb gdn_g gdn_gcol gdn_scal "
                     "gdn_pair gdn_dmin gdn_dexp gdn_lt gdn_qkm gdn_bt gdn_t0 y_done y_copied tyuy_done inv_ready "
                     "gdn_kbg gdn_f1 gdn_e1 gdn_f2 gdn_e2 gdn_f3 gdn_e3 gdn_f4 gdn_e4 bst_landed gdn_sx gdn_sbc gdn_sval "
                     "gdn_ub gdn_ubt gdn_surow gdn_u norm_sq norm_sum norm_rb silu_g o_ready tails_copied "
                     "m_turned m_ready kv_turned kv_copied att_qk att_max att_exp att_norm att_pturned att_pT att_o att_oe "
                     "gdn_uspread k_out k_out3 qc_split s_qb s_dot s_st s_sm s_exp s_pn s_ptt s_pT s_o s_oe y_norm y_turned y_copied_act y_copied_dve "
                     "gla_eexp gla_la gla_bgate").split():
            N[name] = sem(name)

        def W(eng, name, n):
            eng.wait_ge(N[name], n)

        def tile_wait(eng, ph, i, u):
            eng.wait_ge(units_done, ph.u0 + 4 * i + u + 1 + UNIT_CREDIT)

        def out_of(ph, u):
            return ps[:, acc(ph, u), 0:ph.cols]

        def dve_take(dve):
            R = rstd[:, :]

            def residual(ph, i, u, base, gain):
                n = i * 2 + (u - 2) if ph.down else i * 4 + u
                tile_wait(dve, ph, i, u)
                dve.tensor_tensor(x[:, ds(n, 1), :], x[:, ds(n, 1), :], out_of(ph, u), ALU.add).then_inc(x_ready, 1)
                dve.wait_ge(x_ready, n + base + KT + 1)
                if gain is not None:
                    g = cols[:, ds(n + gain, 1)]
                    dve.tensor_scalar(act_hi[:, ds(n, 1), :], x[:, ds(n, 1), :], g, None, ALU.mult).then_inc(x_split, 1)
                    dve.wait_ge(x_split, n + base + 1)
                    dve.scalar_tensor_tensor(out=act_lo[:, ds(n, 1), :], in0=x[:, ds(n, 1), :], scalar=g,
                                             in1=act_hi[:, ds(n, 1), :], op0=ALU.mult, op1=ALU.subtract)\
                       .then_inc(acc_free, 1)

            def scaled(dst, r):
                def f(ph, i, u):
                    tile_wait(dve, ph, i, u)
                    dve.tensor_tensor(dst[:, ds(i * 4 + u, 1), 0:ph.cols], out_of(ph, u), r, ALU.mult)\
                       .then_inc(acc_free, 1)
                return f

            def gdn(ph, i, u):
                n = i * 4 + u
                b = u % 2
                tile_wait(dve, ph, i, u)
                dve.wait_ge(conv_done, i * 4 + u + 1)
                dve.tensor_tensor(pre[:, b, 3:3 + TT], out_of(ph, u), R, ALU.mult).then_inc(acc_free, 1)
                dve.wait_ge(acc_free, ph.t0 + n + 1 + ACC_CREDIT)
                for j in range(CW):
                    w = convw[:, ds(n + j * CT, 1)]
                    for dst, src in ((cacc[:, b, 0:T], pre[:, b, j:j + T]),
                                     (cacc[:, b, T:TT], cst[:, ds(n, 1), j * NB:(j + 1) * NB] if j < CW - 1
                                      else pre[:, b, 3 + T:3 + TT])):
                        if j == 0:
                            ins = dve.tensor_scalar(dst, src, w, None, ALU.mult)
                        else:
                            ins = dve.scalar_tensor_tensor(out=dst, in0=src, scalar=w, in1=dst, op0=ALU.mult,
                                                           op1=ALU.add)
                    ins.then_inc(conv_ready, 1)
                    dve.wait_ge(conv_ready, n * 4 + j + 1)

            def gate_up(half):
                def f(ph, i, u):
                    n = 2 * i + u // 2
                    c = HALF_K * half + n
                    b = u // 2
                    tile_wait(dve, ph, i, u)
                    if u % 2 == 0:
                        dve.tensor_tensor(g_s[:, b, :], out_of(ph, u), R, ALU.mult).then_inc(acc_free, 1)
                        return
                    dve.tensor_tensor(u_s[:, b, :], out_of(ph, u), R, ALU.mult).then_inc(acc_free, 1)
                    dve.wait_ge(gate_act, c + 1)
                    dve.wait_ge(acc_free, ph.t0 + 4 * i + u + 1 + ACC_CREDIT)
                    dve.tensor_tensor(f_s[:, b, :], g_s[:, b, :], u_s[:, b, :], ALU.mult).then_inc(gate_in, 1)
                    dve.wait_ge(gate_in, 2 * c + 1)
                    dve.tensor_copy(ff_hi[:, ds(n, 1), :], f_s[:, b, :]).then_inc(gate_in, 1)
                    dve.wait_ge(gate_in, 2 * c + 2)
                    dve.tensor_tensor(ff_lo[:, ds(n, 1), :], f_s[:, b, :], ff_hi[:, ds(n, 1), :], ALU.subtract)\
                       .then_inc(ff_split, 1)
                return f

            def down(last):
                def f(ph, i, u):
                    if u < 2:
                        return
                    n = i * 2 + (u - 2)
                    tile_wait(dve, ph, i, u)
                    ins = dve.tensor_tensor(x[:, ds(n, 1), :], x[:, ds(n, 1), :], out_of(ph, u), ALU.add)
                    ins.then_inc(acc_free, 1)
                return f

            return scaled, gdn, residual, gate_up, down

        G2 = [a["gla_w_gate2"][0], a["gla_b_gate"][0]]
        DA, DB, TMP, SP_, EB, EAL, G_, BETA, GC, GL, GD, EG1, KD, EGL, BG = range(15)

        def sm(k):
            return small[:, k, :].rearrange("p (h c) -> p h c", c=3)

        def unit_ps(b0, n):
            return ps[:, b0 + n // 4, (n % 4) * P:(n % 4) * P + P]

        def heads_of(bank):
            return ps[:, bank, :].rearrange("p (u t) -> p u t", u=4)

        def halves(v, m):
            return v.rearrange("p h (n s m) -> p h n s m", s=2, m=m)

        def prompt_tiles(b):
            return range((b - 2) * KT // (NB - 2), (b - 1) * KT // (NB - 2)) if b >= 2 else range(0)

        block = ctx.enter_context(nc.Block())

        @block.sync
        def _(sp):
            for name, r0, n in (("g_mix", GAIN_MIX, 16), ("g_xattn", GAIN_X, 16), ("g_mem", GAIN_MEM, 16),
                                ("g_ffn", GAIN_FFN, 16), ("g_final", GAIN_FINAL, 16),
                                ("gla_b_gate", GAIN_GATE_B, 4), ("gla_g_out", GAIN_GLA, 2), ("gdn_g_out", GAIN_GDN, 1)):
                src = a[name] if name == "g_final" else a[name][0]
                sp.dma_start(grows[r0:r0 + n, :], src.rearrange("(r p) -> r p", p=P)).then_inc(rows_landed, 16)
            sp.dma_start(cwrows[:, :], a["gdn_conv_w"][0].rearrange("j (t p) -> (j t) p", p=P)).then_inc(rows_landed, 16)
            sp.dma_start(crows[:, :], a["state_conv"][0].rearrange("b j c -> (b j) c")).then_inc(crows_landed, 16)
            sp.dma_start(xrows[:, :, :], a["x_prompt"][0].rearrange("(c p) d -> p c d", p=P)).then_inc(xrows_landed, 16)
            sp.dma_start(xsrow[:, :], a["x_sample"].rearrange("b s d -> (b s) d")).then_inc(xrows_landed, 16)
            load(sp, PH["strip"], 0, 0)
            sp.dma_start(dtb[:, :], a["gdn_dt_bias"][0].partition_broadcast(P)).then_inc(scalars_landed, 16)
            sp.dma_start(alog[:, :], a["gdn_a_log"][0].partition_broadcast(P)).then_inc(scalars_landed, 16)
            sp.dma_start(o["conv_s"][0][:, 0:CW - 2, :], a["state_conv"][0][:, 1:CW - 1, :]).then_inc(outs, 16)

            def stream(name):
                ph = PH[name]
                with sp.Fori(0, ph.loops) as i:
                    for j in range(2):
                        load(sp, ph, i, j)

            stream("gdn")
            stream("gla")
            sp.wait_ge(conv_done, CT + 2)
            sp.dma_start(w2[:, :], G2[0]).then_inc(scalars_landed, 16)
            stream("r")
            stream("z")
            for j in range(2):
                load(sp, PH["w_out"], 0, j)
            sp.wait_ge(units_done, PH["w_out"].u0 + UNIT_CREDIT)
            sp.dma_start(gst[:, :, :, :], a["state_gla"][0].rearrange("b h k v -> k b h v")).then_inc(N["sstate_landed"], 16)
            W(sp, "tails_copied", 3)
            sp.dma_start(o["conv_p"][0, 0].rearrange("j (t p) -> (j t) p", p=P), tails[0:3 * CT, 0, :]).then_inc(tails_out, 16)
            for b in range(NB):
                sp.dma_start(o["conv_s"][0][b, CW - 2].rearrange("(t p) -> t p", p=P),
                             tails[(b % 4) * CT:(b % 4 + 1) * CT, 1 + b // 4, :]).then_inc(tails_out, 16)
            W(sp, "gla_out", 3)
            sp.dma_start(o["gla_p"][0, 0].rearrange("h k v -> k h v"), gsf[:, :, :]).then_inc(N["state_out"], 16)
            W(sp, "gla_srow", NB)
            sp.dma_start(o["gla_s"][0].rearrange("b h k v -> k b h v"), gst[:, :, :, :]).then_inc(N["state_out"], 16)
            W(sp, "inv_ready", 4 * (LEVELS - 2))
            W(sp, "tyuy_done", 4 * (LEVELS - 2))
            sgdn, half = a["state_gdn"][0].rearrange("b h k v -> k b h v"), NB // 2
            sp.dma_start(bst[:, 0:half, :, :], sgdn[:, 0:half]).then_inc(N["bst_landed"], 16)
            sp.dma_start(bst[:, half:NB, :, :], sgdn[:, half:NB]).then_inc(bst_landed1, 16)
            W(sp, "gdn_e4", 4)
            sp.dma_start(o["gdn_p"][0, 0].rearrange("h k v -> k h v"), bsf[:, :, :]).then_inc(N["state_out"], 16)
            for b in range(0, NB, 2):
                W(sp, "gdn_surow", 2 * b + 4)
                sp.dma_start(o["gdn_s"][0].rearrange("b h k v -> k b h v")[:, b:b + 2], bst[:, b:b + 2, :, :])\
                  .then_inc(N["state_out"], 16)

            def rest(name, first):
                ph = PH[name]
                if first:
                    with sp.Fori(1, ph.loops) as i:
                        for j in range(2):
                            load(sp, ph, i, j)
                else:
                    stream(name)

            W(sp, "o_ready", 4)
            W(sp, "state_out", 16 * (3 + NB // 2))
            sp.dma_start(mrows[:, :, :], a["mem_prompt"][0].rearrange("(c p) d -> p c d", p=P)).then_inc(mrows_landed, 16)
            rest("w_out", True)
            rest("x_q", False)

            def key_cache(b, h):
                sp.dma_start(kc[h][:, :, :], a["cache_mem_k"][0][ds(b, 1), :, h, :].rearrange("o (m p) d -> p (o m) d", p=P))\
                  .then_inc(kc_landed[h], 16)

            def store_rows(dst, c0, n):
                return sp.dma_start(o[dst][0, 0].rearrange("(c p) h d -> p c (h d)", p=P)[:, :, ds(c0, n)],
                                    vm[:, :, ds(c0, n)])

            for name, b0 in (("mem_k", 0), ("mem_v", NB // 2)):
                ph = PH[name]
                for j in range(2):
                    load(sp, ph, 0, j)
                if b0 == 0:
                    sp.wait_ge(units_done, ph.u0 + UNIT_CREDIT)
                for h in range(XH):
                    if b0:
                        W(sp, "s_dot", XH * (b0 - 1) + h + 1 + 2)
                    key_cache(b0, h)
                if b0:
                    W(sp, "kv_copied", KT + 2)
                    store_rows("mem_k", XD * (XH - 1), XD).then_inc(N["k_out3"], 16)
                    sp.dma_start(vc[0][:, :, :], a["cache_mem_v"][0][0].rearrange("(m p) h d -> p m (h d)", p=P))\
                      .then_inc(vc_landed[0], 16)
                with sp.Fori(1, ph.loops) as i:
                    for j in range(2):
                        load(sp, ph, i, j)
                        for h in (2 * j, 2 * j + 1):
                            W(sp, "s_dot", i * XH + (XH * (b0 - 1) + h + 1 + 2))
                            key_cache(i + b0, h)
                    if b0 == 0:
                        W(sp, "kv_copied", i * 4 + 2)
                        store_rows("mem_k", i * XD - XD, XD).then_inc(N["k_out"], 16)
            for j in range(2):
                load(sp, PH["x_o"], 0, j)
            for b in range(1, NB):
                if b == 1:
                    W(sp, "s_dot", XH * NB + 2)
                else:
                    W(sp, "s_o", b - 1)
                sp.dma_start(vc[b % 2][:, :, :], a["cache_mem_v"][0][b].rearrange("(m p) h d -> p m (h d)", p=P))\
                  .then_inc(vc_landed[b % 2], 16)
                if b == 1:
                    W(sp, "kv_copied", 2 * KT + 2)
                    store_rows("mem_v", 0, D).then_inc(kv_out, 16)
            rest("x_o", True)
            for name in ("gu0", "dn0", "gu1", "dn1"):
                stream(name)
            W(sp, "y_copied_act", 4)
            W(sp, "y_copied_dve", 4)
            sp.dma_start(o["y_p"][0].rearrange("(c p) d -> p c d", p=P), yrows[:, :, :]).then_inc(outs, 16)
            sp.dma_start(o["y_s"].rearrange("b s d -> (b s) d"), ysrow[:, :]).then_inc(outs, 16)
            sp.wait_ge(outs, 16 * 3)
            sp.wait_ge(tails_out, 16 * (1 + NB))
            sp.wait_ge(kv_out, 16)
            W(sp, "k_out", 16 * (XH - 1))
            W(sp, "k_out3", 16)

        @block.gpsimd
        def _(pool):
            pool_link(pool, pool.memset(levels[:, :, :], 0.0))
            pool_link(pool, pool.memset(consts[:, 0:1], EPS))
            pool_link(pool, pool.memset(consts[:, 1:2], 1.0))
            pool_link(pool, pool.memset(ones[:, :], 1.0))
            pool_link(pool, pool.affine_select(out=levels[:, 0, :], in_=levels[:, 0, :], compare_op=ALU.not_equal,
                                               fill=1.0, base=0, pattern=[[-1, P]], channel_multiplier=1))
            pool_link(pool, pool.tensor_copy(ident[:, :], levels[:, 0, :]))
            pool_link(pool, pool.affine_select(out=tri[:, :], in_=ones[:, :], compare_op=ALU.is_ge, fill=0.0, base=0,
                                               pattern=[[1, P]], channel_multiplier=-1))
            for l in range(1, LEVELS):
                m = 1 << (l - 1)
                v = levels[:, l, :].rearrange("p (n s m) -> p n s m", s=2, m=m)[:, :, 1, :]
                nb = P // (2 * m)
                pool_link(pool, pool.memset(v, 1.0))
                pool_link(pool, pool.affine_select(out=v, in_=v, compare_op=ALU.is_ge, fill=0.0, base=0,
                                                   pattern=[[-2 * m, nb], [0, m]], channel_multiplier=1))
                pool_link(pool, pool.affine_select(out=v, in_=v, compare_op=ALU.is_ge, fill=0.0, base=m - 1,
                                                   pattern=[[2 * m, nb], [0, m]], channel_multiplier=-1))
            pool.memset(pre[:, :, 0:CW - 1], 0.0).then_inc(consts_ready, 1)

            def squares(k, waits, src, width):
                base = KT * (k - 1 if k < 3 else k - 2)
                waits(0)
                if k > 1:
                    pool.wait_ge(sum_ready, k - 1)
                pool.memset(ssq[:, 0:width], 0.0).then_inc(ssq_zero, 1)
                pool.wait_ge(ssq_zero, k)
                with pool.Fori(0, KT // 2) as i:
                    for b in range(2):
                        n = i * 2 + b
                        waits(n)
                        pool.tensor_tensor(sq[:, b, 0:width], src[:, ds(n, 1), 0:width], src[:, ds(n, 1), 0:width],
                                           ALU.mult).then_inc(sq_ready, 1)
                        pool.wait_ge(sq_ready, n + base + 1)
                        pool.tensor_tensor(ssq[:, 0:width], ssq[:, 0:width], sq[:, b, 0:width], ALU.add)\
                            .then_inc(ssq_ready, 1)

            def taken(ph):
                return lambda n: pool.wait_ge(acc_free, n + ph.t0 + 1 + ACC_CREDIT)

            squares(1, lambda n: pool.wait_ge(x_ready, n + 1), x, TT)
            pool.wait_ge(acc_free, PH["w_out"].t0 + ACC_CREDIT)
            for b in range(2):
                pool.memset(gq[b][:, :, :], 0.0)
                last = pool.memset(gk[b][:, :, :], 0.0)
            last.then_inc(N["prep"], 1)
            W(pool, "gla_dec", LEVELS + 1)
            pool.memset(gqe[:, :, :], 0.0).then_inc(columns_ready, 1)
            W(pool, "gdn_vb", 4)
            pool_link(pool, pool.memset(sqk, 0.0))
            for m in range(2):
                for s in range(2):
                    ins = pool.tensor_copy(sqk[:, m:NB:2, 16 * m + s:16 * m + s + 34 * HB - 33:34],
                                           cv[:, 8 * s:8 * s + 8, T + m:TT:2].rearrange("p h b -> p b h"))
            ins.then_inc(columns_ready, 1)
            for g in range(4):
                W(pool, "gdn_lt", g + 1)
                v = QK[:, 4 * g:4 * g + 4, :]
                pool.tensor_tensor(v, v, tri[:, :].unsqueeze(1).broadcast_to([P, 4, P]), ALU.mult)\
                    .then_inc(N["gdn_qkm"], 1)
                pool.tensor_tensor(Bt[:, 4 * g:4 * g + 4, :], Lt[:, 4 * g:4 * g + 4, :],
                                   levels[:, 1, :].unsqueeze(1).broadcast_to([P, 4, P]), ALU.mult)\
                    .then_inc(N["gdn_bt"], 1)
            for l in range(2, LEVELS):
                for g in range(4):
                    if l == 2:
                        W(pool, "gdn_t0", g + 1)
                        W(pool, "inv_ready", g + 1)
                    else:
                        W(pool, "y_done", 4 * (l - 3) + g + 1)
                    pool.tensor_tensor(Bt[:, 4 * g:4 * g + 4, :], Lt[:, 4 * g:4 * g + 4, :],
                                       levels[:, l, :].unsqueeze(1).broadcast_to([P, 4, P]), ALU.mult)\
                        .then_inc(N["gdn_bt"], 1)
            W(pool, "gdn_sval", 1)
            for b in range(NB):
                pool.tensor_tensor(bst[:, b, :, :], bst[:, b, :, :],
                                   sbc[:, 0, b * HB:(b + 1) * HB].unsqueeze(2).broadcast_to([P, HB, P]), ALU.mult)\
                    .then_inc(N["gdn_ubt"], 1)
            squares(2, taken(PH["w_out"]), x, TT)
            pool.wait_ge(mrows_landed, 16)
            pool.wait_ge(sum_ready, 2)
            pool.memset(ssq[:, 0:NM], 0.0).then_inc(ssq_zero, 1)
            pool.wait_ge(ssq_zero, 3)
            with pool.Fori(0, KT // 2) as i:
                for b in range(2):
                    n = i * 2 + b
                    W(pool, "m_turned", n + 1)
                    pool.tensor_copy(mt[b], mrows[:, :, ds(i * 2 * P + b * P, P)]).then_inc(mt_ready, 1)
                    pool.wait_ge(m_squared, n + 1 + 2)
                    pool.wait_ge(ssq_ready, n + 2 * KT)
                    pool.tensor_tensor(ssq[:, 0:NM], ssq[:, 0:NM], sq[:, b, 0:NM], ALU.add).then_inc(ssq_ready, 1)
            with pool.Fori(0, KT // 2) as i:
                for b in range(2):
                    pool.wait_ge(acc_free, i * 2 + (PH["mem_k"].t0 + b + 1 + ACC_CREDIT))
                    pool.tensor_copy(kT[:, ds(i * 2 + b, 1), :], vt[b]).then_inc(k_kept, 1)
            pool_link(pool, pool.memset(window, 0.0))
            pool.memset(window[:, NB * XH - 1:NB * XH], 1.0).then_inc(columns_ready, 1)
            squares(4, taken(PH["x_o"]), x, TT)
            squares(5, taken(PH["dn1"]), x, TT)

        @block.tensor
        def _(pe):
            def turn(dst, src):
                return pe.transpose(dst, src, ident[0:src.shape[0], 0:src.shape[0]])

            def sum_squares(k, width):
                pe.wait_ge(ssq_ready, KT * k)
                pe.matmul(ps[:, 7, 0:width], ones[:, :], ssq[:, 0:width], start=True, stop=True).then_inc(sum_ready, 1)

            pe.wait_ge(consts_ready, 1)
            pe.wait_ge(rows_landed, 16 * 9)
            turn(ps[:, 4, 0:87], grows[:, :])
            turn(ps[:, 4, P:P + CW * CT], cwrows[:, :])
            pe.wait_ge(crows_landed, 16)
            for t in range(CT):
                mm = turn(ps[:, 5 + t // 12, (t % 12) * 24:(t % 12) * 24 + 24], crows[:, t * P:(t + 1) * P])
            mm.then_inc(cols_turned, 1)
            pe.wait_ge(xrows_landed, 32)
            pe.wait_ge(cols_ready, 3)
            for k in range(KT):
                if k >= 4:
                    pe.wait_ge(x_taken, k - 3)
                for c in range(NC):
                    turn(ps[:, W4 + k % 4, c * P:(c + 1) * P], xrows[:, c, k * P:(k + 1) * P])
                turn(ps[:, W4 + k % 4, T:TT], xsrow[:, k * P:(k + 1) * P]).then_inc(x_turned, 1)
            pe.wait_ge(x_taken, KT)
            sum_squares(1, TT)
            products(pe, PH["strip"], 0, 0, act_hi, act_lo)
            phase_pe(pe, PH["gdn"], act_hi, act_lo)
            ph = PH["gla"]
            with pe.Fori(0, ph.loops) as i:
                for u in range(4):
                    products(pe, ph, i, u, act_hi, act_lo)
                    W(pe, "gdn_sq", i * 4 + u + 1)
                    W(pe, "gdn_ln", i * 4 + u + 1)
                    pe.matmul(ps[:, 4 + u % 2, 0:TT], ones[:, :], sq[:, u % 2, :], start=True, stop=True)\
                      .then_inc(N["gdn_sum"], 1)
            phase_pe(pe, PH["r"], act_hi, act_lo)
            phase_pe(pe, PH["z"], act_hi, act_lo)

            pe.wait_ge(acc_free, PH["w_out"].t0 + ACC_CREDIT)
            for c in range(NC):
                turn(ps[:, 0, c * P:(c + 1) * P], strip[:, c * P:(c + 1) * P])
            turn(ps[0:NB, 0, 2 * P:3 * P], strip[:, T:TT])
            pe.wait_ge(conv_done, CT + 2)
            for g, (j0, nj) in enumerate(((0, 3), (3, 4), (7, 4))):
                mm = turn(ps[0:nj * CT, 1, g * P:(g + 1) * P], tail[:, j0:j0 + nj, :].rearrange("p j t -> p (j t)"))
            mm.then_inc(N["turned"], 1)
            pe.wait_ge(scalars_landed, 16 * 3)
            for h in range(GH):
                mm = pe.matmul(ps[:, 4 + h, 0:TT], w2[:, h * P:(h + 1) * P], strip[0:RANK, :], start=True, stop=True)
            mm.then_inc(N["gla_pre"], 1)
            W(pe, "gdn_g", 1)
            for c in range(NC):
                pe.matmul(ps[:, 2, c * HB:(c + 1) * HB], tri[:, :], sm(G_)[:, :, c], start=True, stop=True)
                mm = pe.matmul(ps[:, 2, (2 + c) * HB:(3 + c) * HB], ones[:, :], sm(G_)[:, :, c], start=True, stop=True)
            mm.then_inc(N["gdn_gcol"], 1)
            W(pe, "gla_la", 1)
            W(pe, "gdn_scal", 1)
            for n in range(NC * 8):
                c, t = n // 8, n % 8
                mm = turn(unit_ps(4, n), gla[:, 8 + t, c * P:(c + 1) * P])
            mm.then_inc(N["gla_turned"], 1)
            for l in range(LEVELS):
                qs, ks = (gla[:, 0:GH, :], gla[:, GH:2 * GH, :]) if l == 0 else (gq[l % 2], gk[l % 2])
                if l:
                    W(pe, "gla_lvl", l)
                if l >= 2:
                    W(pe, "gla_picked", l - 1)
                for n in range(GH * NC):
                    h, c = n // NC, n % NC
                    mm = pe.matmul(unit_ps(2 * (l % 2), n), ks[:, h, c * P:(c + 1) * P], qs[:, h, c * P:(c + 1) * P],
                                   start=True, stop=True)
                mm.then_inc(N["gla_scored"], 1)
            W(pe, "gla_picked", LEVELS)
            W(pe, "gla_dec", LEVELS + 1)
            for n in range(GH * NC):
                mm = turn(unit_ps(0, n), gkd[:, n // NC, (n % NC) * P:(n % NC + 1) * P])
            for t in range(8):
                mm = turn(ps[0:NB, 2 + t // 4, (t % 4) * P:(t % 4 + 1) * P], gla[:, 8 + t, T:TT])
            mm.then_inc(N["gla_turned"], 1)
            W(pe, "gla_tok", 8)
            for h in range(GH):
                pe.matmul(ps[:, h // 2, (h % 2) * GDV:(h % 2 + 1) * GDV], gkdt[:, 2 * h, :],
                          gvt[:, 0, h * GDV:(h + 1) * GDV], start=True, stop=True)
            for j in range(8):
                mm = pe.matmul(unit_ps(4, j), gvt[:, 0, j * P:(j + 1) * P], gsc[:, 2 * (j // 2), :], start=True, stop=True)
            mm.then_inc(N["gla_mm"], 1)
            W(pe, "gla_out", 1)
            W(pe, "gla_s", 1)
            for j in range(8):
                h, e = j // 2, j % 2
                pe.matmul(unit_ps(6, j), gs1[:, h, e * P:(e + 1) * P], gqd[:, h, :], start=True, stop=False)
                mm = pe.matmul(unit_ps(6, j), gvt[:, 1, j * P:(j + 1) * P], gsc[:, 2 * h + 1, :], start=False, stop=True)
            for h in range(GH):
                mm = pe.matmul(ps[:, h // 2, (h % 2) * GDV:(h % 2 + 1) * GDV], gkdt[:, 2 * h + 1, :],
                               gvt[:, 1, h * GDV:(h + 1) * GDV], start=True, stop=True)
            mm.then_inc(N["gla_mm"], 1)
            W(pe, "gla_qe", 1)
            W(pe, "gla_out", 3)
            pe.wait_ge(N["sstate_landed"], 16)
            pe.matmul(ps[:, 4, 0:GH * NB], ones[:, :], gkq[:, :, :].rearrange("p h b -> p (h b)"), start=True, stop=True)
            for b in range(NB):
                for h in range(GH):
                    n = h * NB + b
                    mm = pe.matmul(ps[0:GH * NB, 5, 0:GDV], gqe[:, n, :], gst[:, b, h, :],
                                   start=b == 0 and h == 0, stop=b == NB - 1 and h == GH - 1)
                mm.then_inc(N["gla_smm"], 1)
            for b in range(NB):
                if b >= 3:
                    W(pe, "gla_srow", b - 2)
                bank = (0, 2, 6)[b % 3]
                for m in range(2):
                    mm = pe.matmul(ps[:, bank + m, :], ident[0:NB, b:b + 1].broadcast_to([NB, P]),
                                   gvrow[:, m * 512:(m + 1) * 512], start=True, stop=True)
                mm.then_inc(N["gla_bc"], 1)
                if b == 3:
                    pe.wait_ge(rows_copied, 1)
                    for e in range(2):
                        mm = turn(ps[:, 5, 256 + e * 32:256 + (e + 1) * 32], grow[:, e * P:(e + 1) * P])
                    mm.then_inc(N["gla_turned"], 1)

            W(pe, "gla_srow", NB)
            W(pe, "gdn_normed", 4)
            for g in range(4):
                if g >= 2:
                    W(pe, "gdn_ktok", g - 1)
                    W(pe, "gdn_vb", g - 1)
                if g == 1:
                    pe.wait_ge(gla_done, 1)
                for t in range(2):
                    for n in range(4):
                        h, c = 2 * g + n // 2, n % 2
                        mm = turn(ps[:, 4 * (g % 2) + t, n * P:(n + 1) * P], cv[:, 8 + 8 * t + h, c * P:(c + 1) * P])
                mm.then_inc(N["gdn_turned"], 1)
            W(pe, "norm_sq", 1)
            for t in range(GH):
                bank = (2, 3, 6, 7)[t]
                pe.matmul(ps[:, bank, 0:TT], ones[:, :], nsq[:, 2 * t, :], start=True, stop=False)
                pe.matmul(ps[:, bank, 0:TT], ones[:, :], nsq[:, 2 * t + 1, :], start=False, stop=True)\
                  .then_inc(N["norm_sum"], 1)
            for g in range(4):
                if g >= 2:
                    W(pe, "gdn_lt", g - 1)
                else:
                    W(pe, "gdn_ktok", g + 3)
                    W(pe, "gdn_vb", g + 3)
                    W(pe, "norm_rb", 2 * g + 2)
                b0 = 4 * (g % 2)
                for n in range(4):
                    h, c = 2 * g + n // 2, n % 2
                    tok = slice(c * P, (c + 1) * P)
                    at_n = slice(n * P, (n + 1) * P)
                    pe.matmul(ps[:, b0, at_n], sm(G_)[:, h, c:c + 1].broadcast_to([P, P]), tri[:, :], start=True, stop=True)
                    pe.matmul(ps[:, b0 + 1, at_n], sm(BETA)[:, h, c:c + 1].broadcast_to([P, P]), ident[:, :],
                              start=True, stop=True)
                    pe.matmul(ps[:, b0 + 2, at_n], cv[:, 8 + h, tok], cv[:, 8 + h, tok], start=True, stop=True)
                    mm = pe.matmul(ps[:, b0 + 3, at_n], cv[:, 8 + h, tok], cv[:, h, tok], start=True, stop=True)
                mm.then_inc(N["gdn_pair"], 1)
            for g in range(4):
                W(pe, "gdn_bt", g + 1)
                if g == 0:
                    W(pe, "gdn_lt", 4)
                for n in range(4):
                    mm = turn(ps[:, g, n * P:(n + 1) * P], Bt[:, 4 * g + n, :])
                mm.then_inc(N["gdn_t0"], 1)
            for l in range(2, LEVELS):
                for g in range(4):
                    W(pe, "inv_ready", 4 * (l - 2) + g + 1)
                    W(pe, "gdn_bt", 4 * (l - 1) + g + 1)
                    for n in range(4):
                        mm = pe.matmul(ps[:, g, n * P:(n + 1) * P], Bt[:, 4 * g + n, :], Tm[:, 4 * g + n, :],
                                       start=True, stop=True)
                    mm.then_inc(N["y_done"], 1)
                for g in range(4):
                    W(pe, "y_copied", 4 * (l - 2) + g + 1)
                    if g >= 2:
                        W(pe, "inv_ready", 4 * (l - 1) + g - 1)
                    b0 = 4 + 2 * (g % 2)
                    for n in range(4):
                        v = 4 * g + n
                        if l < LEVELS - 1:
                            pe.matmul(ps[:, b0, n * P:(n + 1) * P], U[:, v, :], Y[:, v, :], start=True, stop=True)
                        mm = pe.matmul(ps[:, b0 + 1, n * P:(n + 1) * P], Y[:, v, :], U[:, v, :], start=True, stop=True)
                    mm.then_inc(N["tyuy_done"], 1)
            W(pe, "inv_ready", 4 * (LEVELS - 1))
            W(pe, "gdn_kbg", 1)
            W(pe, "gdn_qkm", 4)
            for g in range(2):
                for n in range(4):
                    h = 4 * g + n
                    pe.matmul(unit_ps(g, n), kbg[:, h, :], U[:, 2 * h + 1, :], start=True, stop=True)
                    mm = pe.matmul(unit_ps(2 + g, n), U[:, 2 * h, :], vb[:, 2 * h, :], start=True, stop=True)
                mm.then_inc(N["gdn_f1"], 1)
            for g in range(2):
                W(pe, "gdn_e1", g + 1)
                for n in range(4):
                    h = 4 * g + n
                    pe.matmul(unit_ps(4 + g, n), ktok[:, 2 * h, :], uu[:, 2 * h, :], start=True, stop=True)
                    mm = pe.matmul(unit_ps(6 + g, n), uu[:, 2 * h, :], QK[:, 2 * h, :], start=True, stop=True)
                mm.then_inc(N["gdn_f2"], 1)
            W(pe, "gdn_sx", 1)
            for m in range(2):
                pe.matmul(ps[:, 2, m * 64:(m + 1) * 64], ones[0:NB, :],
                          sdiag[:, m, :, :].rearrange("p b h -> p (b h)"), start=True, stop=True)
            pe.matmul(ps[:, 2, 2 * 64:3 * 64], ones[:, :], skq[:, :, :].rearrange("p b h -> p (b h)"), start=True, stop=True)

            def on_state(b):
                for h in range(HB):
                    at = b // 2 * P
                    mm = pe.matmul(ps[0:32, 3, at:at + P], sqk[:, b, 32 * h:32 * h + 32], bst[:, b, h, :],
                                   start=b % 2 == 0 and h == 0, stop=b % 2 == 1 and h == HB - 1)
                if b == NB - 1:
                    mm.then_inc(srow_done, 1)

            pe.wait_ge(columns_ready, 2)
            for g in range(2):
                W(pe, "gdn_e2", g + 1)
                for n in range(4):
                    h = 4 * g + n
                    pe.matmul(unit_ps(g, n), U[:, 2 * h + 1, :], vb[:, 2 * h + 1, :], start=True, stop=False)
                    mm = pe.matmul(unit_ps(g, n), nw[:, h, :], bs1[:, h, :], start=False, stop=True)
                mm.then_inc(N["gdn_f3"], 1)
            pe.wait_ge(N["bst_landed"], 16)
            for b in range(2):
                on_state(b)
            for g in range(2):
                W(pe, "gdn_e3", g + 1)
                for n in range(4):
                    h = 4 * g + n
                    pe.matmul(unit_ps(4 + g, n), bs1[:, h, :], cv[:, h, P:T], start=True, stop=False)
                    pe.matmul(unit_ps(4 + g, n), uu[:, 2 * h + 1, :], QK[:, 2 * h + 1, :], start=False, stop=True)
                    mm = pe.matmul(unit_ps(6 + g, n), ktok[:, 2 * h + 1, :], uu[:, 2 * h + 1, :], start=True, stop=True)
                mm.then_inc(N["gdn_f4"], 1)
                if g == 0:
                    for b in range(2, 4):
                        on_state(b)
            pe.wait_ge(bst_landed1, 16)
            for b in range(4, NB):
                on_state(b)
            pe.wait_ge(rows_copied, 2)
            for g in range(4):
                mm = turn(ps[:, 2, 256 + 32 * g:288 + 32 * g], srow[:, g * P:(g + 1) * P])
            mm.then_inc(N["gdn_sbc"], 1)
            W(pe, "gdn_sval", 1)
            turn(ps[0:NB * HB, 2, 0:P], su[:, :, :].rearrange("p b h -> p (b h)")).then_inc(N["gdn_u"], 1)
            W(pe, "gdn_e4", 4)
            W(pe, "gdn_ub", 1)
            for g in range(16):
                if g >= 4:
                    W(pe, "gdn_surow", g - 3)
                for n in range(4):
                    mm = pe.matmul(ps[:, 3 + g % 4, n * P:(n + 1) * P],
                                   ident[0:64, 4 * g + n:4 * g + n + 1].broadcast_to([64, P]), urow[:, :],
                                   start=True, stop=True)
                mm.then_inc(N["gdn_uspread"], 1)
                if g == 3:
                    W(pe, "norm_sq", 2)
                    for t in range(HB):
                        if t >= 4:
                            W(pe, "norm_rb", GH + 1 + t - 3)
                        pe.matmul(ps[:, (0, 1, 2, 7)[t % 4], 0:TT], ones[:, :], nsq[:, t, :], start=True, stop=True)\
                          .then_inc(N["norm_sum"], 1)

            W(pe, "o_ready", 4)
            phase_pe(pe, PH["w_out"], ow_hi, ow_lo)
            sum_squares(2, TT)
            pe.wait_ge(acc_free, PH["x_q"].t0 + ACC_CREDIT)
            ph = PH["x_q"]
            with pe.Fori(0, ph.loops) as i:
                for u in range(4):
                    pe.wait_ge(m_taken, i * 4 + u + 1)
                    pe.wait_ge(m_squared, i * 4 + u + 1)
                    pe.wait_ge(mt_ready, i * 4 + u + 1)
                    for c in range(2):
                        mm = turn(ps[:, W4 + u % 2, c * P:(c + 1) * P], mt[u % 2][:, c, :])
                    mm.then_inc(N["m_turned"], 1)
                    products(pe, ph, i, u, act_hi, act_lo)
            pe.wait_ge(m_taken, KT + 2)
            sum_squares(3, NM)

            for name, b0 in (("mem_k", 0), ("mem_v", NB // 2)):
                ph = PH[name]
                with pe.Fori(0, ph.loops) as i:
                    for u in range(4):
                        products(pe, ph, i, u, ow_hi, ow_lo)
                        W(pe, "qc_split", i + b0 + 1)
                        W(pe, "s_dot", i * 4 + (4 * b0 + u + 1))
                        for d in range(4):
                            for m, part in enumerate((qc_lo, qc_hi)):
                                mm = pe.matmul(ps[:, 4 + u % 2, d * P:(d + 1) * P],
                                               part[:, 4 * u + d:4 * u + d + 1].broadcast_to([P, P]), ident_r[:, :],
                                               start=m == 0, stop=m == 1)
                        mm.then_inc(N["s_qb"], 1)
                        pe.wait_ge(acc_free, i * 4 + (ph.t0 + u + 1 + ACC_CREDIT))
                        W(pe, "kv_copied", i * 4 + (4 * b0 + u + 1))
                        for c in range(2):
                            mm = turn(ps[:, 6 + u % 2, c * P:(c + 1) * P], vt[u % 2][:, c * P:(c + 1) * P])
                        mm.then_inc(N["kv_turned"], 1)
            pe.wait_ge(acc_free, PH["x_o"].t0 + ACC_CREDIT)

            def scores(h):
                for c in range(NC):
                    for d in range(4):
                        mm = pe.matmul(ps[:, h, c * NM:(c + 1) * NM], q[:, 4 * h + d, c * P:(c + 1) * P],
                                       kT[:, 4 * h + d, :], start=d == 0, stop=d == 3)
                mm.then_inc(N["att_qk"], 1)

            def sample_values(b):
                for h in range(XH):
                    pe.wait_ge(v_mixed, XH * b + h + 1)
                    at = NB * XH - 1 - (NB * h + b)
                    mm = pe.matmul(ps[0:NB * XH, 5, :], window[:, at:at + NB * XH], vc[b % 2][:, 0, h * XD:(h + 1) * XD],
                                   start=b == 0 and h == 0, stop=b == NB - 1 and h == XH - 1)
                mm.then_inc(N["s_o"], 1)

            pe.wait_ge(s_kept, NB + 1)
            for m in range(2):
                mm = turn(ps[0:NB * XH, 4, m * P:(m + 1) * P], sc_s[:, m, :])
            mm.then_inc(N["s_st"], 1)
            pe.wait_ge(k_kept, KT + 2)
            scores(0)
            W(pe, "s_pn", 1)
            for m in range(2):
                mm = turn(ps[:, 4, NM + m * 32:NM + (m + 1) * 32], p_s[:, m * P:(m + 1) * P])
            mm.then_inc(N["s_ptt"], 1)
            scores(1)
            pe.wait_ge(columns_ready, 3)
            sample_values(0)
            scores(2)
            scores(3)
            sample_values(1)
            for h in range(XH):
                W(pe, "att_norm", h + 1)
                for m in range(2):
                    for c in range(NC):
                        mm = turn(ps[:, h, m * T + c * P:m * T + (c + 1) * P], pr[:, h, c * NM + m * P:c * NM + (m + 1) * P])
                mm.then_inc(N["att_pturned"], 1)
            W(pe, "kv_copied", 2 * KT + 2)
            for b in range(2, NB):
                for j in prompt_tiles(b):
                    W(pe, "att_pT", j // 4 + 1)
                    if j >= 2:
                        W(pe, "att_oe", j - 1)
                    for m in range(2):
                        mm = pe.matmul(ps[:, 6 + j % 2, 0:T], vm[:, m, j * P:(j + 1) * P],
                                       prT[:, j // 4, m * T:(m + 1) * T], start=m == 0, stop=m == 1)
                    mm.then_inc(N["att_o"], 1)
                sample_values(b)
            pe.wait_ge(rows_copied, 3)
            for d in range(4):
                mm = turn(ps[:, 4, d * 32:(d + 1) * 32], orow[:, d * P:(d + 1) * P])
            mm.then_inc(rows_turned, 1)

            W(pe, "s_oe", 1)
            phase_pe(pe, PH["x_o"], ow_hi, ow_lo)
            sum_squares(4, TT)
            for half in range(2):
                pe.wait_ge(acc_free, PH[f"gu{half}"].t0 + ACC_CREDIT)
                phase_pe(pe, PH[f"gu{half}"], act_hi, act_lo)
                pe.wait_ge(ff_split, HALF_K * (half + 1))
                phase_pe(pe, PH[f"dn{half}"], ff_hi, ff_lo)
            sum_squares(5, TT)
            for g in range(4):
                W(pe, "y_norm", g + 1)
                if g >= 2:
                    W(pe, "y_copied_act", g - 1)
                    W(pe, "y_copied_dve", g - 1)
                for c in range(NC):
                    for t in range(4):
                        turn(ps[:, 3 * (g % 2) + c, t * P:(t + 1) * P], yT[:, 4 * g + t, c * P:(c + 1) * P])
                for t in range(4):
                    mm = turn(ps[0:NB, 3 * (g % 2) + 2, t * P:(t + 1) * P], yT[:, 4 * g + t, T:TT])
                mm.then_inc(N["y_turned"], 1)

        MX, SUM, REC = 0, 1, 2
        SCALE = XD ** -0.5

        @block.scalar
        def _(act):
            def split(ph, i, u):
                split_hi(act, ph, i, u)

            def rms(k, width, n):
                act.wait_ge(sum_ready, k)
                act_link(act, act.activation(rstd[:, 0:width], ps[:, 7, 0:width], ACT.Ln, scale=1.0 / n,
                                             bias=consts[:, 0:1]))
                act.activation(rstd[:, 0:width], rstd[:, 0:width], ACT.Exp, scale=-0.5).then_inc(rstd_ready, 1)

            def none(ph, i, u):
                pass

            def gdn_take(ph, i, u):
                n = i * 4 + u
                act.wait_ge(conv_ready, 4 * n + 4)
                act.activation(tail[:, :, ds(n, 1)], pre[:, u % 2, T:T + 11].unsqueeze(2), ACT.Copy)
                act.activation(cv[:, ds(n, 1), :], cacc[:, u % 2, :], ACT.Silu).then_inc(conv_done, 1)

            def length_squares(i, u):
                W(act, "gdn_sum", i * 4 + u + 1)
                act.activation(sq[:, u % 2, :], cv[:, ds(i * 4 + u, 1), :], ACT.Square).then_inc(N["gdn_sq"], 1)

            def length_log(ph, i, u):
                W(act, "gdn_sum", i * 4 + u + 1 + 2)
                act.activation(rlen[:, ds(i * 4 + u, 1), :], ps[:, 4 + u % 2, 0:TT], ACT.Ln, bias=consts[:, 0:1])\
                   .then_inc(N["gdn_ln"], 1)

            def output_gate(t0):
                def f(ph, i, u):
                    act.wait_ge(acc_free, ph.t0 + 4 * i + u + 1 + ACC_CREDIT)
                    v = gla[:, ds(i * 4 + (16 + t0 + u), 1), :]
                    act.activation(v, v, ACT.Silu).then_inc(N["silu_g"], 1)
                return f

            def gate_take(ph, i, u):
                if u % 2 == 0:
                    act.wait_ge(acc_free, ph.t0 + 4 * i + u + 1 + ACC_CREDIT)
                    act.activation(g_s[:, u // 2, :], g_s[:, u // 2, :], ACT.Silu).then_inc(gate_act, 1)

            def memory_squares(i, u):
                W(act, "m_turned", i * 4 + u + 1 + 2)
                act.wait_ge(ssq_ready, i * 4 + (u + 2 * KT - 1))
                act.activation(sq[:, u % 2, 0:NM], ps[:, W4 + u % 2, 0:NM], ACT.Square).then_inc(m_squared, 1)

            def run(name, take, nxt, before=None):
                ph = PH[name]
                with act.Fori(0, ph.loops - 1) as i:
                    for u in range(4):
                        if before is not None:
                            before(i, u)
                        split(ph, i, u + 2) if u < 2 else split(ph, i + 1, u - 2)
                        take(ph, i, u)
                i = ph.loops - 1
                for u in range(4):
                    if before is not None:
                        before(i, u)
                    if u < 2:
                        split(ph, i, u + 2)
                    elif nxt is not None:
                        split(PH[nxt], 0, u - 2)
                    take(ph, i, u)

            act.wait_ge(dve_credit, 1)
            act.wait_ge(cols_turned, 1)
            split(PH["strip"], 0, 0)
            split(PH["gdn"], 0, 0)
            act.wait_ge(consts_ready, 1)
            rms(1, TT, D)
            split(PH["gdn"], 0, 1)
            run("gdn", gdn_take, "gla")
            run("gla", length_log, "r", length_squares)
            W(act, "gdn_ln", KT + 2)
            act.activation(rlen[:, :, :], rlen[:, :, :], ACT.Exp, scale=-0.5).then_inc(N["gdn_ln"], 1)
            run("r", output_gate(0), "z")
            run("z", output_gate(8), None)

            c1 = consts[:, 1:2]
            act.wait_ge(scalars_landed, 16 * 3)
            W(act, "scalars", 1)
            act.activation(sm(SP_), sm(TMP), ACT.Exp, scale=-1.0)
            act.activation(sm(EB), sm(DB), ACT.Exp, scale=-1.0)
            act.activation(sm(EAL)[:, :, 0], alog[:, :], ACT.Exp)
            act.wait_ge(N["turned"], 1)
            for g, rows in enumerate((3 * CT, 4 * CT, 4 * CT)):
                act.activation(tails[0:rows, g, :], ps[0:rows, 1, g * P:(g + 1) * P], ACT.Copy).then_inc(N["tails_copied"], 1)
            W(act, "gla_dec", 1)
            act_link(act, act.activation(gaz[:, :, :], gaz[:, :, :], ACT.Exp, scale=-1.0))
            act.activation(sm(SP_), sm(SP_), ACT.Ln, bias=c1).then_inc(N["scalars"], 1)
            act.activation(gaz[:, :, :], gaz[:, :, :], ACT.Ln, bias=c1).then_inc(N["gla_exp"], 1)
            W(act, "gdn_scal", 1)
            act.activation(sm(EG1), sm(GC), ACT.Exp)
            act.activation(sm(KD), sm(GD), ACT.Exp)
            act.activation(sm(EGL), sm(GL), ACT.Exp).then_inc(N["gdn_scal"], 1)
            W(act, "gla_la", 1)
            act.activation(ges[:, :, :], gz[:, :, T:TT], ACT.Exp).then_inc(N["gla_bgate"], 1)
            for l in range(1, LEVELS):
                W(act, "gla_dec", l + 1)
                act.activation(gE[l % 2][:, :, :], gE[l % 2][:, :, :], ACT.Exp).then_inc(N["gla_exp"], 1)
                if l == 2:
                    W(act, "gla_turned", 1)
                    W(act, "gla_bgate", 1)
                    for c in range(NC):
                        for m in range(2):
                            act.activation(gvt[:, c, m * 512:(m + 1) * 512], ps[:, 4 + 2 * c + m, :], ACT.Copy)\
                               .then_inc(N["gla_tok"], 1)
            W(act, "gla_eexp", 1)
            act.activation(gE[0][:, :, :], gE[0][:, :, :], ACT.Exp)
            act.activation(gE[1][:, :, 0:P], gb[:, :, P:T], ACT.Exp)
            act.activation(gel[:, :, :], gb[:, :, T - 1:T], ACT.Exp).then_inc(N["gla_exp"], 1)
            W(act, "gla_turned", 2)
            for m in range(2):
                act.activation(gkdt[:, 4 * m:4 * m + 4, :], heads_of(m), ACT.Copy).then_inc(N["gla_tok"], 1)
            for m in range(2):
                act.activation(gvrow[:, m * 512:(m + 1) * 512], ps[0:NB, 2 + m, :], ACT.Copy).then_inc(N["gla_tok"], 1)
            W(act, "gla_mm", 1)
            act.wait_ge(tails_out, 16 * (1 + NB))
            for m in range(2):
                ins = act.activation(gs1[:, 2 * m:2 * m + 2, :], ps[:, m, :].rearrange("p (h v) -> p h v", h=2), ACT.Copy)
            ins.then_inc(N["gla_s"], 1)
            for b in range(NB):
                W(act, "gla_smm", b + 1)
                for h in range(GH):
                    ins = act.activation(gst[:, b, h, :], gst[:, b, h, :], ACT.Copy, scale=ges[:, h, b:b + 1])
                ins.then_inc(N["gla_sc"], 1)
                if b == 0:
                    W(act, "gla_smm", NB)
                    act.activation(grow[:, :], ps[0:GH * NB, 5, 0:GDV], ACT.Copy).then_inc(rows_copied, 1)
            W(act, "gla_bc", NB)
            act.wait_ge(gla_done, 1)
            act.activation(nsq, gla[:, 0:8, :], ACT.Square).then_inc(N["norm_sq"], 1)
            for g in range(4):
                W(act, "gdn_turned", g + 1)
                act.activation(ktok[:, 4 * g:4 * g + 4, :], heads_of(4 * (g % 2)), ACT.Copy).then_inc(N["gdn_ktok"], 1)
            for t in range(GH):
                W(act, "norm_sum", t + 1)
                act.activation(nsq[:, t, :], ps[:, (2, 3, 6, 7)[t], 0:TT], ACT.Ln, bias=consts[:, 0:1], scale=1.0 / GDV)\
                   .then_inc(N["norm_rb"], 1)
            for g in range(4):
                W(act, "gdn_dmin", g + 1)
                W(act, "gdn_pair", g + 1)
                act.activation(EG[:, 2 * g:2 * g + 2, :],
                               ps[:, 4 * (g % 2), :].rearrange("p (h c t) -> p h c t", h=2, c=2)[:, :, 1, :], ACT.Exp)
                act.activation(QK[:, 4 * g:4 * g + 4, :], QK[:, 4 * g:4 * g + 4, :], ACT.Exp).then_inc(N["gdn_dexp"], 1)
            W(act, "norm_rb", GH)
            act.activation(nsq[:, 0:GH, :], nsq[:, 0:GH, :], ACT.Exp, scale=-0.5).then_inc(N["norm_rb"], 1)
            for l in range(2, LEVELS):
                for g in range(4):
                    W(act, "y_done", 4 * (l - 2) + g + 1)
                    if l == 2:
                        act.wait_ge(N["state_out"], 32)
                    act.activation(Y[:, 4 * g:4 * g + 4, :], heads_of(g), ACT.Copy).then_inc(N["y_copied"], 1)
            act.wait_ge(N["state_out"], 32)
            for g in range(2):
                W(act, "gdn_f1", g + 1)
                act.activation(nw[:, 4 * g:4 * g + 4, :], heads_of(g), ACT.Copy, scale=-1.0)
                act.activation(uu[:, 8 * g:8 * g + 8:2, :], heads_of(2 + g), ACT.Copy).then_inc(N["gdn_e1"], 1)
            for g in range(2):
                W(act, "gdn_f2", g + 1)
                act.activation(bs1[:, 4 * g:4 * g + 4, :], heads_of(4 + g), ACT.Copy)
                act.activation(cv[:, 4 * g:4 * g + 4, 0:P], heads_of(6 + g), ACT.Copy).then_inc(N["gdn_e2"], 1)
            for g in range(2):
                W(act, "gdn_f3", g + 1)
                act.activation(uu[:, 8 * g + 1:8 * g + 8:2, :], heads_of(g), ACT.Copy).then_inc(N["gdn_e3"], 1)
            act.wait_ge(srow_done, 1)
            act.activation(srow[:, :], ps[0:32, 3, :], ACT.Copy).then_inc(rows_copied, 1)
            W(act, "gdn_u", 1)
            act.activation(urow[:, :], ps[0:NB * HB, 2, 0:P], ACT.Copy).then_inc(N["gdn_ub"], 1)
            act.wait_ge(gla_gated, 4)
            W(act, "gdn_e4", 4)
            W(act, "gdn_sval", 1)
            act.activation(nsq, cv[:, 0:8, :], ACT.Square).then_inc(N["norm_sq"], 1)
            for t in range(HB):
                W(act, "norm_sum", GH + t + 1)
                act.activation(nsq[:, t, :], ps[:, (0, 1, 2, 7)[t % 4], 0:TT], ACT.Ln, bias=consts[:, 0:1], scale=1.0 / P)\
                   .then_inc(N["norm_rb"], 1)
            W(act, "norm_rb", GH + 1 + HB)
            act.activation(nsq, nsq, ACT.Exp, scale=-0.5).then_inc(N["norm_rb"], 1)
            act.wait_ge(o_gated, 1)
            for c in range(4):
                if c == 2:
                    W(act, "gdn_surow", 16)
                act.activation(ow_hi[:, 4 * c:4 * c + 4, :], gla[:, 16 + 4 * c:20 + 4 * c, :], ACT.Copy).then_inc(o_hi, 1)

            W(act, "o_ready", 4)
            act.wait_ge(N["state_out"], 16 * (3 + NB // 2))
            split(PH["w_out"], 0, 0)
            split(PH["w_out"], 0, 1)
            run("w_out", none, "x_q")
            rms(2, TT, D)
            run("x_q", none, "mem_k", memory_squares)
            act.wait_ge(acc_free, PH["mem_k"].t0 + ACC_CREDIT)
            rms(3, NM, D)
            act.activation(ident_r[:, :], ident[:, :], ACT.Copy)

            def sample_queries(b0):
                def f(i, u):
                    if u == 0:
                        act.wait_ge(s_kept, i + b0 + 1)
                        act.activation(qc_hi[:, :].unsqueeze(2), q[:, :, ds(i + (T + b0), 1)], ACT.Copy).then_inc(qc_ready, 1)
                return f

            def rows(b0):
                def f(ph, i, u):
                    W(act, "kv_turned", i * 4 + (4 * b0 + u + 1 + 2))
                    if b0:
                        W(act, "k_out", 16 * (XH - 1))
                        if isinstance(i, int):
                            W(act, "k_out3", 16)
                    act.activation(vm[:, :, ds(i * 4 * P + u * P, P)],
                                   ps[:, 6 + u % 2, 0:2 * P].rearrange("p (c d) -> p c d", c=2), ACT.Copy)\
                       .then_inc(N["kv_copied"], 1)
                return f

            run("mem_k", rows(0), "mem_v", sample_queries(0))
            run("mem_v", rows(NB // 2), "x_o", sample_queries(NB // 2))

            def exponentials(h):
                W(act, "att_max", h + 1)
                for c in range(NC):
                    ins = act.activation(pr[:, h, c * NM:(c + 1) * NM], ps[:, h, c * NM:(c + 1) * NM], ACT.Exp, scale=SCALE,
                                         bias=small[:, MX, 2 * h + c:2 * h + c + 1],
                                         accum_out=small[:, SUM, 2 * h + c:2 * h + c + 1])
                ins.then_inc(N["att_exp"], 1)

            def first_values(b):
                act.wait_ge(vc_landed[b % 2], 16 * (b // 2 + 1))
                W(act, "s_pT", 1)
                for h in range(XH):
                    v = vc[b % 2][:, 0, h * XD:(h + 1) * XD]
                    act.activation(v, v, ACT.Copy, scale=pT_s[:, 0, b * XH + h:b * XH + h + 1]).then_inc(v_first, 1)

            W(act, "s_sm", 1)
            act.activation(p_s, ps[0:32, 4, 0:NM], ACT.Exp, scale=SCALE, bias=small[0:32, MX, 12:13],
                           accum_out=small[0:32, SUM, 12:13]).then_inc(N["s_exp"], 1)
            exponentials(0)
            first_values(0)
            exponentials(1)
            first_values(1)
            exponentials(2)
            exponentials(3)
            for h in range(XH):
                W(act, "att_pturned", h + 1)
                act.activation(prT[:, h, 0:2 * T], ps[:, h, :], ACT.Copy).then_inc(N["att_pT"], 1)
            for b in range(2, NB):
                first_values(b)
            W(act, "s_o", NB)
            act.activation(orow[:, :], ps[0:NB * XH, 5, :], ACT.Copy).then_inc(rows_copied, 1)

            run("x_o", none, "gu0")
            rms(4, TT, D)
            run("gu0", gate_take, "dn0")
            run("dn0", none, "gu1")
            run("gu1", gate_take, "dn1")
            run("dn1", none, None)
            rms(5, TT, D)
            for g in range(4):
                W(act, "y_turned", g + 1)
                act.activation(ysrow[:, g * 512:(g + 1) * 512], ps[0:NB, 3 * (g % 2) + 2, :], ACT.Copy)
                act.activation(yrows[:, 1, g * 512:(g + 1) * 512], ps[:, 3 * (g % 2) + 1, :], ACT.Copy)\
                   .then_inc(N["y_copied_act"], 1)

        @block.vector
        def _(dve):
            scaled, gdn, residual, gate_up, down = dve_take(dve)

            def link(ins):
                dve_link(dve, ins)

            def split(ph, i, u):
                split_lo(dve, ph, i, u)

            def run(name, take, nxt):
                ph = PH[name]
                with dve.Fori(0, ph.loops - 1) as i:
                    for u in range(4):
                        take(ph, i, u)
                        split(ph, i, u + 2) if u < 2 else split(ph, i + 1, u - 2)
                i = ph.loops - 1
                for u in range(4):
                    take(ph, i, u)
                    if u < 2:
                        split(ph, i, u + 2)
                    elif nxt is not None:
                        split(PH[nxt], 0, u - 2)

            def halves_of(k, src, gain, hi, lo, done):
                w = src.shape[-1]
                g = cols[:, gain + k:gain + k + 1]
                link(dve.tensor_scalar(hi[:, k, 0:w], src, g, None, ALU.mult))
                dve.scalar_tensor_tensor(out=lo[:, k, 0:w], in0=src, scalar=g, in1=hi[:, k, 0:w], op0=ALU.mult,
                                         op1=ALU.subtract).then_inc(done, 1)

            dve.memset(strip[:, 0:1], 0.0).then_inc(units_done, UNIT_CREDIT)
            dve.memset(strip[:, 1:2], 0.0).then_inc(lo_split, LO_CREDIT)
            dve.memset(strip[:, 2:3], 0.0).then_inc(acc_free, ACC_CREDIT)
            dve.memset(strip[:, 3:4], 0.0).then_inc(conv_done, 2)
            dve.memset(strip[:, 4:5], 0.0).then_inc(m_taken, 2)
            dve.memset(strip[:, 10:11], 0.0).then_inc(m_squared, 2)
            dve.memset(strip[:, 11:12], 0.0).then_inc(s_kept, 1)
            dve.memset(strip[:, 12:13], 0.0).then_inc(N["gdn_sum"], 2)
            dve.memset(strip[:, 13:14], 0.0).then_inc(N["gdn_ln"], 2)
            dve.memset(strip[:, 7:8], 0.0).then_inc(N["m_turned"], 2)
            dve.memset(strip[:, 8:9], 0.0).then_inc(N["kv_turned"], 2)
            dve.memset(strip[:, 9:10], 0.0).then_inc(k_kept, 2)
            dve.memset(strip[:, 5:6], 0.0).then_inc(N["s_dot"], 2)
            dve.memset(strip[:, 6:7], 0.0).then_inc(N["kv_copied"], 2)
            dve.memset(small[:, :, :], 0.0).then_inc(dve_credit, 1)
            dve.wait_ge(cols_turned, 1)
            dve.tensor_copy(cols[:, :], ps[:, 4, 0:87]).then_inc(cols_ready, 1)
            dve.tensor_copy(convw[:, :], ps[:, 4, P:P + CW * CT]).then_inc(cols_ready, 1)
            for m in range(2):
                ins = dve.tensor_copy(cst[:, 12 * m:12 * m + 12, :].rearrange("p t (j b) -> p t b j", j=3),
                                      ps[:, 5 + m, 0:288].rearrange("p (t b j) -> p t b j", t=12, j=3))
            ins.then_inc(cols_ready, 1)
            dve.wait_ge(cols_ready, 3)
            for k in range(KT):
                dve.wait_ge(x_turned, k + 1)
                src = ps[:, W4 + k % 4, 0:TT]
                dve.tensor_copy(x[:, k, :], src).then_inc(x_ready, 1)
                halves_of(k, src, GAIN_MIX, act_hi, act_lo, x_taken)
            split(PH["strip"], 0, 0)
            split(PH["gdn"], 0, 0)
            dve.wait_ge(rstd_ready, 1)
            dve.wait_ge(consts_ready, 1)
            tile_wait(dve, PH["strip"], 0, 0)
            dve.tensor_tensor(strip[:, :], ps[:, 0, 0:TT], rstd[:, :], ALU.mult).then_inc(acc_free, 1)
            split(PH["gdn"], 0, 1)
            run("gdn", gdn, "gla")
            run("gla", scaled(gla, rstd[:, :]), "r")
            run("r", scaled(gla[:, 16:24, :], rstd[:, :]), "z")

            def lengths(t):
                v = cv[:, 4 * t:4 * t + 4, :]
                dve.scalar_tensor_tensor(out=v, in0=v, scalar=P ** -0.5 if t < 2 else 1.0, in1=rlen[:, 4 * t:4 * t + 4, :],
                                         op0=ALU.mult, op1=ALU.mult).then_inc(N["gdn_normed"], 1)

            W(dve, "gdn_ln", KT + 2 + 1)
            lengths(0)
            lengths(1)
            run("z", scaled(gla[:, 24:32, :], rstd[:, :]), None)
            lengths(2)
            lengths(3)

            def b3(v, n):
                return v.unsqueeze(1).broadcast_to([P, n, P])

            W(dve, "turned", 1)
            for dst, c0 in ((DA, 112), (DB, 120)):
                dve.tensor_copy(sm(dst)[:, :, 0:2], ps[:, 0, 0:256].rearrange("p (c h) -> p h c", h=P)[:, c0:c0 + HB, :])
                ins = dve.tensor_copy(sm(dst)[0:NB, :, 2], ps[0:NB, 0, 2 * P + c0:2 * P + c0 + HB])
            link(ins)
            dve.wait_ge(scalars_landed, 16 * 3)
            link(dve.tensor_tensor(sm(DA), sm(DA), dtb[:, :].unsqueeze(2).broadcast_to([P, HB, 3]), ALU.add))
            dve.scalar_tensor_tensor(out=sm(TMP), in0=sm(DA), scalar=-1.0, in1=sm(DA), op0=ALU.mult, op1=ALU.max)\
               .then_inc(N["scalars"], 1)
            W(dve, "gla_pre", 1)
            for h in range(GH):
                ins = dve.tensor_scalar(gz[:, h, :], ps[:, 4 + h, 0:TT], cols[:, GAIN_GATE_B + h:GAIN_GATE_B + h + 1], None,
                                        ALU.add)
            link(ins)
            dve.scalar_tensor_tensor(out=gaz[:, :, :], in0=gz[:, :, :], scalar=-1.0, in1=gz[:, :, :], op0=ALU.mult,
                                     op1=ALU.max).then_inc(N["gla_dec"], 1)
            W(dve, "scalars", 2)
            link(dve.scalar_tensor_tensor(out=sm(TMP), in0=sm(DA), scalar=0.0, in1=sm(SP_), op0=ALU.max, op1=ALU.add))
            link(dve.scalar_tensor_tensor(out=sm(G_), in0=sm(TMP), scalar=-1.0,
                                          in1=sm(EAL)[:, :, 0:1].broadcast_to([P, HB, 3]), op0=ALU.mult, op1=ALU.mult))
            link(dve.tensor_scalar(sm(EB), sm(EB), 1.0, None, ALU.add))
            dve.reciprocal(sm(BETA), sm(EB)).then_inc(N["gdn_g"], 1)
            W(dve, "gdn_gcol", 1)
            dve.tensor_copy(sm(GC)[:, :, 2], sm(G_)[:, :, 2])
            dve.tensor_copy(sm(GL)[:, :, 2], sm(G_)[:, :, 2])
            dve.tensor_copy(sm(GC)[:, :, 0:2], ps[:, 2, 0:16].rearrange("p (c h) -> p h c", c=2))
            link(dve.tensor_copy(sm(GL)[:, :, 0:2], ps[:, 2, 16:32].rearrange("p (c h) -> p h c", c=2)))
            dve.tensor_tensor(sm(GD), sm(GL), sm(GC), ALU.subtract).then_inc(N["gdn_scal"], 1)
            W(dve, "gla_exp", 1)
            link(dve.scalar_tensor_tensor(out=gz[:, :, :], in0=gz[:, :, :], scalar=0.0, in1=gaz[:, :, :], op0=ALU.min,
                                          op1=ALU.subtract))
            link(dve.tensor_scalar(gz[:, :, :], gz[:, :, :], 1.0 / 16.0, None, ALU.mult))
            link(dve.tensor_scalar(gla[:, 0:GH, :], gla[:, 0:GH, :], GDK ** -0.5, None, ALU.mult))
            for h in range(GH):
                for c in range(NC):
                    tok = slice(c * P, (c + 1) * P)
                    ins = dve.tensor_tensor_scan(gb[:, h, tok], ones[:, :], gz[:, h, tok], 0.0, ALU.mult, ALU.add)
            ins.then_inc(N["gla_la"], 1)
            W(dve, "gla_la", 1)
            W(dve, "prep", 1)
            W(dve, "gdn_scal", 2)
            dve.tensor_tensor(sm(BG), sm(EG1), sm(BETA), ALU.mult)

            def differences(l):
                m = 1 << (l - 1)
                nb = T // (2 * m)
                v = gb[:, :, :].rearrange("p h (n s m) -> p (h n) s m", s=2, m=m)
                e = gE[l % 2][:, :, :].rearrange("p h (n s m) -> p (h n) s m", s=2, m=m)
                if l >= 3:
                    W(dve, "gla_lvl", l - 2)
                mid = v[:, :, 0, m - 1:m].broadcast_to([P, GH * nb, m])
                dve.tensor_tensor(e[:, :, 1, :], v[:, :, 1, :], mid, ALU.subtract)
                dve.tensor_tensor(e[:, :, 0, :], mid, v[:, :, 0, :], ALU.subtract).then_inc(N["gla_dec"], 1)

            def pick(l):
                W(dve, "gla_scored", l + 1)
                if l:
                    W(dve, "gla_picked", l)
                for m in range(2):
                    v = gsc[:, 4 * m:4 * m + 4, :]
                    mask = b3(levels[:, l, :], 4)
                    if l == 0:
                        ins = dve.tensor_tensor(v, heads_of(m), mask, ALU.mult)
                    else:
                        ins = dve.copy_predicated(v, mask.bitcast(U32), heads_of(2 * (l % 2) + m))
                ins.then_inc(N["gla_picked"], 1)

            differences(1)
            for l in range(1, LEVELS):
                if l + 1 < LEVELS:
                    differences(l + 1)
                m = 1 << (l - 1)
                W(dve, "gla_exp", l + 1)
                if l >= 3:
                    W(dve, "gla_scored", l - 1)
                e = halves(gE[l % 2][:, :, :], m)
                dve.tensor_tensor(halves(gq[l % 2][:, :, :], m)[:, :, :, 1, :], halves(gla[:, 0:GH, 0:T], m)[:, :, :, 1, :],
                                  e[:, :, :, 1, :], ALU.mult)
                dve.tensor_tensor(halves(gk[l % 2][:, :, :], m)[:, :, :, 0, :],
                                  halves(gla[:, GH:2 * GH, 0:T], m)[:, :, :, 0, :],
                                  e[:, :, :, 0, :], ALU.mult).then_inc(N["gla_lvl"], 1)
                pick(l - 1)
            W(dve, "gla_lvl", LEVELS - 2)
            gv = gb[:, :, :].rearrange("p h (c s) -> p (h c) s", s=P)
            dve.tensor_tensor(gE[0][:, :, :].rearrange("p h (c s) -> p (h c) s", s=P),
                              gv[:, :, P - 1:P].broadcast_to([P, GH * NC, P]), gv, ALU.subtract).then_inc(N["gla_eexp"], 1)
            pick(LEVELS - 1)
            W(dve, "gla_exp", LEVELS + 1)
            dve.tensor_tensor(gkd[:, :, :], gla[:, GH:2 * GH, 0:T], gE[0][:, :, :], ALU.mult)
            dve.tensor_tensor(gqd[:, :, :], gla[:, 0:GH, P:T], gE[1][:, :, 0:P], ALU.mult).then_inc(N["gla_dec"], 1)
            W(dve, "gla_bgate", 1)
            dve.wait_ge(columns_ready, 1)
            on_diagonal = gqe[:, :, :].rearrange("p n m -> p (n m)")[:, 0::GH * NB + 1].rearrange("p (h b) -> p h b", h=GH)
            dve.tensor_tensor(on_diagonal, gla[:, 0:GH, T:TT], ges[:, :, :], ALU.mult)
            dve.tensor_tensor(gkq[:, :, :], gla[:, 0:GH, T:TT], gla[:, GH:2 * GH, T:TT], ALU.mult)
            dve.tensor_copy(gks[:, :, :], gla[:, GH:2 * GH, T:TT]).then_inc(N["gla_qe"], 1)
            W(dve, "gla_mm", 1)
            for m in range(2):
                ins = dve.tensor_copy(gla[:, 4 * m:4 * m + 4, 0:P], heads_of(4 + m))
            ins.then_inc(N["gla_out"], 1)
            W(dve, "gla_mm", 2)
            for m in range(2):
                ins = dve.tensor_copy(gla[:, 4 * m:4 * m + 4, P:T], heads_of(6 + m))
            ins.then_inc(N["gla_out"], 1)
            W(dve, "gla_s", 1)
            for h in range(GH):
                ins = dve.scalar_tensor_tensor(out=gsf[:, h, :], in0=gs1[:, h, :], scalar=gel[:, h, :],
                                               in1=ps[:, h // 2, (h % 2) * GDV:(h % 2 + 1) * GDV], op0=ALU.mult, op1=ALU.add)
            ins.then_inc(N["gla_out"], 1)
            for b in range(NB):
                W(dve, "gla_bc", b + 1)
                W(dve, "gla_sc", b + 1)
                bank = (0, 2, 6)[b % 3]
                for h in range(GH):
                    ins = dve.scalar_tensor_tensor(out=gst[:, b, h, :],
                                                   in0=ps[:, bank + h // 2, (h % 2) * GDV:(h % 2 + 1) * GDV],
                                                   scalar=gks[:, h, b:b + 1], in1=gst[:, b, h, :], op0=ALU.mult, op1=ALU.add)
                ins.then_inc(N["gla_srow"], 1)
            W(dve, "gla_turned", 3)
            W(dve, "gla_qe", 1)
            link(dve.tensor_tensor(got[:, :, :].rearrange("p (h e) b -> p h e b", e=2),
                                   gla[:, 8:16, T:TT].rearrange("p (h e) b -> p h e b", e=2),
                                   ps[:, 4, 0:32].rearrange("p (h b) -> p h b", h=GH).unsqueeze(2).broadcast_to([P, GH, 2, NB]),
                                   ALU.mult))
            dve.tensor_tensor(gla[:, 0:8, T:TT].rearrange("p (h e) b -> p h e b", e=2),
                              got[:, :, :].rearrange("p (h e) b -> p h e b", e=2),
                              ps[:, 5, 256:320].rearrange("p (e h b) -> p h e b", e=2, h=GH), ALU.add)\
               .then_inc(gla_done, 1)

            def of_units(k, g):
                return sm(k)[:, 2 * g:2 * g + 2, 0:2].unsqueeze(3).broadcast_to([P, 2, 2, P])

            def four(v):
                return v.rearrange("p (h c) d -> p h c d", c=2)

            for g in range(4):
                W(dve, "gdn_turned", g + 1)
                dve.tensor_tensor(four(vb[:, 4 * g:4 * g + 4, :]), four(heads_of(4 * (g % 2) + 1)), of_units(BETA, g), ALU.mult)\
                   .then_inc(N["gdn_vb"], 1)

            def decays(g):
                W(dve, "gdn_pair", g + 1)
                for n in range(4):
                    ins = dve.tensor_scalar(QK[:, 4 * g + n, :], ps[:, 4 * (g % 2), n * P:(n + 1) * P],
                                            sm(GC)[:, 2 * g + n // 2, n % 2:n % 2 + 1], 0.0, ALU.subtract, ALU.min)
                ins.then_inc(N["gdn_dmin"], 1)

            for g in range(4):
                decays(g)
                W(dve, "gdn_dexp", g + 1)
                b0 = 4 * (g % 2)
                lt, qk = Lt[:, 4 * g:4 * g + 4, :], QK[:, 4 * g:4 * g + 4, :]
                if g == 0:
                    dve.wait_ge(N["state_out"], 32)
                link(dve.tensor_tensor(lt, qk, heads_of(b0 + 1), ALU.mult))
                dve.tensor_tensor(lt, lt, heads_of(b0 + 2), ALU.mult)
                dve.tensor_tensor(qk, qk, heads_of(b0 + 3), ALU.mult).then_inc(N["gdn_lt"], 1)
            dve.tensor_tensor(cv[:, 0:HB, P:T], cv[:, 0:HB, P:T], EG[:, :, :], ALU.mult)
            W(dve, "gdn_ktok", 4)
            kt4 = four(ktok[:, :, :])
            link(dve.tensor_tensor(kbg[:, :, :], kt4[:, :, 1, :], sm(BG)[:, :, 1:2].broadcast_to([P, HB, P]), ALU.mult))
            dve.tensor_tensor(kt4, kt4, sm(KD)[:, :, 0:2].unsqueeze(3).broadcast_to([P, HB, 2, P]), ALU.mult)\
               .then_inc(N["gdn_kbg"], 1)
            i8 = ident[0:NB, 0:NB].unsqueeze(2).broadcast_to([NB, NB, HB])

            def on_samples(v):
                return v.rearrange("p h b -> p b h")

            for m, k in ((0, EG1), (1, BETA)):
                dve.tensor_tensor(sdiag[:, m, :, :], i8, sm(k)[0:NB, :, 2].unsqueeze(1).broadcast_to([NB, NB, HB]), ALU.mult)
            dve.tensor_tensor(skq[:, :, :], on_samples(cv[:, 0:8, T:TT]), on_samples(cv[:, 8:16, T:TT]), ALU.mult)\
               .then_inc(N["gdn_sx"], 1)

            def gla_gate(p):
                for j in (2 * p, 2 * p + 1):
                    ins = dve.scalar_tensor_tensor(out=gla[:, j, :], in0=gla[:, j, :],
                                                   scalar=cols[:, GAIN_GLA + j % 2:GAIN_GLA + j % 2 + 1], in1=nsq[:, p, :],
                                                   op0=ALU.mult, op1=ALU.mult)
                link(ins)
                v = gla[:, 16 + 2 * p:18 + 2 * p, :]
                dve.tensor_tensor(v, v, gla[:, 2 * p:2 * p + 2, :], ALU.mult).then_inc(gla_gated, 1)

            for g in range(4):
                W(dve, "gdn_bt", g + 1)
                W(dve, "gdn_t0", g + 1)
                dve.tensor_tensor(U[:, 4 * g:4 * g + 4, :], b3(ident[:, :], 4), Bt[:, 4 * g:4 * g + 4, :], ALU.subtract)
                dve.tensor_tensor(Tm[:, 4 * g:4 * g + 4, :], b3(ident[:, :], 4), heads_of(g), ALU.subtract)\
                   .then_inc(N["inv_ready"], 1)
            for l in range(2, LEVELS):
                for g in range(4):
                    W(dve, "tyuy_done", 4 * (l - 2) + g + 1)
                    W(dve, "inv_ready", 4 * (l - 2) + g + 1)
                    b0 = 4 + 2 * (g % 2)
                    if l < LEVELS - 1:
                        tm = Tm[:, 4 * g:4 * g + 4, :]
                        dve.tensor_tensor(tm, tm, heads_of(b0), ALU.subtract)
                    um = U[:, 4 * g:4 * g + 4, :]
                    dve.tensor_tensor(um, um, heads_of(b0 + 1), ALU.subtract).then_inc(N["inv_ready"], 1)
                if l < 2 + GH:
                    W(dve, "norm_rb", GH + 1)
                    W(dve, "silu_g", 16)
                    gla_gate(l - 2)
            for g in range(2):
                W(dve, "gdn_f4", g + 1)
                dve.tensor_copy(cv[:, 4 * g:4 * g + 4, P:T], heads_of(4 + g)).then_inc(N["gdn_e4"], 1)
                link(dve.tensor_tensor(bsf[:, 4 * g:4 * g + 4, :], bs1[:, 4 * g:4 * g + 4, :],
                                       sm(EGL)[:, 4 * g:4 * g + 4, 1:2].broadcast_to([P, 4, P]), ALU.mult))
                dve.tensor_tensor(bsf[:, 4 * g:4 * g + 4, :], bsf[:, 4 * g:4 * g + 4, :], heads_of(6 + g), ALU.add)\
                   .then_inc(N["gdn_e4"], 1)

            W(dve, "gdn_sbc", 1)
            link(dve.tensor_copy(sbc[:, :, :], ps[:, 2, 0:128].rearrange("p (m n) -> p m n", m=2)))
            prod = ps[:, 2, 256:384].rearrange("p (n s) -> p s n", s=2)
            flat = [v[:, :, :].rearrange("p b h -> p (b h)") for v in (su, so, skq2)]
            link(dve.tensor_tensor(flat[0], prod[:, 1, :], sbc[:, 0, :], ALU.mult))
            link(dve.tensor_tensor(su[:, :, :], on_samples(cv[:, 16:24, T:TT]), su[:, :, :], ALU.subtract))
            link(dve.tensor_tensor(flat[0], flat[0], sbc[:, 1, :], ALU.mult))
            link(dve.tensor_tensor(flat[1], prod[:, 0, :], sbc[:, 0, :], ALU.mult))
            link(dve.tensor_tensor(flat[2], flat[0], ps[:, 2, 128:192], ALU.mult))
            dve.tensor_tensor(on_samples(cv[:, 0:8, T:TT]), so[:, :, :], skq2[:, :, :], ALU.add).then_inc(N["gdn_sval"], 1)
            def new_states(g):
                W(dve, "gdn_uspread", g + 1)
                W(dve, "gdn_ubt", g // 2 + 1)
                for n in range(4):
                    b, h = (4 * g + n) // HB, (4 * g + n) % HB
                    ins = dve.scalar_tensor_tensor(out=bst[:, b, h, :], in0=ps[:, 3 + g % 4, n * P:(n + 1) * P],
                                                   scalar=cv[:, 8 + h, T + b:T + b + 1], in1=bst[:, b, h, :],
                                                   op0=ALU.mult, op1=ALU.add)
                ins.then_inc(N["gdn_surow"], 1)

            for g in range(8):
                new_states(g)
            W(dve, "norm_rb", GH + 1 + HB + 1)
            for j in range(HB):
                ins = dve.scalar_tensor_tensor(out=cv[:, j, :], in0=cv[:, j, :], scalar=cols[:, GAIN_GDN:GAIN_GDN + 1],
                                               in1=nsq[:, j, :], op0=ALU.mult, op1=ALU.mult)
            link(ins)
            dve.tensor_tensor(gla[:, 24:32, :], gla[:, 24:32, :], cv[:, 0:8, :], ALU.mult).then_inc(o_gated, 1)
            for g in range(8, 16):
                new_states(g)
            for c in range(4):
                dve.wait_ge(o_hi, c + 1)
                dve.tensor_tensor(ow_lo[:, 4 * c:4 * c + 4, :], gla[:, 16 + 4 * c:20 + 4 * c, :], ow_hi[:, 4 * c:4 * c + 4, :],
                                  ALU.subtract).then_inc(N["o_ready"], 1)

            split(PH["w_out"], 0, 0)
            split(PH["w_out"], 0, 1)
            dve.wait_ge(x_ready, KT)
            run("w_out", lambda ph, i, u: residual(ph, i, u, 0, GAIN_X), "x_q")
            dve.wait_ge(rstd_ready, 2)
            queries = scaled(q, rstd[:, :])

            def query_and_memory(ph, i, u):
                n = i * 4 + u
                W(dve, "m_turned", n + 1 + 2)
                dve.wait_ge(m_squared, n + 1 + 2)
                src = ps[:, W4 + u % 2, 0:NM]
                g = cols[:, ds(n + GAIN_MEM, 1)]
                dve.tensor_scalar(ow_hi[:, ds(n, 1), 0:NM], src, g, None, ALU.mult).then_inc(N["m_ready"], 1)
                W(dve, "m_ready", n + 1)
                dve.scalar_tensor_tensor(out=ow_lo[:, ds(n, 1), 0:NM], in0=src, scalar=g, in1=ow_hi[:, ds(n, 1), 0:NM],
                                         op0=ALU.mult, op1=ALU.subtract).then_inc(m_taken, 1)
                queries(ph, i, u)

            run("x_q", query_and_memory, "mem_k")

            def memory_and_scores(b0):
                def f(ph, i, u):
                    if u == 0:
                        dve.wait_ge(qc_ready, i + b0 + 1)
                        dve.tensor_tensor(qc_lo[:, :].unsqueeze(2), q[:, :, ds(i + (T + b0), 1)], qc_hi[:, :].unsqueeze(2),
                                          ALU.subtract).then_inc(N["qc_split"], 1)
                    tile_wait(dve, ph, i, u)
                    W(dve, "kv_turned", i * 4 + (4 * b0 + u + 1))
                    dve.wait_ge(k_kept, KT + 2 if b0 else i * 4 + u + 1)
                    dve.tensor_tensor(vt[u % 2], out_of(ph, u), rstd[:, 0:NM], ALU.mult).then_inc(acc_free, 1)
                    W(dve, "s_qb", i * 4 + (4 * b0 + u + 1))
                    dve.wait_ge(kc_landed[u], i * 16 + 16 * (b0 + 1))
                    dve.wait_ge(s_kept, i + b0 + 1)
                    for m in range(2):
                        ins = dve.tensor_tensor_reduce(kc[u][:, m, :], kc[u][:, m, :], ps[:, 4 + u % 2, :], 1.0, 0.0, ALU.mult,
                                                       ALU.add, sc_b[:, m, u:u + 1])
                    ins.then_inc(N["s_dot"], 1)
                    if u == 3:
                        W(dve, "s_dot", i * 4 + (4 * b0 + u + 1 + 2))
                        dve.tensor_copy(sc_s[:, :, ds(i * 4 + 4 * b0, 4)], sc_b).then_inc(s_kept, 1)
                return f

            dve.wait_ge(rstd_ready, 3)
            run("mem_k", memory_and_scores(0), "mem_v")
            run("mem_v", memory_and_scores(NB // 2), "x_o")

            def row_max(v, src):
                link(dve.tensor_reduce(v, src, AX_X, ALU.max))
                return dve.tensor_scalar(v, v, -SCALE, None, ALU.mult)

            def prompt_max(h):
                W(dve, "att_qk", h + 1)
                row_max(small[:, MX, 2 * h:2 * h + 2], ps[:, h, :].rearrange("p (c m) -> p c m", c=2)).then_inc(N["att_max"], 1)

            def second_values(b):
                for h in range(XH):
                    dve.wait_ge(v_first, XH * b + h + 1)
                    v = vc[b % 2][:, :, h * XD:(h + 1) * XD]
                    dve.scalar_tensor_tensor(out=v[:, 0, :], in0=v[:, 1, :], scalar=pT_s[:, 1, b * XH + h:b * XH + h + 1],
                                             in1=v[:, 0, :], op0=ALU.mult, op1=ALU.add).then_inc(v_mixed, 1)

            W(dve, "s_st", 1)
            row_max(small[0:32, MX, 12:13], ps[0:32, 4, 0:NM]).then_inc(N["s_sm"], 1)
            W(dve, "s_exp", 1)
            link(dve.reciprocal(small[0:32, REC, 12:13], small[0:32, SUM, 12:13]))
            dve.tensor_scalar(p_s, p_s, small[0:32, REC, 12:13], None, ALU.mult).then_inc(N["s_pn"], 1)
            prompt_max(0)
            W(dve, "s_ptt", 1)
            dve.tensor_copy(pT_s, ps[:, 4, NM:NM + 64].rearrange("p (m n) -> p m n", m=2)).then_inc(N["s_pT"], 1)
            W(dve, "s_pT", 1)
            second_values(0)
            prompt_max(1)
            prompt_max(2)
            second_values(1)
            prompt_max(3)
            for h in range(XH):
                W(dve, "att_exp", h + 1)
                link(dve.reciprocal(small[:, REC, 2 * h:2 * h + 2], small[:, SUM, 2 * h:2 * h + 2]))
                for c in range(NC):
                    v = pr[:, h, c * NM:(c + 1) * NM]
                    ins = dve.tensor_scalar(v, v, small[:, REC, 2 * h + c:2 * h + c + 1], None, ALU.mult)
                ins.then_inc(N["att_norm"], 1)
            for b in range(2, NB):
                second_values(b)
                for j in prompt_tiles(b):
                    W(dve, "att_o", j + 1)
                    src = ps[:, 6 + j % 2, 0:T]
                    link(dve.tensor_copy(ow_hi[:, j, 0:T], src))
                    dve.tensor_tensor(ow_lo[:, j, 0:T], src, ow_hi[:, j, 0:T], ALU.subtract).then_inc(N["att_oe"], 1)
            dve.wait_ge(rows_turned, 1)

            def by_head(v):
                return v.rearrange("p (h d) b -> p h d b", d=4)

            src = ps[:, 4, 0:KT * NB].rearrange("p (d h b) -> p h d b", d=4, h=XH)
            link(dve.tensor_copy(by_head(ow_hi[:, :, T:TT]), src))
            dve.tensor_tensor(by_head(ow_lo[:, :, T:TT]), src, by_head(ow_hi[:, :, T:TT]), ALU.subtract).then_inc(N["s_oe"], 1)

            run("x_o", lambda ph, i, u: residual(ph, i, u, KT, GAIN_FFN), "gu0")
            dve.wait_ge(rstd_ready, 4)
            for half in range(2):
                run(f"gu{half}", gate_up(half), f"dn{half}")
                run(f"dn{half}", down(half), "gu1" if half == 0 else None)
            dve.wait_ge(rstd_ready, 5)
            for g in range(4):
                for t in range(4):
                    k = 4 * g + t
                    ins = dve.scalar_tensor_tensor(out=yT[:, k, :], in0=x[:, k, :],
                                                   scalar=cols[:, GAIN_FINAL + k:GAIN_FINAL + k + 1], in1=rstd[:, :],
                                                   op0=ALU.mult, op1=ALU.mult)
                ins.then_inc(N["y_norm"], 1)
            for g in range(4):
                W(dve, "y_turned", g + 1)
                dve.tensor_copy(yrows[:, 0, g * 512:(g + 1) * 512], ps[:, 3 * (g % 2), :]).then_inc(N["y_copied_dve"], 1)


_INS = ["x_prompt", "x_sample", "mem_prompt", "cache_mem_k", "cache_mem_v", "state_gla", "state_gdn", "state_conv",
        "g_mix", "w_in", "gla_w_gate2", "gla_b_gate", "gla_g_out", "gdn_conv_w", "gdn_a_log", "gdn_dt_bias", "gdn_g_out",
        "w_out", "g_xattn", "g_mem", "xa_w_q", "xa_w_k", "xa_w_v", "xa_w_o", "g_ffn", "ffn_w_gate", "ffn_w_up",
        "ffn_w_down", "g_final"]
_OUTS = [("y_p", (1, T, D)), ("y_s", (NB, 1, D)), ("gla_p", (1, 1, GH, GDK, GDV)), ("gdn_p", (1, 1, HB, P, P)),
         ("conv_p", (1, 1, CW - 1, CT * P)), ("mem_k", (1, 1, NM, XH, XD)), ("mem_v", (1, 1, NM, XH, XD)),
         ("gla_s", (1, NB, GH, GDK, GDV)), ("gdn_s", (1, NB, HB, P, P)), ("conv_s", (1, NB, CW - 1, CT * P))]


def kernel(**inputs):
    import numpy as _np
    import concourse.bacc as _bacc
    from concourse import mybir as _mybir
    from concourse.bass_utils import run_bass_kernel_spmd as _run

    nc = _bacc.Bacc("TRN2", target_bir_lowering=False, num_devices=1)
    arrays, ins, outs = {}, {}, {}
    for name in _INS:
        v = _np.ascontiguousarray(inputs[name])
        arrays[f"in_{name}_dram"] = v
        ins[name] = nc.dram_tensor(f"in_{name}_dram", v.shape, _mybir.dt.from_np(v.dtype), kind="ExternalInput").ap()
    for name, shape in _OUTS:
        outs[name] = nc.dram_tensor(f"out_{name}_dram", shape, _mybir.dt.float32, kind="ExternalOutput").ap()
    build(nc, ins, outs)
    r = _run(nc, [arrays], core_ids=[0])
    return tuple(r.results[0][f"out_{name}_dram"] for name, _ in _OUTS)
```
